# Optimizing a Trainium2 kernel written in Bass

```python
import jax, jax.numpy as jnp
from jax import lax
import numpy as np

D_MODEL = 1024
BATCH = 1
SEQ = 512
DEPTH = 2

CHUNK = 64
Q_BLOCK = 128
D_FF = 2816
EPS = 1e-6
ROPE_BASE = 10000.0
ROPE_DIM = 32

MLA_HEADS = 8
MLA_Q_RANK = 256
MLA_KV_RANK = 128
MLA_NOPE = 64
MLA_ROPE = ROPE_DIM
MLA_V = 64
GLA_HEADS = 4
GLA_DK = 32
GLA_DV = 64
GLA_GATE_RANK = 16
GLA_TAU = 16.0
RET_HEADS = 4
RET_DK = ROPE_DIM
RET_DV = 64

MLA_WIDTH = MLA_HEADS * MLA_V
GLA_WIDTH = GLA_HEADS * GLA_DV
RET_WIDTH = RET_HEADS * RET_DV
MIX_WIDTH = MLA_WIDTH + GLA_WIDTH + RET_WIDTH

IN_SPLITS = (
    MLA_Q_RANK, MLA_KV_RANK, MLA_ROPE,
    GLA_HEADS * GLA_DK, GLA_HEADS * GLA_DK, GLA_WIDTH,
    GLA_GATE_RANK, GLA_WIDTH,
    RET_HEADS * RET_DK, RET_HEADS * RET_DK, RET_WIDTH,
    RET_WIDTH,
)
D_IN = sum(IN_SPLITS)

kernel_name = "hybrid_mla_gla_retention_macaron"

def rms_norm(x, g):
    xf = x.astype(jnp.float32)
    y = xf * lax.rsqrt(jnp.mean(xf * xf, axis=-1, keepdims=True) + EPS)
    return (y * g.astype(jnp.float32)).astype(x.dtype)

def swiglu(x, w_gate, w_up, w_down):
    return (jax.nn.silu(x @ w_gate) * (x @ w_up)) @ w_down

def rope_tables(positions):
    inv = ROPE_BASE ** (-jnp.arange(0, ROPE_DIM, 2, dtype=jnp.float32) / ROPE_DIM)
    ang = positions.astype(jnp.float32)[..., None] * inv
    return jnp.cos(ang), jnp.sin(ang)

def apply_rope(x, cos, sin):
    xf = x.astype(jnp.float32)
    x1, x2 = jnp.split(xf, 2, axis=-1)
    c, s = cos[:, :, None, :], sin[:, :, None, :]
    return jnp.concatenate([x1 * c - x2 * s, x1 * s + x2 * c], axis=-1).astype(x.dtype)

def block_causal_attention(q, k, v):
    B, S, H, Dq = q.shape
    Dv = v.shape[-1]
    nb = S // Q_BLOCK
    scale = Dq ** -0.5
    qb = jnp.moveaxis(q.reshape(B, nb, Q_BLOCK, H, Dq), 1, 0)
    q_chunk = (jnp.arange(S) // CHUNK).reshape(nb, Q_BLOCK)
    k_chunk = jnp.arange(S) // CHUNK

    def one_block(args):
        q_blk, qc = args
        s = jnp.einsum('bqhd,bkhd->bhqk', q_blk, k,
                       preferred_element_type=jnp.float32) * scale
        mask = k_chunk[None, :] <= qc[:, None]
        s = jnp.where(mask, s, jnp.finfo(jnp.float32).min)
        p = jax.nn.softmax(s, axis=-1).astype(v.dtype)
        return jnp.einsum('bhqk,bkhe->bqhe', p, v)

    out = lax.map(one_block, (qb, q_chunk))
    return jnp.moveaxis(out, 0, 1).reshape(B, S, H, Dv)

def chunk_state_scan(d_state, decay):
    def step(s, inp):
        ds, dec = inp
        return dec * s + ds, s
    s0 = jnp.zeros_like(d_state[:, 0])
    _, s_before = lax.scan(step, s0, (jnp.moveaxis(d_state, 1, 0), jnp.moveaxis(decay, 1, 0)))
    return jnp.moveaxis(s_before, 0, 1)

def gla_chunked(q, k, v, log_a):
    B, S, H, DK = q.shape
    DV = v.shape[-1]
    N, L = S // CHUNK, CHUNK
    r = lambda t: t.reshape(B, N, L, H, t.shape[-1]).astype(jnp.float32)
    q, k, v, g = r(q), r(k), r(v), r(log_a)
    b = jnp.cumsum(g, axis=2)
    b_last = b[:, :, -1]
    eb, enb = jnp.exp(b), jnp.exp(-b)
    q_fwd, k_fwd = q * eb, k * enb
    a_low = jnp.einsum('bnihd,bnjhd->bnhij', q_fwd, k_fwd)
    a_up = jnp.einsum('bnihd,bnjhd->bnhij', q * enb, k * eb)
    lower = jnp.tril(jnp.ones((L, L), dtype=bool))
    attn = jnp.where(lower, a_low, a_up)
    o_intra = jnp.einsum('bnhij,bnjhe->bnihe', attn, v)
    k_state = k * jnp.exp(b_last[:, :, None] - b)
    d_state = jnp.einsum('bnjhd,bnjhe->bnhde', k_state, v)
    s_before = chunk_state_scan(d_state, jnp.exp(b_last)[..., None])
    o_inter = jnp.einsum('bnihd,bnhde->bnihe', q_fwd, s_before)
    return (o_intra + o_inter).reshape(B, S, H, DV)

def retention_chunked(q, k, v):
    B, S, H, DK = q.shape
    DV = v.shape[-1]
    N, L = S // CHUNK, CHUNK
    r = lambda t: t.reshape(B, N, L, H, t.shape[-1]).astype(jnp.float32)
    q, k, v = r(q), r(k), r(v)
    log_gamma = jnp.log1p(-jnp.exp2(-5.0 - jnp.arange(H, dtype=jnp.float32)))
    idx = jnp.arange(L, dtype=jnp.float32)
    dist = jnp.abs(idx[:, None] - idx[None, :])
    decay_mat = jnp.exp(log_gamma[:, None, None] * dist)
    scores = jnp.einsum('bnihd,bnjhd->bnhij', q, k) * decay_mat
    o_intra = jnp.einsum('bnhij,bnjhe->bnihe', scores, v)
    q_dec = jnp.exp(log_gamma[None, :] * (idx[:, None] + 1.0))
    k_dec = jnp.exp(log_gamma[None, :] * (L - 1.0 - idx[:, None]))
    d_state = jnp.einsum('bnjhd,bnjhe,jh->bnhde', k, v, k_dec)
    chunk_dec = jnp.broadcast_to(jnp.exp(log_gamma * L)[None, None, :, None, None], (1, N, H, 1, 1))
    s_before = chunk_state_scan(d_state, chunk_dec)
    o_inter = jnp.einsum('bnihd,bnhde,ih->bnihe', q, s_before, q_dec)
    return (o_intra + o_inter).reshape(B, S, H, DV)

def hybrid_mixer(h, cos, sin, w_in, mla_q_norm_g, mla_w_q_up, mla_kv_norm_g, mla_w_kv_up,
                 gla_w_gate_up, gla_b_gate, gla_norm_g, ret_norm_g, w_out):
    B, S, _ = h.shape
    offsets = np.cumsum(IN_SPLITS)[:-1].tolist()
    (mq, mkv, mkr, gq, gk, gv, gg, gr, rq, rk, rv, rg) = jnp.split(h @ w_in, offsets, axis=-1)

    qh = (rms_norm(mq, mla_q_norm_g) @ mla_w_q_up).reshape(B, S, MLA_HEADS, MLA_NOPE + MLA_ROPE)
    q_pe = apply_rope(qh[..., MLA_NOPE:], cos, sin)
    kvh = (rms_norm(mkv, mla_kv_norm_g) @ mla_w_kv_up).reshape(B, S, MLA_HEADS, MLA_NOPE + MLA_V)
    k_pe = apply_rope(mkr[:, :, None, :], cos, sin)
    q_mla = jnp.concatenate([qh[..., :MLA_NOPE], q_pe], axis=-1)
    k_mla = jnp.concatenate([kvh[..., :MLA_NOPE],
                             jnp.broadcast_to(k_pe, (B, S, MLA_HEADS, MLA_ROPE))], axis=-1)
    o_mla = block_causal_attention(q_mla, k_mla, kvh[..., MLA_NOPE:]).reshape(B, S, MLA_WIDTH)

    g_q = gq.reshape(B, S, GLA_HEADS, GLA_DK) * (GLA_DK ** -0.5)
    g_k = gk.reshape(B, S, GLA_HEADS, GLA_DK)
    g_v = gv.reshape(B, S, GLA_HEADS, GLA_DV)
    log_a = jax.nn.log_sigmoid((gg @ gla_w_gate_up + gla_b_gate).astype(jnp.float32)) / GLA_TAU
    o_g = gla_chunked(g_q, g_k, g_v, log_a.reshape(B, S, GLA_HEADS, GLA_DK)).astype(h.dtype)
    o_gla = (rms_norm(o_g, gla_norm_g) * jax.nn.silu(gr.reshape(B, S, GLA_HEADS, GLA_DV))
             ).reshape(B, S, GLA_WIDTH)

    r_q = apply_rope(rq.reshape(B, S, RET_HEADS, RET_DK), cos, sin)
    r_k = apply_rope(rk.reshape(B, S, RET_HEADS, RET_DK), cos, sin) * (RET_DK ** -0.5)
    o_r = retention_chunked(r_q, r_k, rv.reshape(B, S, RET_HEADS, RET_DV)).astype(h.dtype)
    o_ret = (rms_norm(o_r, ret_norm_g) * jax.nn.silu(rg.reshape(B, S, RET_HEADS, RET_DV))
             ).reshape(B, S, RET_WIDTH)

    return jnp.concatenate([o_mla, o_gla, o_ret], axis=-1) @ w_out

def setup_inputs(seed: int = 0) -> dict:
    key = jax.random.key(seed)
    ks = jax.random.split(key, 24)
    f32 = jnp.float32
    nrm = lambda k, shape, fan_in: jax.random.normal(k, shape, f32) * (fan_in ** -0.5)
    gain = lambda k, n: 1.0 + 0.02 * jax.random.normal(k, (DEPTH, n), f32)
    x = jax.random.normal(ks[0], (BATCH, SEQ, D_MODEL), f32)
    offset = jax.random.randint(ks[1], (BATCH, 1), 0, SEQ, dtype=jnp.int32)
    positions = offset + jnp.arange(SEQ, dtype=jnp.int32)[None, :]
    return {
        "x": x,
        "positions": positions,
        "ffn1_pre_g": gain(ks[2], D_MODEL),
        "ffn1_post_g": gain(ks[3], D_MODEL),
        "ffn1_w_gate": nrm(ks[4], (DEPTH, D_MODEL, D_FF), D_MODEL),
        "ffn1_w_up": nrm(ks[5], (DEPTH, D_MODEL, D_FF), D_MODEL),
        "ffn1_w_down": nrm(ks[6], (DEPTH, D_FF, D_MODEL), D_FF),
        "mix_pre_g": gain(ks[7], D_MODEL),
        "mix_post_g": gain(ks[8], D_MODEL),
        "w_in": nrm(ks[9], (DEPTH, D_MODEL, D_IN), D_MODEL),
        "mla_q_norm_g": gain(ks[10], MLA_Q_RANK),
        "mla_w_q_up": nrm(ks[11], (DEPTH, MLA_Q_RANK, MLA_HEADS * (MLA_NOPE + MLA_ROPE)), MLA_Q_RANK),
        "mla_kv_norm_g": gain(ks[12], MLA_KV_RANK),
        "mla_w_kv_up": nrm(ks[13], (DEPTH, MLA_KV_RANK, MLA_HEADS * (MLA_NOPE + MLA_V)), MLA_KV_RANK),
        "gla_w_gate_up": nrm(ks[14], (DEPTH, GLA_GATE_RANK, GLA_HEADS * GLA_DK), GLA_GATE_RANK),
        "gla_b_gate": 0.1 * jax.random.normal(ks[15], (DEPTH, GLA_HEADS * GLA_DK), f32),
        "gla_norm_g": gain(ks[16], GLA_DV),
        "ret_norm_g": gain(ks[17], RET_DV),
        "w_out": nrm(ks[18], (DEPTH, MIX_WIDTH, D_MODEL), MIX_WIDTH),
        "ffn2_pre_g": gain(ks[19], D_MODEL),
        "ffn2_post_g": gain(ks[20], D_MODEL),
        "ffn2_w_gate": nrm(ks[21], (DEPTH, D_MODEL, D_FF), D_MODEL),
        "ffn2_w_up": nrm(ks[22], (DEPTH, D_MODEL, D_FF), D_MODEL),
        "ffn2_w_down": nrm(ks[23], (DEPTH, D_FF, D_MODEL), D_FF),
    }

def reference(x, positions, ffn1_pre_g, ffn1_post_g, ffn1_w_gate, ffn1_w_up, ffn1_w_down,
              mix_pre_g, mix_post_g, w_in, mla_q_norm_g, mla_w_q_up, mla_kv_norm_g, mla_w_kv_up,
              gla_w_gate_up, gla_b_gate, gla_norm_g, ret_norm_g, w_out,
              ffn2_pre_g, ffn2_post_g, ffn2_w_gate, ffn2_w_up, ffn2_w_down):
    cos, sin = rope_tables(positions)
    for l in range(DEPTH):
        f = swiglu(rms_norm(x, ffn1_pre_g[l]), ffn1_w_gate[l], ffn1_w_up[l], ffn1_w_down[l])
        x = x + 0.5 * rms_norm(f, ffn1_post_g[l])
        m = hybrid_mixer(rms_norm(x, mix_pre_g[l]), cos, sin, w_in[l],
                         mla_q_norm_g[l], mla_w_q_up[l], mla_kv_norm_g[l], mla_w_kv_up[l],
                         gla_w_gate_up[l], gla_b_gate[l], gla_norm_g[l], ret_norm_g[l], w_out[l])
        x = x + rms_norm(m, mix_post_g[l])
        f = swiglu(rms_norm(x, ffn2_pre_g[l]), ffn2_w_gate[l], ffn2_w_up[l], ffn2_w_down[l])
        x = x + 0.5 * rms_norm(f, ffn2_post_g[l])
    return x


_drawn_inputs = setup_inputs


def setup_inputs(seed=0):
    import zlib

    import numpy as np

    out = dict(_drawn_inputs(seed))
    spreads = {}
    factors = {'mla_q_norm_g': 8.0,
     'mla_kv_norm_g': 7.035,
     'gla_norm_g': 14.664,
     'ret_norm_g': 15.744,
     'ffn2_pre_g': 3.818,
     'ffn2_post_g': 5.538}
    for name, (base, spread) in spreads.items():
        noise = np.random.default_rng([zlib.crc32(name.encode()), seed]).standard_normal(out[name].shape)
        drawn = base * np.exp(spread * noise) if base else spread * noise
        out[name] = __import__('jax').numpy.asarray(drawn.astype(out[name].dtype))
    for name, factor in factors.items():
        out[name] = (out[name] * factor).astype(out[name].dtype)
    return out
```

```python
from contextlib import ExitStack

import concourse.bass as bass
from concourse import mybir

ALU = mybir.AluOpType
ACT = mybir.ActivationFunctionType
F32 = mybir.dt.float32
F32R = mybir.dt.float32r
I32 = mybir.dt.int32
AX_X = mybir.AxisListType.X

P = 128
SEQ = 512
D = 1024
DT = D // P
DEPTH = 2
FF = 2816
FT = FF // P
CHUNK = 64
NCHUNK = SEQ // CHUNK
BLK = SEQ // P
EPS = 1e-6
TAU = 16.0
HEADS = 8
NOPE, ROPE, DV = 64, 32, 64
QK = NOPE + ROPE
QR, KVR = 256, 128
GH, DK = 4, 32
GV = GH * DV
GATE_RANK = 16
MASKED = -3.0e38

FFN_PAIRS = FT + FT // 2
IN_PAIRS, OUT_PAIRS = 8, 4
MIX_PAIRS = IN_PAIRS + OUT_PAIRS
PAIRS = 2 * FFN_PAIRS + MIX_PAIRS
SLAB = 8 * P
NORMS = 8

G_PRE = (0, 16, 32)
G_POST = (8, 24, 40)
G_Q, G_KV, G_GLA, G_RET = 48, 50, 51, 52
GAINS = 53

C_ID = 0
C_TRI = C_ID + P
C_ROT = C_TRI + P
C_DEC = C_ROT + P
C_LOW = C_DEC + GH * P
C_QDEC = C_LOW + CHUNK
C_KDEC = C_QDEC + CHUNK
C_CDEC = C_KDEC + CHUNK
C_HSEL = C_CDEC + 1
C_INV = C_HSEL + 2
CONSTS = C_INV + 1

X_ORDER = [1, 0, 2, 3, 4, 5, 6, 7]
F_ORDER = [4, 5, 6, 7, 0, 1, 2, 3]

TWO_PI = 6.283185307179586
C1 = 6.28125
C2 = 0.0019350051879882812
C3 = TWO_PI - C1 - C2
ROUND = 12582912.0


DVE_STEPS = 158
ACT_STEPS = 2



def hybrid_trunk(nc, x_in, positions, stream, gains_in, w_q_up, w_kv_up, w_gate_up, b_gate, consts, out):
    ctx = ExitStack()
    with ctx:
        def sb(name, shape, dt=F32, stack=ctx):
            return stack.enter_context(nc.sbuf_tensor(name, shape, dt))

        per_layer, ahead = {}, {}

        def sem(name, times, before=0):
            made = ctx.enter_context(nc.semaphore(name))
            per_layer[made], ahead[made] = times, before
            return made

        def counter(layer):
            def due(semaphore, n):
                return layer * per_layer[semaphore] + n + ahead[semaphore]
            return due

        ps = ctx.enter_context(nc.psum_tensor("ps", [P, 8, 512], F32))

        x = sb("x", [P, DT, SEQ])
        xH = sb("xH", [P, DT, SEQ], F32R)
        xL = sb("xL", [P, DT, SEQ], F32R)
        raw = sb("raw", [P, 2, 2 * SLAB])
        WH = sb("WH", [P, 2, 2 * SLAB], F32R)
        WL = sb("WL", [P, 2, 2 * SLAB], F32R)
        rstd_x = sb("rstd_x", [P, SEQ])
        rstd_f = sb("rstd_f", [P, SEQ])
        f0 = sb("f0", [P, SEQ])
        gate = sb("gate", [P, SEQ])
        up = sb("up", [P, SEQ])
        xg = [gate, up]
        sq = sb("sq", [P, 2, SEQ])
        acc = sb("acc", [P, SEQ])
        ident = sb("ident", [P, P])
        ones = sb("ones", [P, 1])
        ones_row = sb("ones_row", [P, P])
        gains_all = sb("gains_all", [P, DEPTH, GAINS])
        gains = sb("gains", [P, GAINS])
        mean = sb("mean", [P, 32])
        rstd = sb("rstd", [P, 32])
        minus_half = sb("minus_half", [P, 32])
        rx_col = sb("rx_col", [P, BLK])
        b_last = sb("b_last", [P, NCHUNK])
        top = sb("top", [P, 2])
        minus_top = sb("minus_top", [P, 2])
        total = sb("total", [P, 2])
        share = sb("share", [P, 2])

        with ExitStack() as hidden:
            hH = sb("hH", [P, FT, SEQ], F32R, hidden)
            hL = sb("hL", [P, FT, SEQ], F32R, hidden)
        mq = sb("mq", [P, 2, SEQ])
        ckv = sb("ckv", [P, SEQ])
        krgg = sb("krgg", [P, SEQ])
        gq = sb("gq", [P, SEQ])
        gk = sb("gk", [P, SEQ])
        rq = sb("rq", [P, SEQ])
        rk = sb("rk", [P, SEQ])
        o_tok = [gq, gk, rq, rk]
        v_tok = sb("v_tok", [P, BLK, 2 * GV])
        gates = [gate, up, f0, rstd_f]
        cos = sb("cos", [P, SEQ])
        sin = sb("sin", [P, SEQ])
        wq = sb("wq", [P, 2, HEADS * QK])
        wkv = sb("wkv", [P, HEADS * (NOPE + DV)])
        wgu = sb("wgu", [P, GH * DK])
        bias = sb("bias", [P, GH * DK])
        const = sb("const", [P, CONSTS])
        zg = sb("zg", [P, SEQ])
        eb = sb("eb", [P, SEQ])
        enb = sb("enb", [P, SEQ])
        kf = sb("kf", [P, SEQ])
        kb = sb("kb", [P, SEQ])
        ks_ret = sb("ks_ret", [P, SEQ])
        kt_gla = sb("kt_gla", [P, BLK, P])
        kt_ret = sb("kt_ret", [P, BLK, P])
        attn_g = sb("attn_g", [P, GH, P])
        attn_r = sb("attn_r", [P, GH, P])
        with ExitStack() as linear:
            qx = sb("qx", [P, 3, 2, GH, P], F32, linear)
            s_gla = sb("s_gla", [P, NCHUNK - 1, GV], F32, linear)
            s_ret = sb("s_ret", [P, NCHUNK - 1, GV], F32, linear)
        with ExitStack() as latent:
            qT = sb("qT", [P, 2, SEQ], F32, latent)
            kT = sb("kT", [P, 2, SEQ], F32, latent)
            v_mla = sb("v_mla", [P, BLK, HEADS * DV], F32, latent)
            prob = sb("prob", [P, 2, SEQ], F32, latent)
            probT = sb("probT", [P, 10 * P], F32, latent)

        tri = const[:, C_TRI:C_TRI + P]
        rot = const[:, C_ROT:C_ROT + P]
        decay = const[:, C_DEC:C_DEC + GH * P].rearrange("p (h i) -> p h i", h=GH)
        low = const[:, C_LOW:C_LOW + CHUNK].bitcast(I32)
        q_dec = const[:, C_QDEC:C_QDEC + CHUNK]
        k_dec = const[:, C_KDEC:C_KDEC + CHUNK]
        chunk_dec = const[:, C_CDEC:C_CDEC + 1]
        head_sel = const[:, C_HSEL:C_HSEL + 2]
        inv_freq = const[:, C_INV:C_INV + 1]

        landed = [sem(f"pair_landed{i}", 16 * PAIRS // 2) for i in range(2)]
        wH_ready = sem("wH_ready", PAIRS)
        wL_ready = sem("wL_ready", PAIRS)
        pair_done = sem("pair_done", PAIRS, 2)
        start_landed = sem("start_landed", 0)
        start_ready = sem("start_ready", 0)
        x_ready = sem("x_ready", 3 * DT, DT)
        gains_ready = sem("gains_ready", 1)
        xH_ready = sem("xH_ready", 3 * DT)
        xL_ready = sem("xL_ready", 3 * DT)
        sq_ready = sem("sq_ready", 6 * DT)
        sq_used = sem("sq_used", 6 * DT)
        f0_ready = sem("f0_ready", 3)
        f_ready = sem("f_ready", 3 * (DT - 1))
        col_ready = sem("col_ready", NORMS)
        mean_ready = sem("mean_ready", NORMS)
        rstd_ready = sem("rstd_ready", NORMS)
        spread_ready = sem("spread_ready", NORMS)
        spread_kept = sem("spread_kept", 6)
        gu_scaled = sem("gu_scaled", 2 * FT)
        silu_ready = sem("silu_ready", 2 * FT)
        h_ready = sem("h_ready", 2 * FT)
        hH_ready = sem("hH_ready", 2 * FT)
        hL_ready = sem("hL_ready", 2 * FT)
        dve_step = sem("dve_step", DVE_STEPS)
        act_step = sem("act_step", ACT_STEPS)
        out_stored = sem("out_stored", 0)
        pool_passed = sem("pool_passed", 0)
        dve_passed = sem("dve_passed", 0)
        mix_landed = sem("mix_landed", 16 * 7)
        in_kept = sem("in_kept", 12)
        v_kept = sem("v_kept", 2)
        gate_silu = sem("gate_silu", 4)
        angle_ready = sem("angle_ready", 1)
        sine_ready = sem("sine_ready", 2)
        rope_ready = sem("rope_ready", 1)
        latent_sq = sem("latent_sq", 3)
        latent_ready = sem("latent_ready", 3)
        z_ready = sem("z_ready", 1)
        soft_ready = sem("soft_ready", 1)
        log_ready = sem("log_ready", 1)
        cum_ready = sem("cum_ready", 1)
        b_last_ready = sem("b_last_ready", 1)
        exp_ready = sem("exp_ready", 3)
        k_ready = sem("k_ready", 3)
        rot_ready = sem("rot_ready", 3)
        ret_ready = sem("ret_ready", 2)
        kpe_ready = sem("kpe_ready", 1)
        kt_psum = sem("kt_psum", 2)
        kt_kept = sem("kt_kept", 2)
        ds_ready = sem("ds_ready", BLK)
        state_ready = sem("state_ready", BLK)
        cleared = sem("cleared", 1)
        qg_ready = sem("qg_ready", BLK)
        qr_ready = sem("qr_ready", BLK)
        gr_scored = sem("gr_scored", BLK)
        up_kept = sem("up_kept", BLK)
        gr_ready = sem("gr_ready", BLK)
        gr_used = sem("gr_used", BLK)
        o_kept = sem("o_kept", 4)
        o_sq = sem("o_sq", 4)
        o_sq_used = sem("o_sq_used", 3)
        o_gated = sem("o_gated", 4)
        mixH_ready = sem("mixH_ready", 8)
        mixL_ready = sem("mixL_ready", 8)
        vm_psum = sem("vm_psum", BLK)
        vm_kept = sem("vm_kept", BLK)
        q_psum = sem("q_psum", HEADS)
        q_kept = sem("q_kept", HEADS)
        q_rot = sem("q_rot", HEADS)
        q_ready = sem("q_ready", HEADS)
        k_psum = sem("k_psum", HEADS)
        k_kept = sem("k_kept", HEADS)
        kpe_copied = sem("kpe_copied", 2)
        scored = sem("scored", HEADS * BLK)
        top_ready = sem("top_ready", HEADS * BLK)
        exped = sem("exped", HEADS * BLK)
        prob_ready = sem("prob_ready", HEADS * BLK)
        turned = sem("turned", HEADS * BLK)
        turn_kept = sem("turn_kept", HEADS * BLK)
        head_done = sem("head_done", HEADS)

        block = ctx.enter_context(nc.Block())

        @block.sync
        def _(sp):
            sp.dma_start(x[:], x_in).then_inc(start_landed, 16)
            sp.dma_start(ident[:], consts[:, C_ID:C_ID + P]).then_inc(start_landed, 16)
            sp.dma_start(gains_all[:], gains_in.rearrange("l p g -> p l g")).then_inc(start_landed, 16)
            for slot in range(2):
                sp.dma_start(raw[:, slot, :], stream[slot]).then_inc(landed[slot], 16)
            with sp.Fori(1, DEPTH * PAIRS // 2) as m:
                for slot in range(2):
                    sp.wait_ge(wH_ready, 2 * m + (slot - 1))
                    sp.wait_ge(wL_ready, 2 * m + (slot - 1))
                    sp.dma_start(raw[:, slot, :], stream[2 * m + slot]).then_inc(landed[slot], 16)
            for n, k in enumerate(X_ORDER):
                sp.wait_ge(x_ready, ahead[x_ready] + DEPTH * per_layer[x_ready] - DT + n + 1)
                sp.dma_start(out[:, k, :], x[:, k, :]).then_inc(out_stored, 16)
            sp.wait_ge(out_stored, 16 * DT)

        @block.tensor
        def _(pe):
            mm = nc.tensor.matmul
            pe.sem_inc(pair_done, 2)
            pe.wait_ge(start_ready, 1)
            pe.wait_ge(start_landed, 48)

            def three(dst, wh, wl, xh, xl, start, stop):
                mm(dst, wh, xh, start=start, stop=False)
                mm(dst, wh, xl, start=False, stop=False)
                return mm(dst, wl, xh, start=False, stop=stop)

            with pe.Fori(0, DEPTH) as layer:
                due = counter(layer)

                def tiles_pair(p, slot, banks, widths=(P, P), split=None):
                    pe.wait_ge(wH_ready, due(wH_ready, p + 1))
                    pe.wait_ge(wL_ready, due(wL_ready, p + 1))
                    for n, k in enumerate(X_ORDER):
                        if split is not None:
                            pe.wait_ge(xH_ready, due(xH_ready, split + n + 1))
                            pe.wait_ge(xL_ready, due(xL_ready, split + n + 1))
                        for j in range(2):
                            at = j * SLAB + k * P
                            last = three(ps[0:widths[j], banks[j], :], WH[:, slot, at:at + widths[j]],
                                         WL[:, slot, at:at + widths[j]], xH[:, k, :], xL[:, k, :],
                                         n == 0, n == DT - 1)
                    last.then_inc(pair_done, 1)

                def columns(src, bank, squares):
                    pe.wait_ge(sq_used, due(sq_used, squares))
                    for c in range(BLK):
                        last = mm(ps[:, bank, c:c + 1], src[:, c * P:(c + 1) * P], ones[:], start=True, stop=True)
                    last.then_inc(col_ready, 1)

                def spread(norm, bank):
                    pe.wait_ge(rstd_ready, due(rstd_ready, norm + 1))
                    for c in range(BLK):
                        last = mm(ps[:, bank, c * P:(c + 1) * P], rstd[:, c:c + 1].broadcast_to([P, P]), ident[:],
                                  start=True, stop=True)
                    last.then_inc(spread_ready, 1)

                def down_pair(p, slot, moving, first, last_pair):
                    pe.wait_ge(wH_ready, due(wH_ready, p + 1))
                    pe.wait_ge(wL_ready, due(wL_ready, p + 1))
                    for d in F_ORDER:
                        for j in range(2):
                            at = j * SLAB + d * P
                            h, l = moving[j]
                            last = three(ps[:, d, :], WH[:, slot, at:at + P], WL[:, slot, at:at + P], h, l,
                                         first and j == 0, last_pair and j == 1)
                        if last_pair and d != F_ORDER[-1]:
                            last.then_inc(f_ready, 1)
                    last.then_inc(pair_done, 1)

                def ffn(stage, f_stage, base, norm):
                    slot = base % 2
                    for i in range(2):
                        tiles_pair(base + i, (slot + i) % 2, (2 * i, 2 * i + 1),
                                   split=DT * stage if i == 0 else None)
                    columns(acc, 4, 2 * DT * stage + DT)
                    spread(norm, 5)
                    with pe.Fori(1, FT // 2) as i:
                        for j in range(2):
                            pe.wait_ge(gu_scaled, due(gu_scaled, FT * f_stage + 2 * i + j - 1))
                            tiles_pair(base + 2 * i + j, (slot + j) % 2, (2 * j, 2 * j + 1))
                    pe.wait_ge(spread_kept, due(spread_kept, 2 * stage + 1))
                    pe.wait_ge(gu_scaled, due(gu_scaled, FT * (f_stage + 1)))

                    def hidden(j, f):
                        pe.wait_ge(hH_ready, due(hH_ready, FT * f_stage + f + 2))
                        pe.wait_ge(hL_ready, due(hL_ready, FT * f_stage + f + 2))
                        return [(hH[:, f + a, :], hL[:, f + a, :]) for a in range(2)]

                    for j in range(2):
                        down_pair(base + FT + j, (slot + j) % 2, hidden(j, 2 * j), j == 0, False)
                    with pe.Fori(1, FT // 4) as m:
                        for j in range(2):
                            down_pair(base + FT + 2 * m + j, (slot + j) % 2, hidden(j, 4 * m + 2 * j), False, False)
                    down_pair(base + FT + FT // 2 - 1, slot, hidden(0, FT - 2), False, True)
                    after(stage, norm + 1)

                def after(stage, norm):
                    pe.wait_ge(f0_ready, due(f0_ready, stage + 1))
                    columns(acc, 0, 2 * DT * (stage + 1))
                    spread(norm, 0)

                def mixer(base, norm):
                    stage = 1
                    slot = base % 2

                    def pair(i, banks, **kw):
                        tiles_pair(base + i, (slot + i) % 2, banks, **kw)

                    def values_pair(i, banks):
                        s = (slot + i) % 2
                        pe.wait_ge(wH_ready, due(wH_ready, base + i + 1))
                        pe.wait_ge(wL_ready, due(wL_ready, base + i + 1))
                        for b in range(BLK):
                            dst = ps[:, banks[b // 2], (b % 2) * GV:(b % 2 + 1) * GV]
                            for k in range(DT):
                                at, tok = k * GV, slice(b * P, (b + 1) * P)
                                mm(dst, xH[:, k, tok], WH[:, s, at:at + GV], start=k == 0, stop=False)
                                mm(dst, xH[:, k, tok], WL[:, s, at:at + GV], start=False, stop=False)
                                last = mm(dst, xL[:, k, tok], WH[:, s, at:at + GV], start=False, stop=k == DT - 1)
                        last.then_inc(pair_done, 1)

                    pair(0, (0, 1), split=DT * stage)
                    pair(1, (2, 3), widths=(P, QK + GATE_RANK))
                    columns(acc, 6, 2 * DT * stage + DT)
                    spread(norm, 7)
                    pair(2, (4, 5))
                    pe.wait_ge(in_kept, due(in_kept, 2))
                    pair(3, (0, 1))
                    pe.wait_ge(in_kept, due(in_kept, 4))
                    pe.wait_ge(mix_landed, due(mix_landed, 16 * 7))
                    pe.wait_ge(spread_kept, due(spread_kept, 3))
                    for b in range(BLK):
                        dst = ps[:, 7, b * P:(b + 1) * P]
                        mm(dst, krgg[QK:QK + GATE_RANK, b * P:(b + 1) * P], wgu[QK:QK + GATE_RANK, :], start=True, stop=False)
                        last = mm(dst, ones_row[QK:QK + 1, :], bias[QK:QK + 1, :], start=False, stop=True)
                    last.then_inc(z_ready, 1)
                    values_pair(4, (2, 3))
                    pe.wait_ge(latent_sq, due(latent_sq, 3))
                    for c in range(BLK):
                        tok = slice(c * P, (c + 1) * P)
                        mm(ps[:, 6, c:c + 1], sq[:, 0, tok], ones[:], start=True, stop=False)
                        mm(ps[:, 6, c:c + 1], sq[:, 1, tok], ones[:], start=False, stop=True)
                        last = mm(ps[:, 6, 4 + c:5 + c], acc[:, tok], ones[:], start=True, stop=True)
                    last.then_inc(col_ready, 1)
                    pe.wait_ge(in_kept, due(in_kept, 6))
                    values_pair(5, (4, 5))
                    pe.wait_ge(log_ready, due(log_ready, 1))
                    for b in range(BLK):
                        last = mm(ps[:, 7, b * P:(b + 1) * P], zg[:, b * P:(b + 1) * P], tri, start=True, stop=True)
                    last.then_inc(cum_ready, 1)
                    pe.wait_ge(in_kept, due(in_kept, 8))
                    pair(6, (0, 1))
                    pe.wait_ge(v_kept, due(v_kept, 2))
                    pe.wait_ge(rstd_ready, due(rstd_ready, norm + 2))
                    for c in range(BLK):
                        tok = slice(c * P, (c + 1) * P)
                        mm(ps[:, 6, tok], rstd[:, c:c + 1].broadcast_to([P, P]), ident[:], start=True, stop=True)
                        last = mm(ps[:, 4, tok], rstd[:, 4 + c:5 + c].broadcast_to([P, P]), ident[:], start=True, stop=True)
                    last.then_inc(spread_ready, 1)
                    pair(7, (2, 3))
                    mm(ps[:, 5, :], rot, rq[:], start=True, stop=True).then_inc(rot_ready, 1)
                    pe.wait_ge(in_kept, due(in_kept, 10))
                    mm(ps[:, 0, :], rot, rk[:], start=True, stop=True).then_inc(rot_ready, 1)
                    mm(ps[0:QK, 1, :], rot[NOPE:QK, 0:QK], krgg[NOPE:QK, :], start=True, stop=True).then_inc(rot_ready, 1)
                    pe.wait_ge(k_ready, due(k_ready, 3))
                    pe.wait_ge(latent_ready, due(latent_ready, 3))
                    for b in range(BLK):
                        last = nc.tensor.transpose(ps[:, 6, b * P:(b + 1) * P], zg[:, b * P:(b + 1) * P], ident[:])
                    last.then_inc(kt_psum, 1)
                    pe.wait_ge(ret_ready, due(ret_ready, 2))
                    pe.wait_ge(in_kept, due(in_kept, 12))
                    for b in range(BLK):
                        last = nc.tensor.transpose(ps[:, 7, b * P:(b + 1) * P], ks_ret[:, b * P:(b + 1) * P], ident[:])
                    last.then_inc(kt_psum, 1)
                    pe.wait_ge(kt_kept, due(kt_kept, 2))
                    for b in range(BLK):
                        banks = (4, 5) if b % 2 == 0 else (2, 3)
                        if b >= 2:
                            pe.wait_ge(state_ready, due(state_ready, b - 1))
                        for c in range(2 if b < BLK - 1 else 1):
                            rows = slice(c * CHUNK, (c + 1) * CHUNK)
                            mm(ps[:, banks[c], 0:GV], kt_gla[rows, b, :], v_tok[rows, b, 0:GV], start=True, stop=True)
                            last = mm(ps[:, banks[c], GV:2 * GV], kt_ret[rows, b, :], v_tok[rows, b, GV:2 * GV],
                                      start=True, stop=True)
                        last.then_inc(ds_ready, 1)
                    pe.wait_ge(kpe_ready, due(kpe_ready, 1))

                    def gr_scores(b):
                        tok = slice(b * P, (b + 1) * P)
                        pe.wait_ge(qg_ready, due(qg_ready, b + 1))
                        pe.wait_ge(qr_ready, due(qr_ready, b + 1))
                        if b >= 1:
                            pe.wait_ge(gr_ready, due(gr_ready, b))
                        mm(ps[:, 4, :], kf[:, tok], qx[:, 0, b % 2].rearrange("p h i -> p (h i)"), start=True, stop=True)
                        mm(ps[:, 5, :], kb[:, tok], qx[:, 1, b % 2].rearrange("p h i -> p (h i)"), start=True, stop=True)
                        mm(ps[:, 6, :], rk[:, tok], qx[:, 2, b % 2].rearrange("p h i -> p (h i)"), start=True,
                           stop=True).then_inc(gr_scored, 1)

                    def gr_values(b):
                        pe.wait_ge(gr_ready, due(gr_ready, b + 1))
                        for kind, (attn, state) in enumerate(((attn_g, s_gla), (attn_r, s_ret))):
                            for h in range(GH):
                                rows = slice(DV * (h % 2), DV * (h % 2 + 1))
                                bank = 2 * kind + h // 2
                                vcol = slice(kind * GV + h * DV, kind * GV + (h + 1) * DV)
                                last = mm(ps[rows, bank, b * P:(b + 1) * P], v_tok[:, b, vcol], attn[:, h, :],
                                          start=True, stop=False)
                                for c in range(2):
                                    n = 2 * b + c
                                    if n == 0:
                                        continue
                                    last = mm(ps[rows, bank, n * CHUNK:(n + 1) * CHUNK],
                                              state[:, n - 1, h * DV:(h + 1) * DV],
                                              qx[:, 2 * kind, b % 2, h, c * CHUNK:(c + 1) * CHUNK],
                                              start=False, stop=c == 1)
                        last.then_inc(gr_used, 1)

                    pe.wait_ge(state_ready, due(state_ready, BLK))
                    for b in range(BLK):
                        gr_scores(b)
                        gr_values(b)
                    for t in range(4):
                        pe.wait_ge(o_sq, due(o_sq, t + 1))
                        for c in range(BLK):
                            last = mm(ps[:, 7, t * 8 + 2 * c:t * 8 + 2 * c + 2], sq[:, t % 2, c * P:(c + 1) * P],
                                      head_sel, start=True, stop=True)
                        if t < 3:
                            last.then_inc(o_sq_used, 1)
                    last.then_inc(col_ready, 1)

                    def make_values(b):
                        if b >= 2:
                            pe.wait_ge(vm_kept, due(vm_kept, b - 1))
                        mm(ps[:, 2 + b % 2, :], ckv[:, b * P:(b + 1) * P],
                           wkv[:].rearrange("p (h c) -> p h c", h=HEADS)[:, :, NOPE:NOPE + DV],
                           start=True, stop=True).then_inc(vm_psum, 1)

                    def make_q(h):
                        if h >= 1:
                            pe.wait_ge(q_kept, due(q_kept, h))
                        for k in range(2):
                            last = mm(ps[0:QK, 0, :], wq[:, k, h * QK:(h + 1) * QK], mq[:, k, :],
                                      start=k == 0, stop=k == 1)
                        last.then_inc(q_psum, 1)

                    def turn_q(h):
                        pe.wait_ge(q_kept, due(q_kept, h + 1))
                        mm(ps[0:QK, 1, :], rot[NOPE:QK, 0:QK], qT[NOPE:QK, h % 2, :], start=True,
                           stop=True).then_inc(q_rot, 1)

                    def make_k(h):
                        if h == 0:
                            pe.wait_ge(vm_kept, due(vm_kept, BLK))
                        if h >= 1:
                            pe.wait_ge(k_kept, due(k_kept, h))
                        at = h * (NOPE + DV)
                        mm(ps[0:NOPE, 2, :], wkv[:, at:at + NOPE], ckv[:], start=True, stop=True).then_inc(k_psum, 1)

                    for b in range(BLK):
                        make_values(b)
                    make_q(0)
                    make_k(0)
                    turn_q(0)
                    pe.wait_ge(rstd_ready, due(rstd_ready, norm + 3))
                    for t in range(4):
                        for c in range(BLK):
                            for h in range(2):
                                at = t * 8 + 2 * c + h
                                last = mm(ps[h * DV:(h + 1) * DV, 4 + t, c * P:(c + 1) * P],
                                          rstd[:, at:at + 1].broadcast_to([P, DV]), ident[:], start=True, stop=True)
                    last.then_inc(spread_ready, 1)
                    pe.wait_ge(o_gated, due(o_gated, 4))

                    def scores(h, b):
                        n = h * BLK + b
                        if b == 0:
                            pe.wait_ge(q_ready, due(q_ready, h + 1))
                            pe.wait_ge(k_kept, due(k_kept, h + 1))
                            pe.wait_ge(kpe_copied, due(kpe_copied, 2))
                        if n >= 2:
                            pe.wait_ge(exped, due(exped, n - 1))
                        mm(ps[:, 3 + n % 2, 0:(b + 1) * P], qT[0:QK, h % 2, b * P:(b + 1) * P],
                           kT[0:QK, h % 2, 0:(b + 1) * P], start=True, stop=True).then_inc(scored, 1)

                    def turn(h, b):
                        n = h * BLK + b
                        pe.wait_ge(prob_ready, due(prob_ready, n + 1))
                        if n >= 2:
                            pe.wait_ge(turn_kept, due(turn_kept, n - 1))
                        for kk in range(b + 1):
                            last = nc.tensor.transpose(ps[:, 5 + n % 2, kk * P:(kk + 1) * P],
                                                       prob[:, n % 2, kk * P:(kk + 1) * P], ident[:])
                        last.then_inc(turned, 1)

                    def values(h):
                        pe.wait_ge(turn_kept, due(turn_kept, (h + 1) * BLK))
                        if h % 2 == 0 and h >= 2:
                            pe.wait_ge(mixH_ready, due(mixH_ready, 4 + h // 2))
                            pe.wait_ge(mixL_ready, due(mixL_ready, 4 + h // 2))
                        rows = slice(DV * (h % 2), DV * (h % 2 + 1))
                        n = 0
                        for b in range(BLK):
                            for kk in range(b + 1):
                                last = mm(ps[rows, 7, b * P:(b + 1) * P], v_mla[:, kk, h * DV:(h + 1) * DV],
                                          probT[:, n * P:(n + 1) * P], start=kk == 0, stop=kk == b)
                                n += 1
                        last.then_inc(head_done, 1)

                    for h in range(HEADS):
                        scores(h, 0)
                        scores(h, 1)
                        if h + 1 < HEADS:
                            make_q(h + 1)
                        turn(h, 0)
                        scores(h, 2)
                        if h + 1 < HEADS:
                            make_k(h + 1)
                        turn(h, 1)
                        scores(h, 3)
                        if h + 1 < HEADS:
                            turn_q(h + 1)
                        turn(h, 2)
                        turn(h, 3)
                        values(h)
                    pe.wait_ge(mixH_ready, due(mixH_ready, 8))
                    pe.wait_ge(mixL_ready, due(mixL_ready, 8))
                    for i in range(OUT_PAIRS):
                        down_pair(base + IN_PAIRS + i, (slot + i) % 2,
                                  [(xH[:, 2 * i + a, :], xL[:, 2 * i + a, :]) for a in range(2)],
                                  i == 0, i == OUT_PAIRS - 1)
                    after(stage, norm + 3)

                ffn(0, 0, 0, 0)
                mixer(FFN_PAIRS, 2)
                ffn(2, 1, FFN_PAIRS + MIX_PAIRS, 6)

        @block.scalar
        def _(act):
            af = nc.scalar.activation
            steps = [0]
            with act.Fori(0, DEPTH) as layer:
                due = counter(layer)
                steps[0] = 0

                def link(instruction):
                    steps[0] += 1
                    instruction.then_inc(act_step, 1)
                    act.wait_ge(act_step, due(act_step, steps[0]))

                act.wait_ge(gains_ready, due(gains_ready, 1))

                def high(p, m, slot):
                    act.wait_ge(landed[slot], due(landed[slot], 16 * (m + 1)))
                    act.wait_ge(pair_done, due(pair_done, p - 1))
                    af(WH[:, slot, :], raw[:, slot, :], ACT.Copy).then_inc(wH_ready, 1)

                def high_at(p):
                    high(p, p // 2, p % 2)

                def split_x(stage, p):
                    for n, k in enumerate(X_ORDER):
                        act.wait_ge(x_ready, due(x_ready, DT * stage + n + 1 - DT))
                        g = gains[:, G_PRE[stage] + k:G_PRE[stage] + k + 1]
                        af(xH[:, k, :], x[:, k, :], ACT.Copy, scale=g)
                        if n >= 2:
                            act.wait_ge(xL_ready, due(xL_ready, DT * stage + n - 1))
                        af(xg[n % 2][:], x[:, k, :], ACT.Copy, scale=g).then_inc(xH_ready, 1)
                    high_at(p)
                    for n, k in enumerate(X_ORDER):
                        square(2 * DT * stage + n, x[:, k, :])

                def square(n, src):
                    if n >= 2:
                        act.wait_ge(sq_used, due(sq_used, n - 1))
                    af(sq[:, n % 2, :], src, ACT.Square).then_inc(sq_ready, 1)

                def keep_spread(norm, kept, dst, bank, scale):
                    act.wait_ge(spread_ready, due(spread_ready, norm + 1))
                    af(dst[:], ps[:, bank, :], ACT.Copy, scale=scale).then_inc(spread_kept, 1)

                def hidden(n, f):
                    act.wait_ge(gu_scaled, due(gu_scaled, n + 1))
                    af(gate[:], gate[:], ACT.Silu).then_inc(silu_ready, 1)
                    act.wait_ge(h_ready, due(h_ready, n + 1))
                    af(hH[:, f, :], up[:], ACT.Copy).then_inc(hH_ready, 1)

                def after(stage, norm, scale, p):
                    for n, d in enumerate(F_ORDER):
                        if n < DT - 1:
                            act.wait_ge(f_ready, due(f_ready, (DT - 1) * stage + n + 1))
                        else:
                            act.wait_ge(pair_done, due(pair_done, p + 1))
                        square(2 * DT * stage + DT + n, ps[:, d, :])
                    keep_spread(norm, 0, rstd_f, 0, scale)

                def ffn(stage, f_stage, base, norm):
                    if stage == 0:
                        high_at(base)
                    split_x(stage, base + 1)
                    keep_spread(norm, 0, rstd_x, 5, 1.0)
                    high_at(base + 2)
                    hidden(FT * f_stage, 0)
                    slot = (base + 1) % 2
                    with act.Fori(1, FT // 2) as i:
                        for j in range(2):
                            f = 2 * i + j - 1
                            p = base + 2 + f
                            high(p, (base + 1 + j) // 2 + i, (base + 1 + j) % 2)
                            hidden(FT * f_stage + f, f)
                    high_at(base + FT + 1)
                    hidden(FT * (f_stage + 1) - 1, FT - 1)
                    with act.Fori(1, FT // 4) as m:
                        for j in range(2):
                            p = base + FT + 2 * m + j
                            high(p, (base + FT + j) // 2 + m, (base + FT + j) % 2)
                    high_at(base + FT + FT // 2 - 1)
                    if stage == 0:
                        high_at(base + FT + FT // 2)
                    after(stage, norm + 1, 0.5, base + FFN_PAIRS - 1)

                def mixer(base, norm):
                    split_x(1, base + 1)
                    keep_spread(norm, 0, rstd_x, 7, 1.0)
                    act.dma_start(const[:], consts).then_inc(mix_landed, 16)
                    act.dma_start(wgu[QK:QK + GATE_RANK, :], w_gate_up[layer]).then_inc(mix_landed, 16)
                    act.dma_start(bias[QK:QK + 1, :], b_gate[layer]).then_inc(mix_landed, 16)
                    act.dma_start(cos[:].bitcast(I32), positions.partition_broadcast(P)).then_inc(mix_landed, 16)
                    act.dma_start(wq[:, 0, :], w_q_up[layer, 0]).then_inc(mix_landed, 16)
                    act.dma_start(wq[:, 1, :], w_q_up[layer, 1]).then_inc(mix_landed, 16)
                    act.dma_start(wkv[:], w_kv_up[layer]).then_inc(mix_landed, 16)
                    high_at(base + 2)
                    high_at(base + 3)
                    act.wait_ge(angle_ready, due(angle_ready, 1))
                    af(cos[:], sin[:], ACT.Sin, scale=0.5).then_inc(sine_ready, 1)
                    act.wait_ge(sine_ready, due(sine_ready, 1))
                    af(sin[:], sin[:], ACT.Sin).then_inc(sine_ready, 1)
                    act.wait_ge(in_kept, due(in_kept, 3))
                    act.wait_ge(mean_ready, due(mean_ready, norm + 1))
                    for j in range(2):
                        af(sq[:, j, :], mq[:, j, :], ACT.Square).then_inc(latent_sq, 1)
                    af(acc[:], ckv[:], ACT.Square).then_inc(latent_sq, 1)
                    high_at(base + 4)

                    def keep_values(i):
                        banks = (2, 3) if i == 0 else (4, 5)
                        act.wait_ge(pair_done, due(pair_done, base + 5 + i))
                        for b in range(BLK):
                            last = af(v_tok[:, b, i * GV:(i + 1) * GV],
                                      ps[:, banks[b // 2], (b % 2) * GV:(b % 2 + 1) * GV], ACT.Copy,
                                      scale=rx_col[:, b:b + 1])
                        last.then_inc(v_kept, 1)

                    high_at(base + 5)
                    keep_values(0)
                    act.wait_ge(z_ready, due(z_ready, 1))
                    link(af(kf[:], ps[:, 7, :], ACT.Abs))
                    link(af(kf[:], kf[:], ACT.Exp, scale=-1.0))
                    af(kf[:], kf[:], ACT.Ln, bias=1.0).then_inc(soft_ready, 1)
                    high_at(base + 6)
                    keep_values(1)
                    act.wait_ge(b_last_ready, due(b_last_ready, 1))
                    af(eb[:], ps[:, 7, :], ACT.Exp).then_inc(exp_ready, 1)
                    af(enb[:], ps[:, 7, :], ACT.Exp, scale=-1.0).then_inc(exp_ready, 1)
                    for n in range(NCHUNK):
                        tok = slice(n * CHUNK, (n + 1) * CHUNK)
                        last = af(zg[:, tok], ps[:, 7, tok], ACT.Exp, bias=b_last[:, n:n + 1], scale=-1.0)
                    last.then_inc(exp_ready, 1)
                    high_at(base + 7)
                    for t in range(4):
                        act.wait_ge(in_kept, due(in_kept, 9 + t))
                        af(gates[t][:], gates[t][:], ACT.Silu).then_inc(gate_silu, 1)
                    high_at(base + 8)
                    high_at(base + 9)
                    act.wait_ge(kt_psum, due(kt_psum, 1))
                    af(kt_gla[:].rearrange("p b f -> p (b f)"), ps[:, 6, :], ACT.Copy).then_inc(kt_kept, 1)
                    act.wait_ge(kt_psum, due(kt_psum, 2))
                    af(kt_ret[:].rearrange("p b f -> p (b f)"), ps[:, 7, :], ACT.Copy).then_inc(kt_kept, 1)
                    act.wait_ge(cleared, due(cleared, 1))
                    for b in range(BLK):
                        act.wait_ge(gr_scored, due(gr_scored, b + 1))
                        if b >= 1:
                            act.wait_ge(gr_used, due(gr_used, b))
                        up_scores = ps[:, 5, :].rearrange("p (h i) -> p h i", h=GH)
                        for c in range(2):
                            r = slice(c * CHUNK, (c + 1) * CHUNK)
                            last = af(attn_g[r, :, r], up_scores[r, :, r], ACT.Copy)
                        last.then_inc(up_kept, 1)
                    act.wait_ge(gr_used, due(gr_used, BLK))
                    for t in range(4):
                        af(o_tok[t][:], ps[:, t, :], ACT.Copy).then_inc(o_kept, 1)
                        if t >= 2:
                            act.wait_ge(o_sq_used, due(o_sq_used, t - 1))
                        af(sq[:, t % 2, :], ps[:, t, :], ACT.Square).then_inc(o_sq, 1)
                    for b in range(BLK):
                        act.wait_ge(vm_psum, due(vm_psum, b + 1))
                        af(v_mla[:, b, :], ps[:, 2 + b % 2, :], ACT.Copy).then_inc(vm_kept, 1)

                    def keep_q(h):
                        act.wait_ge(q_psum, due(q_psum, h + 1))
                        if h >= 2:
                            act.wait_ge(scored, due(scored, (h - 1) * BLK))
                        af(qT[0:QK, h % 2, :], ps[0:QK, 0, :], ACT.Copy).then_inc(q_kept, 1)

                    def keep_k(h):
                        act.wait_ge(k_psum, due(k_psum, h + 1))
                        af(kT[0:NOPE, h % 2, :], ps[0:NOPE, 2, :], ACT.Copy).then_inc(k_kept, 1)

                    keep_q(0)
                    keep_k(0)
                    for t in range(4):
                        act.wait_ge(o_gated, due(o_gated, t + 1))
                        af(xH[:, 4 + t, :], o_tok[t][:], ACT.Copy).then_inc(mixH_ready, 1)

                    def exps(h, b):
                        n = h * BLK + b
                        width = (b + 1) * P
                        act.wait_ge(top_ready, due(top_ready, n + 1))
                        if n >= 2:
                            act.wait_ge(turned, due(turned, n - 1))
                        af(prob[:, n % 2, 0:width], ps[:, 3 + n % 2, 0:width], ACT.Exp, scale=QK ** -0.5,
                           bias=minus_top[:, n % 2:n % 2 + 1],
                           accum_out=total[:, n % 2:n % 2 + 1]).then_inc(exped, 1)

                    def keep_turn(h, b):
                        n = h * BLK + b
                        act.wait_ge(turned, due(turned, n + 1))
                        if h >= 1 and b == 0:
                            act.wait_ge(head_done, due(head_done, h))
                        at = b * (b + 1) // 2 * P
                        af(probT[:, at:at + (b + 1) * P], ps[:, 5 + n % 2, 0:(b + 1) * P],
                           ACT.Copy).then_inc(turn_kept, 1)

                    for h in range(HEADS):
                        exps(h, 0)
                        exps(h, 1)
                        if h + 1 < HEADS:
                            keep_q(h + 1)
                        keep_turn(h, 0)
                        exps(h, 2)
                        if h + 1 < HEADS:
                            keep_k(h + 1)
                        keep_turn(h, 1)
                        exps(h, 3)
                        keep_turn(h, 2)
                        keep_turn(h, 3)
                        if h % 2:
                            act.wait_ge(head_done, due(head_done, h + 1))
                            af(xH[:, h // 2, :], ps[:, 7, :], ACT.Copy).then_inc(mixH_ready, 1)
                    for i in range(2, OUT_PAIRS + 1):
                        high_at(base + IN_PAIRS + i)
                    after(1, norm + 3, 1.0, base + MIX_PAIRS - 1)

                ffn(0, 0, 0, 0)
                mixer(FFN_PAIRS, 2)
                ffn(2, 1, FFN_PAIRS + MIX_PAIRS, 6)

        @block.vector
        def _(dve):
            tt, ts, stt = nc.vector.tensor_tensor, nc.vector.tensor_scalar, nc.vector.scalar_tensor_tensor
            steps = [0]
            nc.vector.memset(ones[:], 1.0)
            nc.vector.memset(ones_row[:], 1.0)
            nc.vector.memset(minus_half[:], -0.5).then_inc(start_ready, 1)
            dve.wait_ge(start_landed, 48)
            dve.sem_inc(x_ready, DT)
            with dve.Fori(0, DEPTH) as layer:
                due = counter(layer)
                steps[0] = 0

                def link(instruction):
                    steps[0] += 1
                    instruction.then_inc(dve_step, 1)
                    dve.wait_ge(dve_step, due(dve_step, steps[0]))

                nc.vector.tensor_copy(gains[:], gains_all[:, bass.ds(layer, 1), :].rearrange("p a g -> p (a g)")).then_inc(gains_ready, 1)
                dve.wait_ge(gains_ready, due(gains_ready, 1))

                def lows(p, slot):
                    dve.wait_ge(wH_ready, due(wH_ready, p + 1))
                    tt(WL[:, slot, :], raw[:, slot, :], WH[:, slot, :].bitcast(F32), ALU.subtract).then_inc(wL_ready, 1)

                def low_at(p):
                    lows(p, p % 2)

                def sum_squares(n0):
                    for n in range(DT):
                        dve.wait_ge(sq_ready, due(sq_ready, n0 + n + 1))
                        if n:
                            dve.wait_ge(sq_used, due(sq_used, n0 + n))
                            tt(acc[:], acc[:], sq[:, (n0 + n) % 2, :], ALU.add).then_inc(sq_used, 1)
                        else:
                            nc.vector.tensor_copy(acc[:], sq[:, (n0 + n) % 2, :]).then_inc(sq_used, 1)

                def mean_of(norm, bank, width):
                    dve.wait_ge(col_ready, due(col_ready, norm + 1))
                    ts(mean[:, 0:BLK], ps[:, bank, 0:BLK], 1.0 / width, EPS, ALU.mult, ALU.add).then_inc(mean_ready, 1)

                def hidden(n, f, banks, first=False):
                    if not first:
                        dve.wait_ge(hL_ready, due(hL_ready, n))
                    for j, dst in enumerate((gate, up)):
                        last = tt(dst[:], ps[:, banks[j], :], rstd_x[:], ALU.mult)
                    last.then_inc(gu_scaled, 1)
                    dve.wait_ge(silu_ready, due(silu_ready, n + 1))
                    tt(up[:], gate[:], up[:], ALU.mult).then_inc(h_ready, 1)
                    dve.wait_ge(hH_ready, due(hH_ready, n + 1))
                    tt(hL[:, f, :], up[:], hH[:, f, :].bitcast(F32), ALU.subtract).then_inc(hL_ready, 1)

                def after(stage, norm, width):
                    n0 = 2 * DT * stage + DT
                    for n in range(DT):
                        dve.wait_ge(sq_ready, due(sq_ready, n0 + n + 1))
                        if n:
                            dve.wait_ge(sq_used, due(sq_used, n0 + n))
                            tt(acc[:], acc[:], sq[:, (n0 + n) % 2, :], ALU.add).then_inc(sq_used, 1)
                        else:
                            nc.vector.tensor_copy(acc[:], sq[:, (n0 + n) % 2, :]).then_inc(sq_used, 1)
                        if F_ORDER[n] == 0:
                            if stage == 1:
                                dve.wait_ge(mixL_ready, due(mixL_ready, 8))
                            nc.vector.tensor_copy(f0[:], ps[:, 0, :]).then_inc(f0_ready, 1)
                    mean_of(norm, 0, D)
                    dve.wait_ge(spread_kept, due(spread_kept, 2 * stage + 2))
                    for n, k in enumerate(X_ORDER):
                        src = f0[:] if k == 0 else ps[:, k, :]
                        link(tt(acc[:], src, rstd_f[:], ALU.mult))
                        g = G_POST[stage] + k
                        stt(x[:, k, :], acc[:], gains[:, g:g + 1], x[:, k, :], ALU.mult,
                            ALU.add).then_inc(x_ready, 1)
                        dve.wait_ge(x_ready, due(x_ready, DT * stage + n + 1))

                def ffn(stage, f_stage, base, norm):
                    n0 = FT * f_stage
                    if stage == 0:
                        low_at(base)
                    low_at(base + 1)
                    sum_squares(2 * DT * stage)
                    mean_of(norm, 4, D)
                    low_at(base + 2)
                    dve.wait_ge(spread_kept, due(spread_kept, 2 * stage + 1))
                    hidden(n0, 0, (0, 1), first=True)
                    with dve.Fori(1, FT // 2) as i:
                        for j in range(2):
                            f = 2 * i + j - 1
                            lows(base + 2 + f, (base + 1 + j) % 2)
                            dve.wait_ge(pair_done, due(pair_done, base + f + 1))
                            hidden(n0 + f, f, (2, 3) if j == 0 else (0, 1))
                    low_at(base + FT + 1)
                    dve.wait_ge(pair_done, due(pair_done, base + FT))
                    hidden(n0 + FT - 1, FT - 1, (2, 3))
                    with dve.Fori(1, FT // 4) as m:
                        for j in range(2):
                            lows(base + FT + 2 * m + j, (base + FT + j) % 2)
                    low_at(base + FT + FT // 2 - 1)
                    if stage == 0:
                        low_at(base + FT + FT // 2)
                    after(stage, norm + 1, D)

                def mixer(base, norm):
                    low_at(base + 1)
                    sum_squares(2 * DT)
                    mean_of(norm, 6, D)
                    low_at(base + 2)
                    low_at(base + 3)

                    def keep(bank, dst, r0=0, r1=P):
                        tt(dst[r0:r1], ps[r0:r1, bank, :], rstd_x[r0:r1, :], ALU.mult).then_inc(in_kept, 1)

                    dve.wait_ge(spread_kept, due(spread_kept, 3))
                    nc.vector.tensor_copy(rx_col[:], rstd[:, 0:BLK])
                    dve.wait_ge(pair_done, due(pair_done, base + 1))
                    keep(0, mq[:, 0, :])
                    keep(1, mq[:, 1, :])
                    dve.wait_ge(pair_done, due(pair_done, base + 2))
                    keep(2, ckv)
                    keep(3, krgg, NOPE, QK + GATE_RANK)
                    dve.wait_ge(mix_landed, due(mix_landed, 16 * 7))
                    link(nc.vector.tensor_copy(sin[:], cos[:].bitcast(I32)))
                    link(ts(sin[:], sin[:], inv_freq, None, ALU.mult))
                    link(ts(cos[:], sin[:], 1.0 / TWO_PI, ROUND, ALU.mult, ALU.add))
                    link(ts(cos[:], cos[:], ROUND, None, ALU.subtract))
                    for c in (C1, C2, C3):
                        link(stt(sin[:], cos[:], -c, sin[:], ALU.mult, ALU.add))
                    ts(sin[:], sin[:], 3.1415925, -3.1415925, ALU.min, ALU.max).then_inc(angle_ready, 1)
                    dve.wait_ge(pair_done, due(pair_done, base + 3))
                    keep(4, gq)
                    keep(5, gk)
                    low_at(base + 4)
                    dve.wait_ge(sine_ready, due(sine_ready, 2))
                    link(tt(cos[:], cos[:], cos[:], ALU.mult))
                    ts(cos[:], cos[:], -2.0, 1.0, ALU.mult, ALU.add).then_inc(rope_ready, 1)
                    dve.wait_ge(pair_done, due(pair_done, base + 4))
                    keep(0, rq)
                    keep(1, rk)
                    low_at(base + 5)
                    dve.wait_ge(col_ready, due(col_ready, norm + 2))
                    ts(mean[:, 0:BLK], ps[:, 6, 0:BLK], 1.0 / QR, EPS, ALU.mult, ALU.add)
                    ts(mean[:, BLK:2 * BLK], ps[:, 6, BLK:2 * BLK], 1.0 / KVR, EPS, ALU.mult, ALU.add).then_inc(mean_ready, 1)
                    dve.wait_ge(z_ready, due(z_ready, 1))
                    dve.wait_ge(soft_ready, due(soft_ready, 1))
                    stt(zg[:], ps[:, 7, :], 0.0, kf[:], ALU.min, ALU.subtract).then_inc(log_ready, 1)
                    low_at(base + 6)
                    dve.wait_ge(cum_ready, due(cum_ready, 1))
                    nc.vector.tensor_copy(b_last[:], ps[:, 7, CHUNK - 1::CHUNK]).then_inc(b_last_ready, 1)
                    low_at(base + 7)
                    dve.wait_ge(spread_ready, due(spread_ready, norm + 2))
                    for j in range(2):
                        stt(mq[:, j, :], mq[:, j, :], gains[:, G_Q + j:G_Q + j + 1], ps[:, 6, :], ALU.mult,
                            ALU.mult).then_inc(latent_ready, 1)
                    stt(ckv[:], ckv[:], gains[:, G_KV:G_KV + 1], ps[:, 4, :], ALU.mult, ALU.mult).then_inc(latent_ready, 1)
                    dve.wait_ge(exp_ready, due(exp_ready, 3))
                    tt(kf[:], gk[:], enb[:], ALU.mult).then_inc(k_ready, 1)
                    tt(kb[:], gk[:], eb[:], ALU.mult).then_inc(k_ready, 1)
                    tt(zg[:], zg[:], gk[:], ALU.mult).then_inc(k_ready, 1)
                    for t in range(4):
                        if t % 2 == 0:
                            dve.wait_ge(pair_done, due(pair_done, base + 7 + t // 2))
                        keep((0, 1, 2, 3)[t], gates[t])
                    dve.wait_ge(rope_ready, due(rope_ready, 1))
                    for n, (t, bank, r0, r1) in enumerate(((rq, 5, 0, P), (rk, 0, 0, P), (krgg, 1, NOPE, QK))):
                        dve.wait_ge(rot_ready, due(rot_ready, n + 1))
                        tmp = attn_r[:].rearrange("p h i -> p (h i)")[r0:r1, :]
                        link(tt(t[r0:r1, :], t[r0:r1, :], cos[r0:r1, :], ALU.mult))
                        link(tt(tmp, ps[r0:r1, bank, :], sin[r0:r1, :], ALU.mult))
                        last = tt(t[r0:r1, :], t[r0:r1, :], tmp, ALU.add)
                        if n == 1:
                            link(last)
                            tt(ks_ret[:].rearrange("p (n i) -> p n i", n=NCHUNK), rk[:].rearrange("p (n i) -> p n i", n=NCHUNK),
                               k_dec.rearrange("p (o i) -> p o i", o=1).broadcast_to([P, NCHUNK, CHUNK]),
                               ALU.mult).then_inc(ret_ready, 1)
                        elif n == 0:
                            last.then_inc(ret_ready, 1)
                        else:
                            last.then_inc(kpe_ready, 1)

                    def queries(b):
                        if b >= 2:
                            dve.wait_ge(gr_used, due(gr_used, b - 1))
                        tok = slice(b * P, (b + 1) * P)
                        for h in range(GH):
                            r = slice(h * DK, (h + 1) * DK)
                            stt(qx[r, 0, b % 2, h, :], gq[r, tok], DK ** -0.5, eb[r, tok], ALU.mult, ALU.mult)
                            last = stt(qx[r, 1, b % 2, h, :], gq[r, tok], DK ** -0.5, enb[r, tok], ALU.mult, ALU.mult)
                        last.then_inc(qg_ready, 1)

                    dve.wait_ge(cleared, due(cleared, 1))
                    queries(0)
                    queries(1)
                    for b in range(BLK):
                        banks = (4, 5) if b % 2 == 0 else (2, 3)
                        dve.wait_ge(ds_ready, due(ds_ready, b + 1))
                        for c in range(2 if b < BLK - 1 else 1):
                            n = 2 * b + c
                            ds_gla, ds_ret = ps[:, banks[c], 0:GV], ps[:, banks[c], GV:2 * GV]
                            if n == 0:
                                nc.vector.tensor_copy(s_gla[:, 0, :], ds_gla)
                                last = nc.vector.tensor_copy(s_ret[:, 0, :], ds_ret)
                            else:
                                at = n * CHUNK + CHUNK - 1
                                stt(s_gla[:, n, :], s_gla[:, n - 1, :], eb[:, at:at + 1], ds_gla,
                                    ALU.mult, ALU.add)
                                last = stt(s_ret[:, n, :], s_ret[:, n - 1, :], chunk_dec, ds_ret,
                                           ALU.mult, ALU.add)
                            if c == 0 and b < BLK - 1:
                                link(last)
                        last.then_inc(state_ready, 1)
                        dve.wait_ge(state_ready, due(state_ready, b + 1))
                    for b in range(BLK):
                        dve.wait_ge(gr_scored, due(gr_scored, b + 1))
                        if b >= 1:
                            dve.wait_ge(gr_used, due(gr_used, b))
                        tt(attn_r[:], ps[:, 6, :].rearrange("p (h i) -> p h i", h=GH), decay, ALU.mult)
                        dve.wait_ge(up_kept, due(up_kept, b + 1))
                        dve.sem_inc(dve_passed)
                        scores = ps[:, 4, :].rearrange("p (h i) -> p h i", h=GH)
                        for c in range(2):
                            r = slice(c * CHUNK, (c + 1) * CHUNK)
                            last = nc.vector.copy_predicated(
                                attn_g[r, :, r],
                                low[r, :].rearrange("p (o i) -> p o i", o=1).broadcast_to([CHUNK, GH, CHUNK]),
                                scores[r, :, r])
                        last.then_inc(gr_ready, 1)
                        if b + 2 < BLK:
                            queries(b + 2)
                    dve.wait_ge(col_ready, due(col_ready, norm + 3))
                    ts(mean[:], ps[:, 7, 0:32], 1.0 / DV, EPS, ALU.mult, ALU.add).then_inc(mean_ready, 1)

                    def turn_q(h):
                        dve.wait_ge(q_rot, due(q_rot, h + 1))
                        q = qT[NOPE:QK, h % 2, :]
                        tmp = acc[NOPE:QK, :]
                        link(tt(q, q, cos[NOPE:QK, :], ALU.mult))
                        link(tt(tmp, ps[NOPE:QK, 1, :], sin[NOPE:QK, :], ALU.mult))
                        tt(q, q, tmp, ALU.add).then_inc(q_ready, 1)

                    turn_q(0)
                    dve.wait_ge(spread_ready, due(spread_ready, norm + 3))
                    dve.wait_ge(gate_silu, due(gate_silu, 4))
                    dve.wait_ge(o_kept, due(o_kept, 4))
                    for t in range(4):
                        g = G_GLA if t < 2 else G_RET
                        link(stt(o_tok[t][:], o_tok[t][:], gains[:, g:g + 1], ps[:, 4 + t, :], ALU.mult, ALU.mult))
                        tt(o_tok[t][:], o_tok[t][:], gates[t][:], ALU.mult).then_inc(o_gated, 1)
                    for t in range(4):
                        dve.wait_ge(mixH_ready, due(mixH_ready, t + 1))
                        tt(xL[:, 4 + t, :], o_tok[t][:], xH[:, 4 + t, :].bitcast(F32), ALU.subtract).then_inc(mixL_ready, 1)

                    def tops(h, b):
                        n = h * BLK + b
                        width = (b + 1) * P
                        dve.wait_ge(scored, due(scored, n + 1))
                        s = ps[:, 3 + n % 2, :]
                        link(nc.vector.memset(s[0:CHUNK, width - CHUNK:width], MASKED))
                        link(nc.vector.reduce_max(top[:, n % 2:n % 2 + 1], s[:, 0:width], AX_X))
                        ts(minus_top[:, n % 2:n % 2 + 1], top[:, n % 2:n % 2 + 1], -(QK ** -0.5), None,
                           ALU.mult).then_inc(top_ready, 1)

                    def probs(h, b):
                        n = h * BLK + b
                        dve.wait_ge(exped, due(exped, n + 1))
                        link(nc.vector.reciprocal(share[:, n % 2:n % 2 + 1], total[:, n % 2:n % 2 + 1]))
                        pr = prob[:, n % 2, 0:(b + 1) * P]
                        ts(pr, pr, share[:, n % 2:n % 2 + 1], None, ALU.mult).then_inc(prob_ready, 1)

                    for h in range(HEADS):
                        tops(h, 0)
                        tops(h, 1)
                        probs(h, 0)
                        tops(h, 2)
                        probs(h, 1)
                        tops(h, 3)
                        if h + 1 < HEADS:
                            turn_q(h + 1)
                        probs(h, 2)
                        probs(h, 3)
                        if h % 2:
                            dve.wait_ge(mixH_ready, due(mixH_ready, 4 + h // 2 + 1))
                            tt(xL[:, h // 2, :], ps[:, 7, :], xH[:, h // 2, :].bitcast(F32),
                               ALU.subtract).then_inc(mixL_ready, 1)
                    for i in range(OUT_PAIRS + 1):
                        low_at(base + IN_PAIRS + i)
                    after(1, norm + 3, D)

                ffn(0, 0, 0, 0)
                mixer(FFN_PAIRS, 2)
                ffn(2, 1, FFN_PAIRS + MIX_PAIRS, 6)

        @block.gpsimd
        def _(pool):
            pool.wait_ge(start_ready, 1)
            with pool.Fori(0, DEPTH) as layer:
                due = counter(layer)
                def split_x(stage):
                    for n, k in enumerate(X_ORDER):
                        pool.wait_ge(xH_ready, due(xH_ready, DT * stage + n + 1))
                        nc.gpsimd.tensor_tensor(xL[:, k, :], xg[n % 2][:], xH[:, k, :].bitcast(F32),
                                                ALU.subtract).then_inc(xL_ready, 1)

                def power(norm, width):
                    pool.wait_ge(mean_ready, due(mean_ready, norm + 1))
                    nc.gpsimd.tensor_tensor(rstd[:, 0:width], mean[:, 0:width], minus_half[:, 0:width],
                                            ALU.pow).then_inc(rstd_ready, 1)

                split_x(0)
                power(0, 4)
                power(1, 4)
                split_x(1)
                power(2, 4)
                pool.wait_ge(spread_kept, due(spread_kept, 3))
                pool.sem_inc(pool_passed)
                nc.gpsimd.memset(attn_g[:].rearrange("p h i -> p (h i)"), 0.0)
                nc.gpsimd.memset(qx[:].rearrange("p a b h i -> p (a b h i)"), 0.0).then_inc(cleared, 1)
                pool.wait_ge(cleared, due(cleared, 1))
                power(3, 8)

                def queries(b):
                    for h in range(GH):
                        r = slice(h * DK, (h + 1) * DK)
                        last = nc.gpsimd.tensor_tensor(
                            qx[r, 2, b % 2, h, :].rearrange("p (c i) -> p c i", c=2),
                            rq[r, b * P:(b + 1) * P].rearrange("p (c i) -> p c i", c=2),
                            q_dec[r, :].rearrange("p (o i) -> p o i", o=1).broadcast_to([DK, 2, CHUNK]), ALU.mult)
                    last.then_inc(qr_ready, 1)

                pool.wait_ge(mix_landed, due(mix_landed, 16 * 7))
                pool.wait_ge(ret_ready, due(ret_ready, 1))
                for b in range(BLK):
                    if b >= 2:
                        pool.wait_ge(gr_used, due(gr_used, b - 1))
                    queries(b)
                power(4, 32)
                pool.wait_ge(vm_psum, due(vm_psum, 1))
                pool.wait_ge(rstd_ready, due(rstd_ready, 5))
                pool.sem_inc(pool_passed)
                for j in range(2):
                    if j:
                        pool.wait_ge(kpe_copied, due(kpe_copied, 1))
                        pool.sem_inc(pool_passed)
                    nc.gpsimd.tensor_copy(kT[NOPE:QK, j, :], krgg[NOPE:QK, :]).then_inc(kpe_copied, 1)
                pool.wait_ge(kpe_copied, due(kpe_copied, 2))
                pool.sem_inc(pool_passed)
                power(5, 4)
                split_x(2)
                power(6, 4)
                power(7, 4)


def pack(np, inputs):
    def tiles(w):
        return w.reshape(DT, P, w.shape[1]).transpose(1, 0, 2).reshape(P, -1)

    def rows(w):
        return w.reshape(-1, 2, P, D).transpose(0, 2, 1, 3).reshape(-1, P, 2 * SLAB)

    blocks = []
    for l in range(DEPTH):
        def ffn(name):
            wg, wu, wd = (inputs[f"{name}_w_{k}"][l] for k in ("gate", "up", "down"))
            for f in range(FT):
                c = slice(f * P, (f + 1) * P)
                blocks.append(np.concatenate([tiles(wg[:, c]), tiles(wu[:, c])], 1)[None])
            blocks.append(rows(wd))

        ffn("ffn1")
        w = inputs["w_in"][l]
        at = np.cumsum([0, 256, 128, 32, 128, 128, 256, 16, 256, 128, 128, 256, 256])
        mq, mkv, mkr, gq, gk, gv, gg, gr, rq, rk, rv, rg = (int(a) for a in at[:-1])
        kr_gg = np.concatenate([w[:, mkr - NOPE:mkr + ROPE], w[:, gg:gg + GATE_RANK], np.zeros((D, P - QK - GATE_RANK), w.dtype)], 1)
        for a, b in ((w[:, mq:mq + P], w[:, mq + P:mq + 2 * P]), (w[:, mkv:mkv + P], kr_gg),
                     (w[:, gq:gq + P], w[:, gk:gk + P]), (w[:, rq:rq + P], w[:, rk:rk + P])):
            blocks.append(np.concatenate([tiles(a), tiles(b)], 1)[None])
        for a in (gv, rv):
            blocks.append(tiles(w[:, a:a + GV])[None])
        for a in (gr, rg):
            blocks.append(np.concatenate([tiles(w[:, a:a + P]), tiles(w[:, a + P:a + 2 * P])], 1)[None])
        blocks.append(rows(inputs["w_out"][l]))
        ffn("ffn2")
    cols = [inputs[n].reshape(DEPTH, -1, P) for n in ("ffn1_pre_g", "ffn1_post_g", "mix_pre_g", "mix_post_g",
                                                     "ffn2_pre_g", "ffn2_post_g", "mla_q_norm_g", "mla_kv_norm_g")]
    cols += [np.concatenate([inputs[n]] * 2, 1)[:, None, :] for n in ("gla_norm_g", "ret_norm_g")]
    return {
        "x_in": inputs["x"][0].T.reshape(DT, P, SEQ).transpose(1, 0, 2),
        "positions": inputs["positions"].reshape(SEQ),
        "stream": np.concatenate(blocks, 0),
        "gains_in": np.concatenate(cols, 1).transpose(0, 2, 1),
        "w_q_up": inputs["mla_w_q_up"].reshape(DEPTH, 2, P, HEADS * QK),
        "w_kv_up": inputs["mla_w_kv_up"],
        "w_gate_up": inputs["gla_w_gate_up"],
        "b_gate": inputs["gla_b_gate"].reshape(DEPTH, 1, GH * DK),
        "consts": constants(np),
    }


def constants(np):
    c = np.zeros((P, CONSTS), np.float64)
    p, i = np.arange(P)[:, None], np.arange(P)[None, :]
    same = p // CHUNK == i // CHUNK
    c[:, C_ID:C_ID + P] = np.eye(P)
    c[:, C_TRI:C_TRI + P] = (same & (p <= i)) / TAU
    half = ROPE // 2
    group = p // ROPE == i // ROPE
    c[:, C_ROT:C_ROT + P] = (group & (p == i - half)) * 1.0 - (group & (p == i + half)) * 1.0
    gamma = np.log1p(-np.exp2(-5.0 - np.arange(GH)))
    for h in range(GH):
        d = np.abs(p % CHUNK - i % CHUNK) - (i % CHUNK + 1.0)
        c[:, C_DEC + h * P:C_DEC + (h + 1) * P] = same * np.exp(gamma[h] * d) * DK ** -0.5
    j = np.arange(CHUNK)[None, :]
    c[:, C_LOW:C_LOW + CHUNK] = p % CHUNK <= j
    g = gamma[np.arange(P) // DK][:, None]
    c[:, C_QDEC:C_QDEC + CHUNK] = np.exp(g * (j + 1.0))
    c[:, C_KDEC:C_KDEC + CHUNK] = np.exp(g * (CHUNK - 1.0 - j)) * DK ** -0.5
    c[:, C_CDEC:C_CDEC + 1] = np.exp(g * CHUNK)
    c[:, C_HSEL:C_HSEL + 2] = p // DV == np.arange(2)[None, :]
    c[:, C_INV:C_INV + 1] = 10000.0 ** (-(2.0 * (p % half)) / ROPE)
    return c.astype(np.float32)


def kernel(**inputs):
    import numpy as np
    import concourse.bacc as bacc
    from concourse.bass_utils import run_bass_kernel_spmd

    nc = bacc.Bacc("TRN2", target_bir_lowering=False, num_devices=1)
    arrays = {k: np.ascontiguousarray(v) for k, v in pack(np, {k: np.asarray(v) for k, v in inputs.items()}).items()}
    args = {k: nc.dram_tensor(k, v.shape, mybir.dt.from_np(v.dtype), kind="ExternalInput").ap()
            for k, v in arrays.items()}
    out = nc.dram_tensor("out", (P, DT, SEQ), F32, kind="ExternalOutput").ap()
    hybrid_trunk(nc, out=out, **args)
    r = run_bass_kernel_spmd(nc, [arrays], core_ids=[0])
    y = r.results[0]["out"]
    return np.ascontiguousarray(y.transpose(1, 0, 2).reshape(D, SEQ).T)[None]
```

```python
from contextlib import ExitStack

import concourse.bass as bass
from concourse import mybir

ALU = mybir.AluOpType
ACT = mybir.ActivationFunctionType
F32 = mybir.dt.float32
F32R = mybir.dt.float32r
I32 = mybir.dt.int32
AX_X = mybir.AxisListType.X

P = 128
SEQ = 512
D = 1024
DT = D // P
DEPTH = 2
FF = 2816
FT = FF // P
CHUNK = 64
NCHUNK = SEQ // CHUNK
BLK = SEQ // P
EPS = 1e-6
TAU = 16.0
HEADS = 8
NOPE, ROPE, DV = 64, 32, 64
QK = NOPE + ROPE
QR, KVR = 256, 128
GH, DK = 4, 32
GV = GH * DV
GATE_RANK = 16
MASKED = -3.0e38

FFN_PAIRS = FT + FT // 2
IN_PAIRS, OUT_PAIRS = 8, 4
MIX_PAIRS = IN_PAIRS + OUT_PAIRS
PAIRS = 2 * FFN_PAIRS + MIX_PAIRS
SLAB = 8 * P
SQUARES = 2 * DT - 1
NORMS = 8

G_PRE = (0, 16, 32)
G_POST = (8, 24, 40)
G_Q, G_KV, G_GLA, G_RET = 48, 50, 51, 52
GAINS = 53

C_ID = 0
C_TRI = C_ID + P
C_ROT = C_TRI + P
C_DEC = C_ROT + P
C_LOW = C_DEC + GH * P
C_QDEC = C_LOW + CHUNK
C_KDEC = C_QDEC + CHUNK
C_CDEC = C_KDEC + CHUNK
C_SIGN = C_CDEC + 1
C_TWICE = C_SIGN + 1
C_HSEL = C_TWICE + 64
C_INV = C_HSEL + 2
CONSTS = C_INV + 1

X_ORDER = [0, 1, 2, 3, 4, 5, 6, 7]
F_ORDER = [0, 1, 2, 3, 4, 5, 6, 7]
FFN_START = [4, 5, 6, 7, 0, 1, 2, 3]
MIX_START, MIX_REST = [0, 1, 6], [2, 3, 4, 5, 7]

TWO_PI = 6.283185307179586
C1 = 6.28125
C2 = 0.0019350051879882812
C3 = TWO_PI - C1 - C2
ROUND = 12582912.0

QK_BANK, LIN_BANKS, OUT_BANK = 0, (1, 6), 7
RING = (2, 3, 4, 5)
STEPS = HEADS * BLK
AHEAD = 3
LIN_STEP = 3
NORM_STEP = LIN_STEP + 3 * BLK
GATE_STEP = NORM_STEP + 5


DVE_STEPS = 120
ACT_STEPS = 2



def hybrid_trunk(nc, x_in, positions, stream, gains_in, w_q_up, w_kv_up, w_gate_up, b_gate, consts, out):
    ctx = ExitStack()
    with ctx:
        def sb(name, shape, dt=F32, stack=ctx):
            return stack.enter_context(nc.sbuf_tensor(name, shape, dt))

        per_layer, ahead = {}, {}

        def sem(name, times, before=0):
            made = ctx.enter_context(nc.semaphore(name))
            per_layer[made], ahead[made] = times, before
            return made

        def counter(layer):
            def due(semaphore, n):
                return layer * per_layer[semaphore] + n + ahead[semaphore]
            return due

        ps = ctx.enter_context(nc.psum_tensor("ps", [P, 8, 512], F32))

        x = sb("x", [P, DT, SEQ])
        with ExitStack() as linear:
            sb("xH_head", [P, 1, SEQ], F32, linear)
            states = sb("states", [P, 2, NCHUNK - 1, GV], F32, linear)
            sb("xL_head", [P, 2, SEQ], F32, linear)
            qx = sb("qx", [P, 3, 2, GH, P], F32, linear)
        s_gla, s_ret = states[:, 0], states[:, 1]
        xH = sb("xH", [P, DT, SEQ], F32R)
        xL = sb("xL", [P, DT, SEQ], F32R)
        raw = sb("raw", [P, 2, 2 * SLAB])
        WH = sb("WH", [P, 2, 2 * SLAB], F32R)
        WL = sb("WL", [P, 2, 2 * SLAB], F32R)
        rstd_x = sb("rstd_x", [P, SEQ])
        f_first = sb("f_first", [P, SEQ])
        gate3 = sb("gate3", [P, SEQ])
        gate = sb("gate", [P, SEQ])
        up = sb("up", [P, SEQ])
        xg = [gate, up]
        sq = sb("sq", [P, 2, SEQ])
        acc = sb("acc", [P, SEQ])
        ident = sb("ident", [P, P])
        ones = sb("ones", [P, 1])
        ones_row = sb("ones_row", [P, P])
        gains_all = sb("gains_all", [P, DEPTH + 1, GAINS])
        gains = sb("gains", [P, GAINS])
        first_gains = sb("first_gains", [P, DT])
        mean = sb("mean", [P, 32])
        rstd = sb("rstd", [P, 32])
        minus_half = sb("minus_half", [P, 32])
        rx_col = sb("rx_col", [P, BLK])
        b_last = sb("b_last", [P, NCHUNK])
        top = sb("top", [P, 4])
        minus_top = sb("minus_top", [P, 4])
        total = sb("total", [P, 4])
        share = sb("share", [P, 4])

        with ExitStack() as hidden:
            hH = sb("hH", [P, FT, SEQ], F32R, hidden)
            hL = sb("hL", [P, FT, SEQ], F32R, hidden)
        mq = sb("mq", [P, 2, SEQ])
        ckv = sb("ckv", [P, SEQ])
        krgg = sb("krgg", [P, SEQ])
        heads = sb("heads", [P, 4, SEQ])
        gq, gk, rq, rk = (heads[:, t, :] for t in range(4))
        v_tok = sb("v_tok", [P, BLK, 2 * GV])
        gates = [gate, up, f_first, gate3]
        cos = sb("cos", [P, SEQ])
        sin = sb("sin", [P, SEQ])
        wq = sb("wq", [P, 2, HEADS * P])
        wkv = sb("wkv", [P, HEADS * (NOPE + DV)])
        wgu = sb("wgu", [P, GH * DK])
        bias = sb("bias", [P, GH * DK])
        const = sb("const", [P, CONSTS])
        zg = sb("zg", [P, SEQ])
        eb = sb("eb", [P, SEQ])
        enb = sb("enb", [P, SEQ])
        kf = sb("kf", [P, SEQ])
        kb = sb("kb", [P, SEQ])
        ks_ret = sb("ks_ret", [P, SEQ])
        kt_gla = sb("kt_gla", [P, BLK, P])
        kt_ret = sb("kt_ret", [P, BLK, P])
        attn_g = sb("attn_g", [P, GH, P])
        attn_r = sb("attn_r", [P, GH, P])
        qT = sb("qT", [P, 2, SEQ])
        kT = sb("kT", [P, 2, SEQ])
        v_mla = sb("v_mla", [P, BLK, HEADS * DV])
        prob = sb("prob", [P, 3, SEQ])
        probT = sb("probT", [P, 2, SEQ])

        tri = const[:, C_TRI:C_TRI + P]
        rot = const[:, C_ROT:C_ROT + P]
        decay = const[:, C_DEC:C_DEC + GH * P].rearrange("p (h i) -> p h i", h=GH)
        low = const[:, C_LOW:C_LOW + CHUNK].bitcast(I32)
        q_dec = const[:, C_QDEC:C_QDEC + CHUNK]
        k_dec = const[:, C_KDEC:C_KDEC + CHUNK]
        chunk_dec = const[:, C_CDEC:C_CDEC + 1]
        sign = const[:, C_SIGN:C_SIGN + 1]
        twice = const[:, C_TWICE:C_TWICE + 2 * ROPE]
        head_sel = const[:, C_HSEL:C_HSEL + 2]
        inv_freq = const[:, C_INV:C_INV + 1]

        landed = [sem(f"pair_landed{i}", 16 * PAIRS // 2) for i in range(2)]
        wH_ready = sem("wH_ready", PAIRS)
        wL_ready = sem("wL_ready", PAIRS)
        pair_done = sem("pair_done", PAIRS, 2)
        gains_landed = sem("gains_landed", 0)
        ident_landed = sem("ident_landed", 0)
        x_landed = [sem(f"x_landed{i}", 0) for i in range(4)]
        start_ready = sem("start_ready", 0)
        x_ready = sem("x_ready", 3 * DT, DT)
        gains_ready = sem("gains_ready", 1, 1)
        first_gains_ready = sem("first_gains_ready", 1, 1)
        xH_ready = sem("xH_ready", 3 * DT)
        xL0_ready = sem("xL0_ready", 3)
        xL_ready = sem("xL_ready", 3 * (DT - 1))
        sq_ready = sem("sq_ready", 6 * DT)
        sq_used = sem("sq_used", 3 * SQUARES)
        f_first_kept = sem("f_first_kept", 3)
        f_ready = sem("f_ready", 3 * (DT - 1))
        f_normed = sem("f_normed", 3 * DT, DT)
        rstd_kept = sem("rstd_kept", 3, 1)
        col_ready = sem("col_ready", NORMS)
        mean_ready = sem("mean_ready", NORMS)
        rstd_ready = sem("rstd_ready", NORMS)
        spread_ready = sem("spread_ready", NORMS)
        o_spread = sem("o_spread", 3)
        spread_kept = sem("spread_kept", 3)
        gu_scaled = sem("gu_scaled", 2 * FT)
        silu_ready = sem("silu_ready", 2 * FT)
        h_ready = sem("h_ready", 2 * FT)
        hH_ready = sem("hH_ready", 2 * FT)
        hL_ready = sem("hL_ready", 2 * FT)
        dve_step = sem("dve_step", DVE_STEPS)
        act_step = sem("act_step", ACT_STEPS)
        out_stored = sem("out_stored", 0)
        pool_passed = sem("pool_passed", 0)
        dve_passed = sem("dve_passed", 0)
        mix_landed = sem("mix_landed", 16 * 7)
        in_kept = sem("in_kept", 12)
        v_kept = sem("v_kept", 2)
        gate_silu = sem("gate_silu", 4)
        angle_ready = sem("angle_ready", 1)
        sine_ready = sem("sine_ready", 2)
        rope_ready = sem("rope_ready", 1)
        latent_sq = sem("latent_sq", 3)
        latent_ready = sem("latent_ready", 3)
        z_ready = sem("z_ready", 1)
        soft_ready = sem("soft_ready", 1)
        log_ready = sem("log_ready", 1)
        cum_ready = sem("cum_ready", 1)
        b_last_ready = sem("b_last_ready", 1)
        exp_ready = sem("exp_ready", 3)
        k_ready = sem("k_ready", 3)
        rot_ready = sem("rot_ready", 3)
        ret_ready = sem("ret_ready", 1)
        kpe_ready = sem("kpe_ready", 1)
        kt_psum = sem("kt_psum", 2)
        kt_kept = sem("kt_kept", 2)
        ds_ready = sem("ds_ready", BLK)
        state_ready = sem("state_ready", BLK)
        cleared = sem("cleared", 1)
        qg_ready = sem("qg_ready", BLK)
        qr_ready = sem("qr_ready", BLK)
        gated_scored = sem("gated_scored", BLK)
        ret_scored = sem("ret_scored", BLK)
        low_kept = sem("low_kept", BLK)
        up_kept = sem("up_kept", BLK)
        gr_ready = sem("gr_ready", BLK)
        gr_used = sem("gr_used", BLK)
        o_kept = sem("o_kept", BLK)
        o_sq = sem("o_sq", 4)
        o_sq_used = sem("o_sq_used", 3)
        o_gated = sem("o_gated", 4)
        gatedH_ready = sem("gatedH_ready", 4)
        gatedL_ready = sem("gatedL_ready", 4)
        headsH_ready = sem("headsH_ready", HEADS // 2)
        headsL_ready = sem("headsL_ready", HEADS // 2)
        vm_psum = sem("vm_psum", BLK)
        vm_kept = sem("vm_kept", BLK)
        q_psum = sem("q_psum", HEADS)
        q_kept = sem("q_kept", HEADS)
        q_ready = sem("q_ready", HEADS)
        k_psum = sem("k_psum", HEADS)
        k_kept = sem("k_kept", HEADS)
        kpe_psum = sem("kpe_psum", 1)
        kpe_copied = sem("kpe_copied", 2)
        scored = sem("scored", HEADS * BLK)
        top_ready = sem("top_ready", HEADS * BLK)
        exped = sem("exped", HEADS * BLK)
        prob_ready = sem("prob_ready", HEADS * BLK)
        turned = sem("turned", HEADS * BLK)
        turn_kept = sem("turn_kept", HEADS * BLK)
        valued = sem("valued", HEADS * BLK)

        block = ctx.enter_context(nc.Block())

        @block.sync
        def _(sp):
            sp.dma_start(raw[:, 0, :], stream[0]).then_inc(landed[0], 16)
            sp.dma_start(gains_all[:], gains_in.rearrange("l p g -> p l g")).then_inc(gains_landed, 16)
            for c in range(4):
                sp.dma_start(x[:, 2 * c:2 * c + 2, :], x_in[:, 2 * c:2 * c + 2, :]).then_inc(x_landed[c], 16)
            sp.dma_start(raw[:, 1, :], stream[1]).then_inc(landed[1], 16)
            sp.dma_start(ident[:], consts[:, C_ID:C_ID + P]).then_inc(ident_landed, 16)
            for c in range(4):
                sp.wait_ge(x_landed[c], 16)
                sp.sem_inc(x_ready, 2)
            with sp.Fori(1, DEPTH * PAIRS // 2) as m:
                for slot in range(2):
                    sp.wait_ge(wH_ready, 2 * m + (slot - 1))
                    sp.wait_ge(wL_ready, 2 * m + (slot - 1))
                    sp.dma_start(raw[:, slot, :], stream[2 * m + slot]).then_inc(landed[slot], 16)
            sp.wait_ge(wH_ready, DEPTH * PAIRS - 1)
            sp.wait_ge(wL_ready, DEPTH * PAIRS - 1)
            sp.dma_start(raw[:, 0, :], stream[0]).then_inc(landed[0], 16)
            for n, k in enumerate(X_ORDER):
                sp.wait_ge(x_ready, ahead[x_ready] + DEPTH * per_layer[x_ready] - DT + n + 1)
                sp.dma_start(out[:, k, :], x[:, k, :]).then_inc(out_stored, 16)
            sp.wait_ge(out_stored, 16 * DT)

        @block.tensor
        def _(pe):
            mm = nc.tensor.matmul
            pe.sem_inc(pair_done, 2)
            pe.sem_inc(rstd_kept, 1)
            pe.sem_inc(f_normed, DT)
            pe.wait_ge(start_ready, 1)
            pe.wait_ge(ident_landed, 16)

            def three(dst, wh, wl, xh, xl, start, stop):
                mm(dst, wh, xh, start=start, stop=False)
                mm(dst, wh, xl, start=False, stop=False)
                return mm(dst, wl, xh, start=False, stop=stop)

            with pe.Fori(0, DEPTH) as layer:
                due = counter(layer)

                def first_pair(p, slot, banks, stage):
                    pe.wait_ge(wH_ready, due(wH_ready, p + 1))
                    pe.wait_ge(wL_ready, due(wL_ready, p + 1))
                    for n, k in enumerate(X_ORDER):
                        pe.wait_ge(xH_ready, due(xH_ready, DT * stage + n + 1))
                        for j in range(2):
                            if n == 0 and j == 0:
                                pe.wait_ge(rstd_kept, due(rstd_kept, stage))
                            elif n == 0:
                                pe.wait_ge(f_normed, due(f_normed, DT * (stage - 1) + 2))
                            at = j * SLAB + k * P
                            mm(ps[:, banks[j], :], WH[:, slot, at:at + P], xH[:, k, :], start=n == 0, stop=False)
                            mm(ps[:, banks[j], :], WL[:, slot, at:at + P], xH[:, k, :], start=False, stop=False)
                        if n == 0:
                            pe.wait_ge(xL0_ready, due(xL0_ready, stage + 1))
                        else:
                            pe.wait_ge(xL_ready, due(xL_ready, (DT - 1) * stage + n))
                        for j in range(2):
                            at = j * SLAB + k * P
                            last = mm(ps[:, banks[j], :], WH[:, slot, at:at + P], xL[:, k, :],
                                      start=False, stop=n == DT - 1)
                    last.then_inc(pair_done, 1)

                def tiles_pair(p, slot, banks, widths=(P, P), spread_norm=None):
                    pe.wait_ge(wH_ready, due(wH_ready, p + 1))
                    pe.wait_ge(wL_ready, due(wL_ready, p + 1))
                    for n, k in enumerate(X_ORDER):
                        if n == DT // 2 and spread_norm is not None:
                            spread(spread_norm, 6)
                        for j in range(2):
                            at = j * SLAB + k * P
                            last = three(ps[0:widths[j], banks[j], :], WH[:, slot, at:at + widths[j]],
                                         WL[:, slot, at:at + widths[j]], xH[:, k, :], xL[:, k, :],
                                         n == 0, n == DT - 1)
                    last.then_inc(pair_done, 1)

                def columns(bank, squares):
                    pe.wait_ge(sq_used, due(sq_used, squares))
                    for c in range(BLK):
                        last = mm(ps[:, bank, c:c + 1], acc[:, c * P:(c + 1) * P], ones[:], start=True, stop=True)
                    last.then_inc(col_ready, 1)

                def spread(norm, bank):
                    pe.wait_ge(rstd_ready, due(rstd_ready, norm + 1))
                    for c in range(BLK):
                        last = mm(ps[:, bank, c * P:(c + 1) * P], rstd[:, c:c + 1].broadcast_to([P, P]), ident[:],
                                  start=True, stop=True)
                    last.then_inc(spread_ready, 1)

                def down_tile(p, slot, d, moving, first, last_pair):
                    for j in range(2):
                        at = j * SLAB + d * P
                        h, l = moving[j]
                        last = three(ps[:, d, :], WH[:, slot, at:at + P], WL[:, slot, at:at + P], h, l,
                                     first and j == 0, last_pair and j == 1)
                    if last_pair and d != F_ORDER[-1]:
                        last.then_inc(f_ready, 1)
                    return last

                def down_pair(p, slot, moving, first, last_pair, order=F_ORDER, scaled=None):
                    pe.wait_ge(wH_ready, due(wH_ready, p + 1))
                    pe.wait_ge(wL_ready, due(wL_ready, p + 1))
                    for d in order:
                        if scaled is not None and d == 0:
                            pe.wait_ge(gu_scaled, due(gu_scaled, scaled))
                        last = down_tile(p, slot, d, moving, first, last_pair)
                    last.then_inc(pair_done, 1)

                def ffn(stage, f_stage, base, norm):
                    slot = base % 2
                    first_pair(base, slot, (0, 1), stage)
                    tiles_pair(base + 1, 1 - slot, (2, 3))
                    columns(6, SQUARES * stage + DT)
                    tiles_pair(base + 2, slot, (4, 5), spread_norm=norm)
                    with pe.Fori(1, FT // 2 - 1) as i:
                        for j in range(2):
                            pe.wait_ge(gu_scaled, due(gu_scaled, FT * f_stage + 2 * i + j))
                            tiles_pair(base + 2 * i + 1 + j, (slot + 1 + j) % 2, (2 * j, 2 * j + 1))
                    pe.wait_ge(gu_scaled, due(gu_scaled, FT * (f_stage + 1) - 2))
                    tiles_pair(base + FT - 1, 1 - slot, (0, 1))
                    pe.wait_ge(spread_kept, due(spread_kept, stage + 1))

                    def hidden(j, f):
                        pe.wait_ge(hH_ready, due(hH_ready, FT * f_stage + f + 2))
                        pe.wait_ge(hL_ready, due(hL_ready, FT * f_stage + f + 2))
                        return [(hH[:, f + a, :], hL[:, f + a, :]) for a in range(2)]

                    for j in range(2):
                        down_pair(base + FT + j, (slot + j) % 2, hidden(j, 2 * j), j == 0, False,
                                  order=FFN_START if j == 0 else F_ORDER,
                                  scaled=FT * (f_stage + 1) if j == 0 else None)
                    with pe.Fori(1, FT // 4) as m:
                        for j in range(2):
                            down_pair(base + FT + 2 * m + j, (slot + j) % 2, hidden(j, 4 * m + 2 * j), False, False)
                    down_pair(base + FT + FT // 2 - 1, slot, hidden(0, FT - 2), False, True)
                    after(stage, norm + 1)

                def after(stage, norm):
                    pe.wait_ge(f_first_kept, due(f_first_kept, stage + 1))
                    pe.wait_ge(sq_used, due(sq_used, SQUARES * (stage + 1)))
                    for c in range(BLK):
                        mm(ps[:, 0, c:c + 1], acc[:, c * P:(c + 1) * P], ones[:], start=c == 0, stop=False,
                           skip_group_check=True)
                    pe.wait_ge(sq_ready, due(sq_ready, 2 * DT * (stage + 1)))
                    for c in range(BLK):
                        last = mm(ps[:, 0, c:c + 1], sq[:, 1, c * P:(c + 1) * P], ones[:], start=False, stop=True,
                                  skip_group_check=True)
                    last.then_inc(col_ready, 1)
                    spread(norm, 0)

                def mixer(base, norm):
                    stage = 1
                    slot = base % 2

                    def pair(i, banks, **kw):
                        tiles_pair(base + i, (slot + i) % 2, banks, **kw)

                    def values_pair(i, banks):
                        s = (slot + i) % 2
                        pe.wait_ge(wH_ready, due(wH_ready, base + i + 1))
                        pe.wait_ge(wL_ready, due(wL_ready, base + i + 1))
                        for b in range(BLK):
                            dst = ps[:, banks[b // 2], (b % 2) * GV:(b % 2 + 1) * GV]
                            for k in range(DT):
                                at, tok = k * GV, slice(b * P, (b + 1) * P)
                                mm(dst, xH[:, k, tok], WH[:, s, at:at + GV], start=k == 0, stop=False)
                                mm(dst, xH[:, k, tok], WL[:, s, at:at + GV], start=False, stop=False)
                                last = mm(dst, xL[:, k, tok], WH[:, s, at:at + GV], start=False, stop=k == DT - 1)
                        last.then_inc(pair_done, 1)

                    first_pair(base, slot, (0, 1), stage)
                    pair(1, (2, 3), widths=(P, QK + GATE_RANK))
                    columns(6, SQUARES * stage + DT)
                    pair(2, (4, 5), spread_norm=norm)
                    pe.wait_ge(in_kept, due(in_kept, 2))
                    pair(3, (0, 1))
                    pe.wait_ge(in_kept, due(in_kept, 4))
                    pe.wait_ge(mix_landed, due(mix_landed, 16 * 7))
                    pe.wait_ge(spread_kept, due(spread_kept, 2))
                    for b in range(BLK):
                        dst = ps[:, 7, b * P:(b + 1) * P]
                        mm(dst, krgg[QK:QK + GATE_RANK, b * P:(b + 1) * P], wgu[QK:QK + GATE_RANK, :], start=True, stop=False)
                        last = mm(dst, ones_row[QK:QK + 1, :], bias[QK:QK + 1, :], start=False, stop=True)
                    last.then_inc(z_ready, 1)
                    values_pair(4, (2, 3))
                    pe.wait_ge(latent_sq, due(latent_sq, 3))
                    for c in range(BLK):
                        tok = slice(c * P, (c + 1) * P)
                        mm(ps[:, 6, c:c + 1], sq[:, 0, tok], ones[:], start=True, stop=False)
                        mm(ps[:, 6, c:c + 1], sq[:, 1, tok], ones[:], start=False, stop=True)
                        last = mm(ps[:, 6, 4 + c:5 + c], acc[:, tok], ones[:], start=True, stop=True)
                    last.then_inc(col_ready, 1)
                    pe.wait_ge(in_kept, due(in_kept, 6))
                    values_pair(5, (4, 5))
                    pe.wait_ge(log_ready, due(log_ready, 1))
                    for b in range(BLK):
                        last = mm(ps[:, 7, b * P:(b + 1) * P], zg[:, b * P:(b + 1) * P], tri, start=True, stop=True)
                    last.then_inc(cum_ready, 1)
                    pe.wait_ge(in_kept, due(in_kept, 8))
                    pair(6, (0, 1))
                    pe.wait_ge(v_kept, due(v_kept, 2))
                    pe.wait_ge(rstd_ready, due(rstd_ready, norm + 2))
                    for c in range(BLK):
                        tok = slice(c * P, (c + 1) * P)
                        mm(ps[:, 6, tok], rstd[:, c:c + 1].broadcast_to([P, P]), ident[:], start=True, stop=True)
                        last = mm(ps[:, 4, tok], rstd[:, 4 + c:5 + c].broadcast_to([P, P]), ident[:], start=True, stop=True)
                    last.then_inc(spread_ready, 1)
                    mm(ps[:, 5, :], rot, rq[:], start=True, stop=True).then_inc(rot_ready, 1)
                    pe.wait_ge(exp_ready, due(exp_ready, 3))
                    mm(ps[:, 7, :], rot, rk[:], start=True, stop=True).then_inc(rot_ready, 1)
                    pair(7, (2, 3))
                    pe.wait_ge(in_kept, due(in_kept, 10))
                    mm(ps[0:QK, 1, :], rot[NOPE:QK, 0:QK], krgg[NOPE:QK, :], start=True, stop=True).then_inc(rot_ready, 1)
                    pe.wait_ge(k_ready, due(k_ready, 3))
                    pe.wait_ge(latent_ready, due(latent_ready, 3))
                    for b in range(BLK):
                        last = nc.tensor.transpose(ps[:, 6, b * P:(b + 1) * P], zg[:, b * P:(b + 1) * P], ident[:])
                    last.then_inc(kt_psum, 1)
                    pe.wait_ge(ret_ready, due(ret_ready, 1))
                    for b in range(BLK):
                        last = nc.tensor.transpose(ps[:, 7, b * P:(b + 1) * P], ks_ret[:, b * P:(b + 1) * P], ident[:])
                    last.then_inc(kt_psum, 1)

                    def make_values(b):
                        mm(ps[:, RING[b], :], ckv[:, b * P:(b + 1) * P],
                           wkv[:].rearrange("p (h c) -> p h c", h=HEADS)[:, :, NOPE:NOPE + DV],
                           start=True, stop=True).then_inc(vm_psum, 1)

                    def make_q(h):
                        if h >= 1:
                            pe.wait_ge(k_kept, due(k_kept, h))
                        for k in range(2):
                            last = mm(ps[:, QK_BANK, :], wq[:, k, h * P:(h + 1) * P], mq[:, k, :],
                                      start=k == 0, stop=k == 1)
                        last.then_inc(q_psum, 1)

                    def make_k(h):
                        pe.wait_ge(q_kept, due(q_kept, h + 1))
                        pe.wait_ge(q_ready, due(q_ready, h + 1))
                        at = h * (NOPE + DV)
                        mm(ps[0:NOPE, QK_BANK, :], wkv[:, at:at + NOPE], ckv[:], start=True, stop=True).then_inc(k_psum, 1)

                    def state_parts(b):
                        if b:
                            pe.wait_ge(state_ready, due(state_ready, b))
                        for c in range(2 if b < BLK - 1 else 1):
                            rows = slice(c * CHUNK, (c + 1) * CHUNK)
                            mm(ps[:, LIN_BANKS[c], 0:GV], kt_gla[rows, b, :], v_tok[rows, b, 0:GV], start=True, stop=True)
                            last = mm(ps[:, LIN_BANKS[c], GV:2 * GV], kt_ret[rows, b, :], v_tok[rows, b, GV:2 * GV],
                                      start=True, stop=True)
                        last.then_inc(ds_ready, 1)

                    def gated_scores(b):
                        tok = slice(b * P, (b + 1) * P)
                        pe.wait_ge(qg_ready, due(qg_ready, b + 1))
                        if b:
                            pe.wait_ge(gr_ready, due(gr_ready, b))
                            pe.wait_ge(o_kept, due(o_kept, b))
                        else:
                            pe.wait_ge(state_ready, due(state_ready, BLK))
                        mm(ps[:, LIN_BANKS[0], :], kf[:, tok], qx[:, 0, b % 2].rearrange("p h i -> p (h i)"), start=True, stop=True)
                        mm(ps[:, LIN_BANKS[1], :], kb[:, tok], qx[:, 1, b % 2].rearrange("p h i -> p (h i)"), start=True,
                           stop=True).then_inc(gated_scored, 1)

                    def retention_scores(b):
                        tok = slice(b * P, (b + 1) * P)
                        pe.wait_ge(qr_ready, due(qr_ready, b + 1))
                        pe.wait_ge(low_kept, due(low_kept, b + 1))
                        mm(ps[:, LIN_BANKS[0], :], rk[:, tok], qx[:, 2, b % 2].rearrange("p h i -> p (h i)"), start=True,
                           stop=True).then_inc(ret_scored, 1)

                    def linear_values(b):
                        pe.wait_ge(gr_ready, due(gr_ready, b + 1))
                        for kind, (attn, state) in enumerate(((attn_g, s_gla), (attn_r, s_ret))):
                            for h in range(GH):
                                rows = slice(DV * (h % 2), DV * (h % 2 + 1))
                                at = (2 * kind + h // 2) * P
                                vcol = slice(kind * GV + h * DV, kind * GV + (h + 1) * DV)
                                last = mm(ps[rows, LIN_BANKS[1], at:at + P], v_tok[:, b, vcol], attn[:, h, :],
                                          start=True, stop=False)
                                for c in range(2):
                                    n = 2 * b + c
                                    if n == 0:
                                        continue
                                    last = mm(ps[rows, LIN_BANKS[1], at + c * CHUNK:at + (c + 1) * CHUNK],
                                              state[:, n - 1, h * DV:(h + 1) * DV],
                                              qx[:, 2 * kind, b % 2, h, c * CHUNK:(c + 1) * CHUNK],
                                              start=False, stop=c == 1)
                        last.then_inc(gr_used, 1)

                    def linear_squares(t):
                        pe.wait_ge(o_sq, due(o_sq, t + 1))
                        for c in range(BLK):
                            last = mm(ps[:, LIN_BANKS[0], t * 8 + 2 * c:t * 8 + 2 * c + 2], sq[:, t % 2, c * P:(c + 1) * P],
                                      head_sel, start=True, stop=True)
                        last.then_inc(o_sq_used if t < 3 else col_ready, 1)

                    def linear_spread(t):
                        if t == 0:
                            pe.wait_ge(rstd_ready, due(rstd_ready, norm + 3))
                        if t >= 2:
                            pe.wait_ge(o_gated, due(o_gated, t - 1))
                        for c in range(BLK):
                            for h in range(2):
                                at = t * 8 + 2 * c + h
                                last = mm(ps[h * DV:(h + 1) * DV, LIN_BANKS[t % 2], c * P:(c + 1) * P],
                                          rstd[:, at:at + 1].broadcast_to([P, DV]), ident[:], start=True, stop=True)
                        last.then_inc(o_spread if t < 3 else spread_ready, 1)

                    def linear(n):
                        if n < LIN_STEP:
                            state_parts(n + 1)
                        elif n < NORM_STEP:
                            b = (n - LIN_STEP) // 3
                            (gated_scores, retention_scores, linear_values)[(n - LIN_STEP) % 3](b)
                        elif NORM_STEP < n <= NORM_STEP + 2:
                            for t in range(2):
                                linear_squares(2 * (n - NORM_STEP - 1) + t)
                        elif GATE_STEP <= n < GATE_STEP + 4:
                            linear_spread(n - GATE_STEP)

                    def scores(m):
                        h, b = divmod(m, BLK)
                        if b == 0:
                            pe.wait_ge(q_ready, due(q_ready, h + 1))
                            pe.wait_ge(k_kept, due(k_kept, h + 1))
                        if m < BLK:
                            pe.wait_ge(vm_kept, due(vm_kept, m + 1))
                        mm(ps[:, RING[m % 4], 0:(b + 1) * P], qT[:, h % 2, b * P:(b + 1) * P],
                           kT[:, h % 2, 0:(b + 1) * P], start=True, stop=True).then_inc(scored, 1)

                    def turn(m):
                        pe.wait_ge(prob_ready, due(prob_ready, m + 1))
                        for kk in range(m % BLK + 1):
                            last = nc.tensor.transpose(ps[:, RING[m % 4], kk * P:(kk + 1) * P],
                                                       prob[:, m % 3, kk * P:(kk + 1) * P], ident[:])
                        last.then_inc(turned, 1)

                    def values(m):
                        h, b = divmod(m, BLK)
                        pe.wait_ge(turn_kept, due(turn_kept, m + 1))
                        if b == 0 and h % 2 == 0 and h:
                            pe.wait_ge(headsL_ready, due(headsL_ready, h // 2))
                        rows = slice(DV * (h % 2), DV * (h % 2 + 1))
                        for kk in range(b + 1):
                            last = mm(ps[rows, OUT_BANK, b * P:(b + 1) * P], v_mla[:, kk, h * DV:(h + 1) * DV],
                                      probT[:, m % 2, kk * P:(kk + 1) * P], start=kk == 0, stop=kk == b)
                        last.then_inc(valued, 1)

                    def mixed(i):
                        return [(xH[:, 2 * i + a, :], xL[:, 2 * i + a, :]) for a in range(2)]

                    pe.wait_ge(in_kept, due(in_kept, 12))
                    for b in range(BLK):
                        make_values(b)
                    make_q(0)
                    pe.wait_ge(kpe_ready, due(kpe_ready, 1))
                    mm(ps[NOPE:P, LIN_BANKS[0], :], twice[NOPE:QK, :], krgg[NOPE:QK, :], start=True,
                       stop=True).then_inc(kpe_psum, 1)
                    make_k(0)
                    pe.wait_ge(kt_kept, due(kt_kept, 2))
                    pe.wait_ge(kpe_copied, due(kpe_copied, 2))
                    state_parts(0)
                    make_q(1)
                    make_k(1)
                    for m in range(AHEAD):
                        scores(m)
                    for n in range(STEPS):
                        h, b = divmod(n, BLK)
                        turn(n)
                        if n:
                            values(n - 1)
                        if h + 2 < HEADS and b == 1:
                            make_q(h + 2)
                        if h + 2 < HEADS and b == 2:
                            make_k(h + 2)
                        linear(n)
                        if n + AHEAD < STEPS:
                            scores(n + AHEAD)
                        else:
                            if n + AHEAD == STEPS:
                                pe.wait_ge(gatedL_ready, due(gatedL_ready, 4))
                                pe.wait_ge(headsL_ready, due(headsL_ready, 1))
                                pe.wait_ge(wH_ready, due(wH_ready, base + IN_PAIRS + 1))
                                pe.wait_ge(wL_ready, due(wL_ready, base + IN_PAIRS + 1))
                            down_tile(base + IN_PAIRS, slot, MIX_START[n + AHEAD - STEPS], mixed(0), True, False)
                    values(STEPS - 1)
                    for d in MIX_REST:
                        if d == OUT_BANK:
                            pe.wait_ge(headsL_ready, due(headsL_ready, HEADS // 2))
                        last = down_tile(base + IN_PAIRS, slot, d, mixed(0), True, False)
                    last.then_inc(pair_done, 1)
                    for i in range(1, OUT_PAIRS):
                        down_pair(base + IN_PAIRS + i, (slot + i) % 2, mixed(i), False, i == OUT_PAIRS - 1)
                    after(stage, norm + 3)

                ffn(0, 0, 0, 0)
                mixer(FFN_PAIRS, 2)
                ffn(2, 1, FFN_PAIRS + MIX_PAIRS, 6)

        @block.scalar
        def _(act):
            af = nc.scalar.activation
            steps = [0]
            act.wait_ge(landed[0], 16)
            af(WH[:, 0, :], raw[:, 0, :], ACT.Copy).then_inc(wH_ready, 1)
            act.wait_ge(first_gains_ready, 1)
            act.wait_ge(x_ready, 1)
            af(xH[:, 0, :], x[:, 0, :], ACT.Copy, scale=first_gains[:, 0:1]).then_inc(xH_ready, 1)
            with act.Fori(0, DEPTH) as layer:
                due = counter(layer)
                steps[0] = 0

                def link(instruction):
                    steps[0] += 1
                    instruction.then_inc(act_step, 1)
                    act.wait_ge(act_step, due(act_step, steps[0]))


                def high(p, m, slot):
                    act.wait_ge(landed[slot], due(landed[slot], 16 * (m + 1)))
                    act.wait_ge(pair_done, due(pair_done, p - 1))
                    af(WH[:, slot, :], raw[:, slot, :], ACT.Copy).then_inc(wH_ready, 1)

                def high_at(p):
                    high(p, p // 2, p % 2)

                def split_x(stage, p):
                    for n, k in enumerate(X_ORDER):
                        if stage == 0 and n == 0:
                            continue
                        act.wait_ge(x_ready, due(x_ready, DT * stage + n + 1 - DT))
                        g = first_gains[:, k:k + 1] if stage == 0 else gains[:, G_PRE[stage] + k:G_PRE[stage] + k + 1]
                        last = af(xH[:, k, :], x[:, k, :], ACT.Copy, scale=g)
                        if n:
                            if n >= 3:
                                act.wait_ge(xL_ready, due(xL_ready, (DT - 1) * stage + n - 2))
                            last = af(xg[n % 2][:], x[:, k, :], ACT.Copy, scale=g)
                        last.then_inc(xH_ready, 1)
                    high_at(p)
                    for n, k in enumerate(X_ORDER):
                        square(n, SQUARES * stage, x[:, k, :])

                def square(n, used, src):
                    if n >= 2:
                        act.wait_ge(sq_used, due(sq_used, used + n - 1))
                    af(sq[:, n % 2, :], src, ACT.Square).then_inc(sq_ready, 1)

                def keep_spread(stage, norm):
                    act.wait_ge(spread_ready, due(spread_ready, norm + 1))
                    af(rstd_x[:], ps[:, 6, :], ACT.Copy).then_inc(spread_kept, 1)

                def hidden(n, f):
                    act.wait_ge(gu_scaled, due(gu_scaled, n + 1))
                    af(gate[:], gate[:], ACT.Silu).then_inc(silu_ready, 1)
                    act.wait_ge(h_ready, due(h_ready, n + 1))
                    af(hH[:, f, :], up[:], ACT.Copy).then_inc(hH_ready, 1)

                def after(stage, p):
                    for n, d in enumerate(F_ORDER):
                        if n < DT - 1:
                            act.wait_ge(f_ready, due(f_ready, (DT - 1) * stage + n + 1))
                        else:
                            act.wait_ge(pair_done, due(pair_done, p + 1))
                        square(n, SQUARES * stage + DT, ps[:, d, :])

                def ffn(stage, f_stage, base, norm):
                    n0 = FT * f_stage
                    if stage == 0:
                        act.wait_ge(first_gains_ready, due(first_gains_ready, 0))
                    split_x(stage, base + 1)
                    high_at(base + 2)
                    high_at(base + 3)
                    keep_spread(stage, norm)
                    hidden(n0, 0)
                    hidden(n0 + 1, 1)
                    high_at(base + 4)
                    hidden(n0 + 2, 2)
                    with act.Fori(1, FT // 2 - 1) as i:
                        for j in range(2):
                            f = 2 * i + 1 + j
                            high(base + 2 + f, (base + 3 + j) // 2 + i, (base + 3 + j) % 2)
                            hidden(n0 + f, f)
                    high_at(base + FT + 1)
                    hidden(n0 + FT - 1, FT - 1)
                    with act.Fori(1, FT // 4) as m:
                        for j in range(2):
                            high(base + FT + 2 * m + j, (base + FT + j) // 2 + m, (base + FT + j) % 2)
                    high_at(base + FT + FT // 2 - 1)
                    high_at(base + FT + FT // 2)
                    after(stage, base + FFN_PAIRS - 1)

                def mixer(base, norm):
                    split_x(1, base + 1)
                    act.dma_start(const[:], consts).then_inc(mix_landed, 16)
                    act.dma_start(wgu[QK:QK + GATE_RANK, :], w_gate_up[layer]).then_inc(mix_landed, 16)
                    act.dma_start(bias[QK:QK + 1, :], b_gate[layer]).then_inc(mix_landed, 16)
                    act.dma_start(cos[:].bitcast(I32), positions.partition_broadcast(P)).then_inc(mix_landed, 16)
                    act.dma_start(wq[:, 0, :], w_q_up[layer, 0]).then_inc(mix_landed, 16)
                    act.dma_start(wq[:, 1, :], w_q_up[layer, 1]).then_inc(mix_landed, 16)
                    act.dma_start(wkv[:], w_kv_up[layer]).then_inc(mix_landed, 16)
                    high_at(base + 2)
                    high_at(base + 3)
                    keep_spread(1, norm)
                    act.wait_ge(angle_ready, due(angle_ready, 1))
                    af(cos[:], sin[:], ACT.Sin, scale=0.5).then_inc(sine_ready, 1)
                    act.wait_ge(sine_ready, due(sine_ready, 1))
                    af(sin[:], sin[:], ACT.Sin).then_inc(sine_ready, 1)
                    act.wait_ge(in_kept, due(in_kept, 3))
                    act.wait_ge(mean_ready, due(mean_ready, norm + 1))
                    for j in range(2):
                        af(sq[:, j, :], mq[:, j, :], ACT.Square).then_inc(latent_sq, 1)
                    af(acc[:], ckv[:], ACT.Square).then_inc(latent_sq, 1)
                    high_at(base + 4)

                    def keep_values(i):
                        banks = (2, 3) if i == 0 else (4, 5)
                        act.wait_ge(pair_done, due(pair_done, base + 5 + i))
                        for b in range(BLK):
                            last = af(v_tok[:, b, i * GV:(i + 1) * GV],
                                      ps[:, banks[b // 2], (b % 2) * GV:(b % 2 + 1) * GV], ACT.Copy,
                                      scale=rx_col[:, b:b + 1])
                        last.then_inc(v_kept, 1)

                    high_at(base + 5)
                    keep_values(0)
                    act.wait_ge(z_ready, due(z_ready, 1))
                    link(af(kf[:], ps[:, 7, :], ACT.Abs))
                    link(af(kf[:], kf[:], ACT.Exp, scale=-1.0))
                    af(kf[:], kf[:], ACT.Ln, bias=1.0).then_inc(soft_ready, 1)
                    high_at(base + 6)
                    keep_values(1)
                    act.wait_ge(b_last_ready, due(b_last_ready, 1))
                    af(eb[:], ps[:, 7, :], ACT.Exp).then_inc(exp_ready, 1)
                    af(enb[:], ps[:, 7, :], ACT.Exp, scale=-1.0).then_inc(exp_ready, 1)
                    for n in range(NCHUNK):
                        tok = slice(n * CHUNK, (n + 1) * CHUNK)
                        last = af(zg[:, tok], ps[:, 7, tok], ACT.Exp, bias=b_last[:, n:n + 1], scale=-1.0)
                    last.then_inc(exp_ready, 1)
                    high_at(base + 7)
                    for t in range(4):
                        act.wait_ge(in_kept, due(in_kept, 9 + t))
                        af(gates[t][:], gates[t][:], ACT.Silu).then_inc(gate_silu, 1)
                    high_at(base + 8)
                    act.wait_ge(kt_psum, due(kt_psum, 1))
                    af(kt_gla[:].rearrange("p b f -> p (b f)"), ps[:, 6, :], ACT.Copy).then_inc(kt_kept, 1)
                    act.wait_ge(kt_psum, due(kt_psum, 2))
                    af(kt_ret[:].rearrange("p b f -> p (b f)"), ps[:, 7, :], ACT.Copy).then_inc(kt_kept, 1)

                    def keep_q(h):
                        act.wait_ge(q_psum, due(q_psum, h + 1))
                        if h >= 2:
                            act.wait_ge(scored, due(scored, (h - 1) * BLK))
                        af(qT[0:NOPE, h % 2, :], ps[0:NOPE, QK_BANK, :], ACT.Copy).then_inc(q_kept, 1)

                    def keep_k(h):
                        act.wait_ge(k_psum, due(k_psum, h + 1))
                        af(kT[0:NOPE, h % 2, :], ps[0:NOPE, QK_BANK, :], ACT.Copy).then_inc(k_kept, 1)

                    def exps(m):
                        width = (m % BLK + 1) * P
                        act.wait_ge(top_ready, due(top_ready, m + 1))
                        if m >= 3:
                            act.wait_ge(turned, due(turned, m - 2))
                        af(prob[:, m % 3, 0:width], ps[:, RING[m % 4], 0:width], ACT.Exp, scale=QK ** -0.5,
                           bias=minus_top[:, m % 4:m % 4 + 1],
                           accum_out=total[:, m % 4:m % 4 + 1]).then_inc(exped, 1)

                    def keep_turn(m):
                        width = (m % BLK + 1) * P
                        act.wait_ge(turned, due(turned, m + 1))
                        if m >= 2:
                            act.wait_ge(valued, due(valued, m - 1))
                        af(probT[:, m % 2, 0:width], ps[:, RING[m % 4], 0:width], ACT.Copy).then_inc(turn_kept, 1)

                    def keep_heads(i):
                        act.wait_ge(valued, due(valued, 2 * BLK * (i + 1)))
                        af(xH[:, i, :], ps[:, OUT_BANK, :], ACT.Copy).then_inc(headsH_ready, 1)

                    def linear(n):
                        if LIN_STEP <= n < NORM_STEP:
                            b, part = divmod(n - LIN_STEP, 3)
                            if part == 0:
                                act.wait_ge(gated_scored, due(gated_scored, b + 1))
                                if b >= 1:
                                    act.wait_ge(gr_used, due(gr_used, b))
                                up_scores = ps[:, LIN_BANKS[1], :].rearrange("p (h i) -> p h i", h=GH)
                                for c in range(2):
                                    r = slice(c * CHUNK, (c + 1) * CHUNK)
                                    last = af(attn_g[r, :, r], up_scores[r, :, r], ACT.Copy)
                                last.then_inc(up_kept, 1)
                            elif part == 2:
                                act.wait_ge(gr_used, due(gr_used, b + 1))
                                af(heads[:, :, b * P:(b + 1) * P],
                                   ps[:, LIN_BANKS[1], :].rearrange("p (t i) -> p t i", t=4), ACT.Copy).then_inc(o_kept, 1)
                        elif NORM_STEP <= n < NORM_STEP + 2:
                            if n == NORM_STEP:
                                act.wait_ge(o_kept, due(o_kept, BLK))
                            for t in range(2 * (n - NORM_STEP), 2 * (n - NORM_STEP) + 2):
                                if t >= 2:
                                    act.wait_ge(o_sq_used, due(o_sq_used, t - 1))
                                af(sq[:, t % 2, :], heads[:, t, :], ACT.Square).then_inc(o_sq, 1)
                        elif GATE_STEP < n <= GATE_STEP + 4:
                            t = n - GATE_STEP - 1
                            act.wait_ge(o_gated, due(o_gated, t + 1))
                            af(xH[:, 4 + t, :], heads[:, t, :], ACT.Copy).then_inc(gatedH_ready, 1)

                    for b in range(BLK):
                        act.wait_ge(vm_psum, due(vm_psum, b + 1))
                        af(v_mla[:, b, :], ps[:, RING[b], :], ACT.Copy).then_inc(vm_kept, 1)
                    keep_q(0)
                    act.wait_ge(kpe_psum, due(kpe_psum, 1))
                    for j in range(2):
                        af(kT[NOPE:P, j, :], ps[NOPE:P, LIN_BANKS[0], :], ACT.Copy).then_inc(kpe_copied, 1)
                    keep_k(0)
                    keep_q(1)
                    keep_k(1)
                    act.wait_ge(cleared, due(cleared, 1))
                    for m in range(AHEAD):
                        exps(m)
                    for n in range(STEPS):
                        h, b = divmod(n, BLK)
                        keep_turn(n)
                        if h % 2 == 0 and b == 0 and h:
                            keep_heads(h // 2 - 1)
                        if h + 2 < HEADS and b == 1:
                            keep_q(h + 2)
                        if h + 2 < HEADS and b == 2:
                            keep_k(h + 2)
                        linear(n)
                        if n == NORM_STEP + 2:
                            high_at(base + 9)
                        if n + AHEAD < STEPS:
                            exps(n + AHEAD)
                    keep_heads(HEADS // 2 - 1)
                    for i in range(2, OUT_PAIRS + 1):
                        high_at(base + IN_PAIRS + i)
                    after(1, base + MIX_PAIRS - 1)

                ffn(0, 0, 0, 0)
                mixer(FFN_PAIRS, 2)
                ffn(2, 1, FFN_PAIRS + MIX_PAIRS, 6)
                act.wait_ge(first_gains_ready, due(first_gains_ready, 1))
                act.wait_ge(x_ready, due(x_ready, 2 * DT + 1))
                af(xH[:, 0, :], x[:, 0, :], ACT.Copy, scale=first_gains[:, 0:1]).then_inc(xH_ready, 1)

        @block.vector
        def _(dve):
            tt, ts, stt = nc.vector.tensor_tensor, nc.vector.tensor_scalar, nc.vector.scalar_tensor_tensor
            steps = [0]
            nc.vector.memset(ones[:], 1.0)
            nc.vector.memset(ones_row[:], 1.0)
            nc.vector.memset(minus_half[:], -0.5).then_inc(start_ready, 1)
            dve.wait_ge(gains_landed, 16)
            nc.vector.tensor_copy(first_gains[:], gains_all[:, 0, G_PRE[0]:G_PRE[0] + DT]).then_inc(first_gains_ready, 1)
            nc.vector.tensor_copy(gains[:], gains_all[:, 0, :]).then_inc(gains_ready, 1)
            dve.wait_ge(wH_ready, 1)
            tt(WL[:, 0, :], raw[:, 0, :], WH[:, 0, :].bitcast(F32), ALU.subtract).then_inc(wL_ready, 1)
            dve.wait_ge(first_gains_ready, 1)
            dve.wait_ge(gains_ready, 1)
            dve.wait_ge(xH_ready, 1)
            stt(xL[:, 0, :], x[:, 0, :], first_gains[:, 0:1], xH[:, 0, :].bitcast(F32), ALU.mult,
                ALU.subtract).then_inc(xL0_ready, 1)
            with dve.Fori(0, DEPTH) as layer:
                due = counter(layer)
                steps[0] = 0

                def link(instruction):
                    steps[0] += 1
                    instruction.then_inc(dve_step, 1)
                    dve.wait_ge(dve_step, due(dve_step, steps[0]))

                def lows(p, slot):
                    dve.wait_ge(wH_ready, due(wH_ready, p + 1))
                    tt(WL[:, slot, :], raw[:, slot, :], WH[:, slot, :].bitcast(F32), ALU.subtract).then_inc(wL_ready, 1)

                def low_at(p):
                    lows(p, p % 2)

                def add_square(n, ready, used):
                    dve.wait_ge(sq_ready, due(sq_ready, ready + n + 1))
                    if n:
                        dve.wait_ge(sq_used, due(sq_used, used + n))
                        tt(acc[:], acc[:], sq[:, n % 2, :], ALU.add).then_inc(sq_used, 1)
                    else:
                        nc.vector.tensor_copy(acc[:], sq[:, 0, :]).then_inc(sq_used, 1)

                def mean_of(norm, bank, scale, eps):
                    dve.wait_ge(col_ready, due(col_ready, norm + 1))
                    ts(mean[:, 0:BLK], ps[:, bank, 0:BLK], scale, eps, ALU.mult, ALU.add).then_inc(mean_ready, 1)

                def low_first(stage):
                    dve.wait_ge(xH_ready, due(xH_ready, DT * stage + 1))
                    g = first_gains[:, 0:1] if stage == 3 else gains[:, G_PRE[stage]:G_PRE[stage] + 1]
                    stt(xL[:, 0, :], x[:, 0, :], g, xH[:, 0, :].bitcast(F32), ALU.mult,
                        ALU.subtract).then_inc(xL0_ready, 1)

                def hidden(n, f, banks, first=False):
                    if not first:
                        dve.wait_ge(hL_ready, due(hL_ready, n))
                    for j, dst in enumerate((gate, up)):
                        last = tt(dst[:], ps[:, banks[j], :], rstd_x[:], ALU.mult)
                    last.then_inc(gu_scaled, 1)
                    dve.wait_ge(silu_ready, due(silu_ready, n + 1))
                    tt(up[:], gate[:], up[:], ALU.mult).then_inc(h_ready, 1)
                    dve.wait_ge(hH_ready, due(hH_ready, n + 1))
                    tt(hL[:, f, :], up[:], hH[:, f, :].bitcast(F32), ALU.subtract).then_inc(hL_ready, 1)

                def after(stage, norm, share):
                    for n in range(DT - 1):
                        add_square(n, 2 * DT * stage + DT, SQUARES * stage + DT)
                        if n == 0:
                            nc.vector.tensor_copy(f_first[:], ps[:, 0, :]).then_inc(f_first_kept, 1)
                    mean_of(norm, 0, 1.0 / (D * share * share), EPS / (share * share))
                    dve.wait_ge(spread_ready, due(spread_ready, norm + 1))
                    normed = (acc, sq[:, 0, :])

                    def norm_tile(n):
                        k = X_ORDER[n]
                        a, b = (f_first[:], ps[:, 0, :]) if k == 0 else (ps[:, k, :], gate3[:])
                        if n >= 2:
                            dve.wait_ge(x_ready, due(x_ready, DT * stage + n - 1))
                        tt(normed[n % 2][:], a, b, ALU.mult).then_inc(f_normed, 1)

                    def to_residual(n):
                        k = X_ORDER[n]
                        g = G_POST[stage] + k
                        dve.wait_ge(f_normed, due(f_normed, DT * stage + n + 1))
                        stt(x[:, k, :], normed[n % 2][:], gains[:, g:g + 1], x[:, k, :], ALU.mult,
                            ALU.add).then_inc(x_ready, 1)

                    norm_tile(0)
                    to_residual(0)
                    nc.vector.tensor_copy(gate3[:], ps[:, 0, :]).then_inc(rstd_kept, 1)
                    dve.wait_ge(rstd_kept, due(rstd_kept, stage + 1))
                    for n in range(1, DT):
                        norm_tile(n)
                        if n == 1:
                            low_first(stage + 1)
                        if n >= 2:
                            to_residual(n - 1)
                    to_residual(DT - 1)
                    dve.wait_ge(x_ready, due(x_ready, DT * (stage + 1)))

                def ffn(stage, f_stage, base, norm):
                    n0 = FT * f_stage
                    low_at(base + 1)
                    for n in range(DT):
                        add_square(n, 2 * DT * stage, SQUARES * stage)
                    low_at(base + 2)
                    mean_of(norm, 6, 1.0 / D, EPS)
                    low_at(base + 3)
                    dve.wait_ge(spread_kept, due(spread_kept, stage + 1))
                    hidden(n0, 0, (0, 1), first=True)
                    hidden(n0 + 1, 1, (2, 3))
                    low_at(base + 4)
                    dve.wait_ge(pair_done, due(pair_done, base + 3))
                    hidden(n0 + 2, 2, (4, 5))
                    with dve.Fori(1, FT // 2 - 1) as i:
                        for j in range(2):
                            f = 2 * i + 1 + j
                            lows(base + 2 + f, (base + 3 + j) % 2)
                            dve.wait_ge(pair_done, due(pair_done, base + f + 1))
                            hidden(n0 + f, f, (2 * j, 2 * j + 1))
                    dve.wait_ge(pair_done, due(pair_done, base + FT))
                    hidden(n0 + FT - 1, FT - 1, (0, 1))
                    low_at(base + FT + 1)
                    with dve.Fori(1, FT // 4) as m:
                        for j in range(2):
                            lows(base + FT + 2 * m + j, (base + FT + j) % 2)
                    low_at(base + FT + FT // 2 - 1)
                    low_at(base + FT + FT // 2)
                    after(stage, norm + 1, 0.5)

                def mixer(base, norm):
                    low_at(base + 1)
                    for n in range(DT):
                        add_square(n, 2 * DT, SQUARES)
                    low_at(base + 2)
                    mean_of(norm, 6, 1.0 / D, EPS)
                    low_at(base + 3)

                    def keep(bank, dst, r0=0, r1=P):
                        tt(dst[r0:r1], ps[r0:r1, bank, :], rstd_x[r0:r1, :], ALU.mult).then_inc(in_kept, 1)

                    dve.wait_ge(spread_kept, due(spread_kept, 2))
                    nc.vector.tensor_copy(rx_col[:], rstd[:, 0:BLK])
                    dve.wait_ge(pair_done, due(pair_done, base + 1))
                    keep(0, mq[:, 0, :])
                    keep(1, mq[:, 1, :])
                    dve.wait_ge(pair_done, due(pair_done, base + 2))
                    keep(2, ckv)
                    keep(3, krgg, NOPE, QK + GATE_RANK)
                    dve.wait_ge(mix_landed, due(mix_landed, 16 * 7))
                    link(nc.vector.tensor_copy(sin[:], cos[:].bitcast(I32)))
                    link(ts(sin[:], sin[:], inv_freq, None, ALU.mult))
                    link(ts(cos[:], sin[:], 1.0 / TWO_PI, ROUND, ALU.mult, ALU.add))
                    link(ts(cos[:], cos[:], ROUND, None, ALU.subtract))
                    for c in (C1, C2, C3):
                        link(stt(sin[:], cos[:], -c, sin[:], ALU.mult, ALU.add))
                    ts(sin[:], sin[:], 3.1415925, -3.1415925, ALU.min, ALU.max).then_inc(angle_ready, 1)
                    dve.wait_ge(pair_done, due(pair_done, base + 3))
                    keep(4, gq)
                    keep(5, gk)
                    low_at(base + 4)
                    dve.wait_ge(sine_ready, due(sine_ready, 2))
                    link(tt(cos[:], cos[:], cos[:], ALU.mult))
                    ts(cos[:], cos[:], -2.0, 1.0, ALU.mult, ALU.add).then_inc(rope_ready, 1)
                    dve.wait_ge(pair_done, due(pair_done, base + 4))
                    keep(0, rq)
                    keep(1, rk)
                    low_at(base + 5)
                    dve.wait_ge(col_ready, due(col_ready, norm + 2))
                    ts(mean[:, 0:BLK], ps[:, 6, 0:BLK], 1.0 / QR, EPS, ALU.mult, ALU.add)
                    ts(mean[:, BLK:2 * BLK], ps[:, 6, BLK:2 * BLK], 1.0 / KVR, EPS, ALU.mult, ALU.add).then_inc(mean_ready, 1)
                    dve.wait_ge(z_ready, due(z_ready, 1))
                    dve.wait_ge(soft_ready, due(soft_ready, 1))
                    stt(zg[:], ps[:, 7, :], 0.0, kf[:], ALU.min, ALU.subtract).then_inc(log_ready, 1)
                    low_at(base + 6)
                    dve.wait_ge(cum_ready, due(cum_ready, 1))
                    nc.vector.tensor_copy(b_last[:], ps[:, 7, CHUNK - 1::CHUNK]).then_inc(b_last_ready, 1)
                    low_at(base + 7)
                    dve.wait_ge(spread_ready, due(spread_ready, norm + 2))
                    for j in range(2):
                        stt(mq[:, j, :], mq[:, j, :], gains[:, G_Q + j:G_Q + j + 1], ps[:, 6, :], ALU.mult,
                            ALU.mult).then_inc(latent_ready, 1)
                    stt(ckv[:], ckv[:], gains[:, G_KV:G_KV + 1], ps[:, 4, :], ALU.mult, ALU.mult).then_inc(latent_ready, 1)
                    dve.wait_ge(exp_ready, due(exp_ready, 3))
                    tt(kf[:], gk[:], enb[:], ALU.mult).then_inc(k_ready, 1)
                    tt(kb[:], gk[:], eb[:], ALU.mult).then_inc(k_ready, 1)
                    tt(zg[:], zg[:], gk[:], ALU.mult).then_inc(k_ready, 1)

                    def turn(i, t, bank, r0, r1):
                        dve.wait_ge(rot_ready, due(rot_ready, i + 1))
                        tmp = attn_r[:].rearrange("p h i -> p (h i)")[r0:r1, :]
                        link(tt(t[r0:r1, :], t[r0:r1, :], cos[r0:r1, :], ALU.mult))
                        link(tt(tmp, ps[r0:r1, bank, :], sin[r0:r1, :], ALU.mult))
                        return tt(t[r0:r1, :], t[r0:r1, :], tmp, ALU.add)

                    dve.wait_ge(pair_done, due(pair_done, base + 7))
                    keep(0, gates[0])
                    keep(1, gates[1])
                    dve.wait_ge(rope_ready, due(rope_ready, 1))
                    link(turn(0, rq, 5, 0, P))
                    link(turn(1, rk, 7, 0, P))
                    tt(ks_ret[:].rearrange("p (n i) -> p n i", n=NCHUNK), rk.rearrange("p (n i) -> p n i", n=NCHUNK),
                       k_dec.rearrange("p (o i) -> p o i", o=1).broadcast_to([P, NCHUNK, CHUNK]),
                       ALU.mult).then_inc(ret_ready, 1)
                    dve.wait_ge(pair_done, due(pair_done, base + 8))
                    keep(2, gates[2])
                    keep(3, gates[3])
                    link(turn(2, krgg, 1, NOPE, QK))
                    ts(cos[QK:P, :], sin[QK:P, :], sign[QK:P, :], None, ALU.mult).then_inc(kpe_ready, 1)
                    dve.wait_ge(kpe_ready, due(kpe_ready, 1))

                    def turn_q(h):
                        dve.wait_ge(q_psum, due(q_psum, h + 1))
                        if h >= 2:
                            dve.wait_ge(scored, due(scored, (h - 1) * BLK))
                        tt(qT[NOPE:P, h % 2, :], ps[NOPE:P, QK_BANK, :], cos[NOPE:P, :], ALU.mult).then_inc(q_ready, 1)

                    def queries(b):
                        if b >= 2:
                            dve.wait_ge(gr_used, due(gr_used, b - 1))
                        tok = slice(b * P, (b + 1) * P)
                        for h in range(GH):
                            r = slice(h * DK, (h + 1) * DK)
                            stt(qx[r, 0, b % 2, h, :], gq[r, tok], DK ** -0.5, eb[r, tok], ALU.mult, ALU.mult)
                            last = stt(qx[r, 1, b % 2, h, :], gq[r, tok], DK ** -0.5, enb[r, tok], ALU.mult, ALU.mult)
                        last.then_inc(qg_ready, 1)

                    def add_states(b):
                        dve.wait_ge(ds_ready, due(ds_ready, b + 1))
                        for c in range(2 if b < BLK - 1 else 1):
                            n = 2 * b + c
                            ds_gla, ds_ret = ps[:, LIN_BANKS[c], 0:GV], ps[:, LIN_BANKS[c], GV:2 * GV]
                            if n == 0:
                                nc.vector.tensor_copy(s_gla[:, 0, :], ds_gla)
                                last = nc.vector.tensor_copy(s_ret[:, 0, :], ds_ret)
                            else:
                                at = n * CHUNK + CHUNK - 1
                                stt(s_gla[:, n, :], s_gla[:, n - 1, :], eb[:, at:at + 1], ds_gla,
                                    ALU.mult, ALU.add)
                                last = stt(s_ret[:, n, :], s_ret[:, n - 1, :], chunk_dec, ds_ret,
                                           ALU.mult, ALU.add)
                            if c == 0 and b < BLK - 1:
                                link(last)
                        last.then_inc(state_ready, 1)
                        dve.wait_ge(state_ready, due(state_ready, b + 1))

                    def keep_low(b):
                        dve.wait_ge(gated_scored, due(gated_scored, b + 1))
                        dve.wait_ge(up_kept, due(up_kept, b + 1))
                        dve.sem_inc(dve_passed)
                        low_scores = ps[:, LIN_BANKS[0], :].rearrange("p (h i) -> p h i", h=GH)
                        for c in range(2):
                            r = slice(c * CHUNK, (c + 1) * CHUNK)
                            last = nc.vector.copy_predicated(
                                attn_g[r, :, r],
                                low[r, :].rearrange("p (o i) -> p o i", o=1).broadcast_to([CHUNK, GH, CHUNK]),
                                low_scores[r, :, r])
                        last.then_inc(low_kept, 1)

                    def decayed(b):
                        dve.wait_ge(ret_scored, due(ret_scored, b + 1))
                        if b >= 1:
                            dve.wait_ge(gr_used, due(gr_used, b))
                        tt(attn_r[:], ps[:, LIN_BANKS[0], :].rearrange("p (h i) -> p h i", h=GH), decay,
                           ALU.mult).then_inc(gr_ready, 1)

                    def gated_output(t):
                        if t == 0:
                            dve.wait_ge(gate_silu, due(gate_silu, 4))
                            dve.wait_ge(o_kept, due(o_kept, BLK))
                        if t < 3:
                            dve.wait_ge(o_spread, due(o_spread, t + 1))
                        else:
                            dve.wait_ge(spread_ready, due(spread_ready, norm + 3))
                        g = G_GLA if t < 2 else G_RET
                        link(stt(heads[:, t, :], heads[:, t, :], gains[:, g:g + 1], ps[:, LIN_BANKS[t % 2], :], ALU.mult, ALU.mult))
                        tt(heads[:, t, :], heads[:, t, :], gates[t][:], ALU.mult).then_inc(o_gated, 1)

                    def linear(n):
                        if 1 <= n < LIN_STEP:
                            queries(n - 1)
                        if n < LIN_STEP:
                            add_states(n + 1)
                        elif n < NORM_STEP:
                            b, part = divmod(n - LIN_STEP, 3)
                            if part == 0:
                                if 2 <= b + 1 < BLK and b >= 1:
                                    queries(b + 1)
                                keep_low(b)
                            elif part == 1:
                                decayed(b)
                        elif n == NORM_STEP + 2:
                            dve.wait_ge(col_ready, due(col_ready, norm + 3))
                            ts(mean[:], ps[:, LIN_BANKS[0], 0:32], 1.0 / DV, EPS, ALU.mult, ALU.add).then_inc(mean_ready, 1)
                            low_at(base + IN_PAIRS)
                        if GATE_STEP <= n < GATE_STEP + 4:
                            gated_output(n - GATE_STEP)
                        if GATE_STEP + 2 <= n < GATE_STEP + 6:
                            t = n - GATE_STEP - 2
                            dve.wait_ge(gatedH_ready, due(gatedH_ready, t + 1))
                            tt(xL[:, 4 + t, :], heads[:, t, :], xH[:, 4 + t, :].bitcast(F32), ALU.subtract).then_inc(gatedL_ready, 1)
                        if n == GATE_STEP + 6:
                            low_at(base + IN_PAIRS + 1)

                    def tops(m):
                        width = (m % BLK + 1) * P
                        dve.wait_ge(scored, due(scored, m + 1))
                        s = ps[:, RING[m % 4], :]
                        link(nc.vector.memset(s[0:CHUNK, width - CHUNK:width], MASKED))
                        link(nc.vector.reduce_max(top[:, m % 4:m % 4 + 1], s[:, 0:width], AX_X))
                        ts(minus_top[:, m % 4:m % 4 + 1], top[:, m % 4:m % 4 + 1], -(QK ** -0.5), None,
                           ALU.mult).then_inc(top_ready, 1)

                    def probs(m):
                        dve.wait_ge(exped, due(exped, m + 1))
                        link(nc.vector.reciprocal(share[:, m % 4:m % 4 + 1], total[:, m % 4:m % 4 + 1]))
                        pr = prob[:, m % 3, 0:(m % BLK + 1) * P]
                        ts(pr, pr, share[:, m % 4:m % 4 + 1], None, ALU.mult).then_inc(prob_ready, 1)

                    def low_heads(i):
                        dve.wait_ge(headsH_ready, due(headsH_ready, i + 1))
                        tt(xL[:, i, :], ps[:, OUT_BANK, :], xH[:, i, :].bitcast(F32),
                           ALU.subtract).then_inc(headsL_ready, 1)

                    turn_q(0)
                    add_states(0)
                    turn_q(1)
                    dve.wait_ge(cleared, due(cleared, 1))
                    for m in range(AHEAD):
                        tops(m)
                    probs(0)
                    for n in range(STEPS):
                        h, b = divmod(n, BLK)
                        if n + 1 < STEPS:
                            probs(n + 1)
                        if h % 2 == 0 and b == 0 and h:
                            low_heads(h // 2 - 1)
                        if h + 2 < HEADS and b == 1:
                            turn_q(h + 2)
                        linear(n)
                        if n + AHEAD < STEPS:
                            tops(n + AHEAD)
                    low_heads(HEADS // 2 - 1)
                    for i in range(2, OUT_PAIRS + 1):
                        low_at(base + IN_PAIRS + i)
                    after(1, norm + 3, 1.0)

                ffn(0, 0, 0, 0)
                dve.sem_inc(dve_passed)
                nc.vector.tensor_copy(first_gains[:], gains_all[:, bass.ds(layer + 1, 1), G_PRE[0]:G_PRE[0] + DT].rearrange("p a g -> p (a g)")).then_inc(first_gains_ready, 1)
                dve.wait_ge(first_gains_ready, due(first_gains_ready, 1))
                mixer(FFN_PAIRS, 2)
                ffn(2, 1, FFN_PAIRS + MIX_PAIRS, 6)
                dve.sem_inc(dve_passed)
                nc.vector.tensor_copy(gains[:], gains_all[:, bass.ds(layer + 1, 1), :].rearrange("p a g -> p (a g)")).then_inc(gains_ready, 1)
                dve.wait_ge(gains_ready, due(gains_ready, 1))

        @block.gpsimd
        def _(pool):
            pool.wait_ge(start_ready, 1)
            with pool.Fori(0, DEPTH) as layer:
                due = counter(layer)
                def split_x(stage):
                    for n, k in enumerate(X_ORDER[1:], 1):
                        pool.wait_ge(xH_ready, due(xH_ready, DT * stage + n + 1))
                        nc.gpsimd.tensor_tensor(xL[:, k, :], xg[n % 2][:], xH[:, k, :].bitcast(F32),
                                                ALU.subtract).then_inc(xL_ready, 1)

                def power(norm, width):
                    pool.wait_ge(mean_ready, due(mean_ready, norm + 1))
                    nc.gpsimd.tensor_tensor(rstd[:, 0:width], mean[:, 0:width], minus_half[:, 0:width],
                                            ALU.pow).then_inc(rstd_ready, 1)

                split_x(0)
                power(0, 4)
                power(1, 4)
                split_x(1)
                power(2, 4)
                pool.wait_ge(spread_kept, due(spread_kept, 2))
                pool.sem_inc(pool_passed)
                nc.gpsimd.memset(attn_g[:].rearrange("p h i -> p (h i)"), 0.0)
                power(3, 8)
                pool.wait_ge(pair_done, due(pair_done, FFN_PAIRS + IN_PAIRS))
                pool.sem_inc(pool_passed)
                nc.gpsimd.memset(qx[:].rearrange("p a b h i -> p (a b h i)"), 0.0).then_inc(cleared, 1)
                pool.wait_ge(cleared, due(cleared, 1))

                def queries(b):
                    for h in range(GH):
                        r = slice(h * DK, (h + 1) * DK)
                        last = nc.gpsimd.tensor_tensor(
                            qx[r, 2, b % 2, h, :].rearrange("p (c i) -> p c i", c=2),
                            rq[r, b * P:(b + 1) * P].rearrange("p (c i) -> p c i", c=2),
                            q_dec[r, :].rearrange("p (o i) -> p o i", o=1).broadcast_to([DK, 2, CHUNK]), ALU.mult)
                    last.then_inc(qr_ready, 1)

                pool.wait_ge(mix_landed, due(mix_landed, 16 * 7))
                pool.wait_ge(ret_ready, due(ret_ready, 1))
                for b in range(BLK):
                    if b >= 2:
                        pool.wait_ge(gr_used, due(gr_used, b - 1))
                    queries(b)
                power(4, 32)
                power(5, 4)
                split_x(2)
                power(6, 4)
                power(7, 4)


def pack(np, inputs):
    def tiles(w):
        return w.reshape(DT, P, w.shape[1]).transpose(1, 0, 2).reshape(P, -1)

    def rows(w):
        return w.reshape(-1, 2, P, D).transpose(0, 2, 1, 3).reshape(-1, P, 2 * SLAB)

    blocks = []
    for l in range(DEPTH):
        def ffn(name):
            wg, wu, wd = (inputs[f"{name}_w_{k}"][l] for k in ("gate", "up", "down"))
            for f in range(FT):
                c = slice(f * P, (f + 1) * P)
                blocks.append(np.concatenate([tiles(wg[:, c]), tiles(wu[:, c])], 1)[None])
            blocks.append(rows(wd))

        ffn("ffn1")
        w = inputs["w_in"][l]
        at = np.cumsum([0, 256, 128, 32, 128, 128, 256, 16, 256, 128, 128, 256, 256])
        mq, mkv, mkr, gq, gk, gv, gg, gr, rq, rk, rv, rg = (int(a) for a in at[:-1])
        kr_gg = np.concatenate([w[:, mkr - NOPE:mkr + ROPE], w[:, gg:gg + GATE_RANK], np.zeros((D, P - QK - GATE_RANK), w.dtype)], 1)
        for a, b in ((w[:, mq:mq + P], w[:, mq + P:mq + 2 * P]), (w[:, mkv:mkv + P], kr_gg),
                     (w[:, gq:gq + P], w[:, gk:gk + P]), (w[:, rq:rq + P], w[:, rk:rk + P])):
            blocks.append(np.concatenate([tiles(a), tiles(b)], 1)[None])
        for a in (gv, rv):
            blocks.append(tiles(w[:, a:a + GV])[None])
        for a in (gr, rg):
            blocks.append(np.concatenate([tiles(w[:, a:a + P]), tiles(w[:, a + P:a + 2 * P])], 1)[None])
        blocks.append(rows(inputs["w_out"][l]))
        ffn("ffn2")
    cols = [inputs[n].reshape(DEPTH, -1, P) for n in ("ffn1_pre_g", "ffn1_post_g", "mix_pre_g", "mix_post_g",
                                                     "ffn2_pre_g", "ffn2_post_g", "mla_q_norm_g", "mla_kv_norm_g")]
    cols += [np.concatenate([inputs[n]] * 2, 1)[:, None, :] for n in ("gla_norm_g", "ret_norm_g")]
    heads = inputs["mla_w_q_up"].reshape(DEPTH, QR, HEADS, QK)
    wide = np.concatenate([heads, heads[..., NOPE + ROPE // 2:], heads[..., NOPE:NOPE + ROPE // 2]], 3)
    return {
        "x_in": inputs["x"][0].T.reshape(DT, P, SEQ).transpose(1, 0, 2),
        "positions": inputs["positions"].reshape(SEQ),
        "stream": np.concatenate(blocks, 0),
        "gains_in": np.concatenate([np.concatenate(cols, 1)] + [np.concatenate(cols, 1)[:1]], 0).transpose(0, 2, 1),
        "w_q_up": wide.reshape(DEPTH, 2, P, HEADS * P),
        "w_kv_up": inputs["mla_w_kv_up"],
        "w_gate_up": inputs["gla_w_gate_up"],
        "b_gate": inputs["gla_b_gate"].reshape(DEPTH, 1, GH * DK),
        "consts": constants(np),
    }


def constants(np):
    c = np.zeros((P, CONSTS), np.float64)
    p, i = np.arange(P)[:, None], np.arange(P)[None, :]
    same = p // CHUNK == i // CHUNK
    c[:, C_ID:C_ID + P] = np.eye(P)
    c[:, C_TRI:C_TRI + P] = (same & (p <= i)) / TAU
    half = ROPE // 2
    group = p // ROPE == i // ROPE
    c[:, C_ROT:C_ROT + P] = (group & (p == i - half)) * 1.0 - (group & (p == i + half)) * 1.0
    gamma = np.log1p(-np.exp2(-5.0 - np.arange(GH)))
    for h in range(GH):
        d = np.abs(p % CHUNK - i % CHUNK) - (i % CHUNK + 1.0)
        c[:, C_DEC + h * P:C_DEC + (h + 1) * P] = same * np.exp(gamma[h] * d) * DK ** -0.5
    j = np.arange(CHUNK)[None, :]
    c[:, C_LOW:C_LOW + CHUNK] = p % CHUNK <= j
    g = gamma[np.arange(P) // DK][:, None]
    c[:, C_QDEC:C_QDEC + CHUNK] = np.exp(g * (j + 1.0))
    c[:, C_KDEC:C_KDEC + CHUNK] = np.exp(g * (CHUNK - 1.0 - j)) * DK ** -0.5
    c[:, C_CDEC:C_CDEC + 1] = np.exp(g * CHUNK)
    c[:, C_SIGN:C_SIGN + 1] = np.where(p % ROPE < half, -1.0, 1.0)
    c[:, C_TWICE:C_TWICE + 2 * ROPE] = p % ROPE == np.arange(2 * ROPE)[None, :] % ROPE
    c[:, C_HSEL:C_HSEL + 2] = p // DV == np.arange(2)[None, :]
    c[:, C_INV:C_INV + 1] = 10000.0 ** (-(2.0 * (p % half)) / ROPE)
    return c.astype(np.float32)


def kernel(**inputs):
    import numpy as np
    import concourse.bacc as bacc
    from concourse.bass_utils import run_bass_kernel_spmd

    nc = bacc.Bacc("TRN2", target_bir_lowering=False, num_devices=1)
    arrays = {k: np.ascontiguousarray(v) for k, v in pack(np, {k: np.asarray(v) for k, v in inputs.items()}).items()}
    args = {k: nc.dram_tensor(k, v.shape, mybir.dt.from_np(v.dtype), kind="ExternalInput").ap()
            for k, v in arrays.items()}
    out = nc.dram_tensor("out", (P, DT, SEQ), F32, kind="ExternalOutput").ap()
    hybrid_trunk(nc, out=out, **args)
    r = run_bass_kernel_spmd(nc, [arrays], core_ids=[0])
    y = r.results[0]["out"]
    return np.ascontiguousarray(y.transpose(1, 0, 2).reshape(D, SEQ).T)[None]
```

```python
from contextlib import ExitStack

import concourse.bass as bass
from concourse import mybir

ALU = mybir.AluOpType
ACT = mybir.ActivationFunctionType
F32 = mybir.dt.float32
F32R = mybir.dt.float32r
I32 = mybir.dt.int32
AX_X = mybir.AxisListType.X

P = 128
SEQ = 512
D = 1024
DT = D // P
DEPTH = 2
FF = 2816
FT = FF // P
CHUNK = 64
NCHUNK = SEQ // CHUNK
BLK = SEQ // P
EPS = 1e-6
TAU = 16.0
HEADS = 8
NOPE, ROPE, DV = 64, 32, 64
QK = NOPE + ROPE
QR, KVR = 256, 128
GH, DK = 4, 32
GV = GH * DV
GATE_RANK = 16
MASKED = -3.0e38

FFN_PAIRS = FT + FT // 2
IN_PAIRS, OUT_PAIRS = 8, 4
MIX_PAIRS = IN_PAIRS + OUT_PAIRS
PAIRS = 2 * FFN_PAIRS + MIX_PAIRS
SLAB = 8 * P
SQUARES = 2 * DT - 1
NORMS = 8

G_PRE = (0, 16, 32)
G_POST = (8, 24, 40)
G_Q, G_KV, G_GLA, G_RET = 48, 50, 51, 52
GAINS = 53

C_ID = 0
C_TRI = C_ID + P
C_ROT = C_TRI + P
C_DEC = C_ROT + P
C_LOW = C_DEC + GH * P
C_QDEC = C_LOW + CHUNK
C_KDEC = C_QDEC + CHUNK
C_CDEC = C_KDEC + CHUNK
C_SIGN = C_CDEC + 1
C_TWICE = C_SIGN + 1
C_HSEL = C_TWICE + 2 * ROPE
C_INV = C_HSEL + 2
CONSTS = C_INV + 1

BUSY = (1, 4, 5)

X_ORDER = [0, 1, 2, 3, 4, 5, 6, 7]
F_ORDER = [0, 1, 2, 3, 4, 5, 6, 7]
FFN_START = [2, 3, 6, 7, 4, 5, 0, 1]
ROUND_F = 6
FFN_BANKS = ((0, 1), (2, 3), (4, 5))
MIX_START, MIX_REST = [0, 1, 6], [2, 3, 4, 5, 7]

TWO_PI = 6.283185307179586
C1 = 6.28125
C2 = 0.0019350051879882812
C3 = TWO_PI - C1 - C2
ROUND = 12582912.0

QK_BANK, LIN_BANKS, OUT_BANK = 0, (1, 6), 7
RING = (2, 3, 4, 5)
STEPS = HEADS * BLK
AHEAD = 3
LIN_STEP = 3
NORM_STEP = LIN_STEP + 3 * BLK
GATE_STEP = NORM_STEP + 5

DVE_STEPS = 92
ACT_STEPS = 2


def hybrid_trunk(nc, x_in, positions, stream, gains_in, w_q_up, w_kv_up, w_gate_up, b_gate, consts, out):
    ctx = ExitStack()
    with ctx:
        def sb(name, shape, dt=F32, stack=ctx):
            return stack.enter_context(nc.sbuf_tensor(name, shape, dt))

        per_layer, ahead = {}, {}

        def sem(name, times, before=0):
            made = ctx.enter_context(nc.semaphore(name))
            per_layer[made], ahead[made] = times, before
            return made

        def counter(layer):
            def due(semaphore, n):
                return layer * per_layer[semaphore] + n + ahead[semaphore]
            return due

        ps = ctx.enter_context(nc.psum_tensor("ps", [P, 8, 512], F32))

        x = sb("x", [P, DT, SEQ])
        with ExitStack() as linear:
            sb("xH_head", [P, 1, SEQ], F32, linear)
            states = sb("states", [P, 2, NCHUNK - 1, GV], F32, linear)
            sb("xL_head", [P, 2, SEQ], F32, linear)
            qx = sb("qx", [P, 3, 2, GH, P], F32, linear)
        s_gla, s_ret = states[:, 0], states[:, 1]
        xH = sb("xH", [P, DT, SEQ], F32R)
        xL = sb("xL", [P, DT, SEQ], F32R)
        raw = sb("raw", [P, 2, 2 * SLAB])
        WH = sb("WH", [P, 2, 2 * SLAB], F32R)
        WL = sb("WL", [P, 2, 2 * SLAB], F32R)
        rstd_x = sb("rstd_x", [P, SEQ])
        f_first = sb("f_first", [P, SEQ])
        gate3 = sb("gate3", [P, SEQ])
        gate = sb("gate", [P, SEQ])
        up = sb("up", [P, SEQ])
        xg = [gate, up]
        sq = sb("sq", [P, 2, SEQ])
        acc = sb("acc", [P, SEQ])
        ident = sb("ident", [P, P])
        ones = sb("ones", [P, 1])
        ones_row = sb("ones_row", [P, P])
        gains_all = sb("gains_all", [P, DEPTH + 1, GAINS])
        gains = sb("gains", [P, GAINS])
        first_gains = sb("first_gains", [P, DT])
        mean = sb("mean", [P, 32])
        rstd = sb("rstd", [P, 32])
        minus_half = sb("minus_half", [P, 32])
        table_column = sb("table_column", [P, 1])
        rx_col = sb("rx_col", [P, BLK])
        b_last = sb("b_last", [P, NCHUNK])
        top = sb("top", [P, 4])
        minus_top = sb("minus_top", [P, 4])
        total = sb("total", [P, 2, BLK])
        share = sb("share", [P, 2, BLK])

        with ExitStack() as hidden:
            hH = sb("hH", [P, FT, SEQ], F32R, hidden)
            hL = sb("hL", [P, FT, SEQ], F32R, hidden)
        mq = sb("mq", [P, 2, SEQ])
        ckv = sb("ckv", [P, SEQ])
        krgg = sb("krgg", [P, SEQ])
        heads = sb("heads", [P, 4, SEQ])
        gq, gk, rq, rk = (heads[:, t, :] for t in range(4))
        v_tok = sb("v_tok", [P, BLK, 2 * GV])
        gates = [gate, up, f_first, gate3]
        cos = sb("cos", [P, SEQ])
        sin = sb("sin", [P, SEQ])
        wq = sb("wq", [P, 2, HEADS * P])
        wkv = sb("wkv", [P, HEADS * (NOPE + DV)])
        wgu = sb("wgu", [P, GH * DK])
        bias = sb("bias", [P, GH * DK])
        const = sb("const", [P, CONSTS])
        zg = sb("zg", [P, SEQ])
        eb = sb("eb", [P, SEQ])
        enb = sb("enb", [P, SEQ])
        kf = sb("kf", [P, SEQ])
        kb = sb("kb", [P, SEQ])
        ks_ret = sb("ks_ret", [P, SEQ])
        kt_gla = sb("kt_gla", [P, BLK, P])
        kt_ret = sb("kt_ret", [P, BLK, P])
        attn_g = sb("attn_g", [P, GH, P])
        attn_r = sb("attn_r", [P, GH, P])
        qT = sb("qT", [P, 2, SEQ])
        kT = sb("kT", [P, 2, SEQ])
        v_mla = sb("v_mla", [P, BLK, HEADS * DV])
        prob = sb("prob", [P, 3, SEQ])
        probT = sb("probT", [P, 2, SEQ])

        tri = const[:, C_TRI:C_TRI + P]
        rot = const[:, C_ROT:C_ROT + P]
        decay = const[:, C_DEC:C_DEC + GH * P].rearrange("p (h i) -> p h i", h=GH)
        low = const[:, C_LOW:C_LOW + CHUNK].bitcast(I32)
        q_dec = const[:, C_QDEC:C_QDEC + CHUNK]
        k_dec = const[:, C_KDEC:C_KDEC + CHUNK]
        chunk_dec = const[:, C_CDEC:C_CDEC + 1]
        sign = const[:, C_SIGN:C_SIGN + 1]
        twice = const[:, C_TWICE:C_TWICE + 2 * ROPE]
        head_sel = const[:, C_HSEL:C_HSEL + 2]
        inv_freq = const[:, C_INV:C_INV + 1]

        pair_out = (kt_gla, kt_ret)

        landed = [sem(f"pair_landed{i}", 16 * PAIRS // 2) for i in range(2)]
        wH_ready = sem("wH_ready", PAIRS)
        wL_ready = sem("wL_ready", PAIRS)
        pair_done = sem("pair_done", PAIRS, 2)
        gains_landed = sem("gains_landed", 0)
        ident_landed = sem("ident_landed", 0)
        x_landed = [sem(f"x_landed{i}", 0) for i in range(4)]
        start_ready = sem("start_ready", 0)
        x_ready = sem("x_ready", 3 * DT, DT)
        gains_ready = sem("gains_ready", 1, 1)
        first_gains_ready = sem("first_gains_ready", 1, 1)
        xH_ready = sem("xH_ready", 3 * DT)
        xg_ready = sem("xg_ready", 3 * DT)
        xL_ready = sem("xL_ready", 3 * DT)
        sq_ready = sem("sq_ready", 6 * DT)
        sq_used = sem("sq_used", 3 * SQUARES)
        f_kept = sem("f_kept", 6)
        f_ready = sem("f_ready", 3 * (DT - 1))
        f_normed = sem("f_normed", 3 * DT)
        rstd_kept = sem("rstd_kept", 3, 1)
        col_ready = sem("col_ready", NORMS)
        mean_ready = sem("mean_ready", NORMS)
        rstd_ready = sem("rstd_ready", NORMS)
        spread_ready = sem("spread_ready", NORMS)
        o_spread = sem("o_spread", 3)
        spread_kept = sem("spread_kept", 3)
        gu_scaled = sem("gu_scaled", 2 * FT)
        silu_ready = sem("silu_ready", 2 * FT)
        h_ready = sem("h_ready", 2 * FT)
        hH_ready = sem("hH_ready", 2 * FT)
        hL_ready = sem("hL_ready", 2 * FT)
        dve_step = sem("dve_step", DVE_STEPS)
        act_step = sem("act_step", ACT_STEPS)
        out_stored = sem("out_stored", 0)
        pool_passed = sem("pool_passed", 0)
        dve_passed = sem("dve_passed", 0)
        mix_landed = sem("mix_landed", 16 * 7)
        in_kept = sem("in_kept", 12)
        v_kept = sem("v_kept", 2)
        gate_silu = sem("gate_silu", 4)
        angle_ready = sem("angle_ready", 1)
        sine_ready = sem("sine_ready", 2)
        rope_ready = sem("rope_ready", 1)
        latent_sq = sem("latent_sq", 3)
        latent_ready = sem("latent_ready", 3)
        z_ready = sem("z_ready", 1)
        soft_ready = sem("soft_ready", 1)
        log_ready = sem("log_ready", 1)
        cum_ready = sem("cum_ready", 1)
        b_last_ready = sem("b_last_ready", 1)
        exp_ready = sem("exp_ready", 3)
        k_ready = sem("k_ready", 3)
        rot_ready = sem("rot_ready", 3)
        ret_ready = sem("ret_ready", 1)
        kpe_ready = sem("kpe_ready", 1)
        kt_psum = sem("kt_psum", 2)
        kt_kept = sem("kt_kept", 2)
        ds_ready = sem("ds_ready", BLK)
        state_ready = sem("state_ready", BLK)
        cleared = sem("cleared", 1)
        qg_ready = sem("qg_ready", BLK)
        qr_ready = sem("qr_ready", BLK)
        gated_scored = sem("gated_scored", BLK)
        ret_scored = sem("ret_scored", BLK)
        low_kept = sem("low_kept", BLK)
        up_kept = sem("up_kept", BLK)
        gr_ready = sem("gr_ready", BLK)
        gr_used = sem("gr_used", BLK)
        o_kept = sem("o_kept", BLK)
        o_sq = sem("o_sq", 4)
        o_sq_used = sem("o_sq_used", 3)
        o_normed = sem("o_normed", 4)
        o_gated = sem("o_gated", 4)
        gatedH_ready = sem("gatedH_ready", 4)
        gatedL_ready = sem("gatedL_ready", 4)
        headsH_ready = sem("headsH_ready", HEADS // 2)
        headsL_ready = sem("headsL_ready", HEADS // 2)
        vm_psum = sem("vm_psum", BLK)
        vm_kept = sem("vm_kept", BLK)
        q_psum = sem("q_psum", HEADS)
        q_kept = sem("q_kept", HEADS)
        q_ready = sem("q_ready", HEADS)
        k_psum = sem("k_psum", HEADS)
        k_kept = sem("k_kept", HEADS)
        kpe_psum = sem("kpe_psum", 1)
        kpe_copied = sem("kpe_copied", 2)
        scored = sem("scored", HEADS * BLK)
        top_ready = sem("top_ready", HEADS * BLK)
        exped = sem("exped", HEADS * BLK)
        turned = sem("turned", HEADS * BLK)
        turn_kept = sem("turn_kept", HEADS * BLK)
        valued = sem("valued", HEADS * BLK)
        head_kept = sem("head_kept", HEADS)
        heads_turned = sem("heads_turned", HEADS // 2)

        block = ctx.enter_context(nc.Block())

        @block.sync
        def _(sp):
            sp.dma_start(raw[:, 0, :], stream[0]).then_inc(landed[0], 16)
            sp.dma_start(gains_all[:], gains_in.rearrange("l p g -> p l g")).then_inc(gains_landed, 16)
            sp.dma_start(ident[:], consts[:, C_ID:C_ID + P]).then_inc(ident_landed, 16)
            for c in range(4):
                if c == 1:
                    sp.dma_start(raw[:, 1, :], stream[1]).then_inc(landed[1], 16)
                sp.dma_start(x[:, 2 * c:2 * c + 2, :], x_in[:, 2 * c:2 * c + 2, :]).then_inc(x_landed[c], 16)
            for c in range(4):
                sp.wait_ge(x_landed[c], 16)
                sp.sem_inc(x_ready, 2)
            with sp.Fori(1, DEPTH * PAIRS // 2) as m:
                for slot in range(2):
                    sp.wait_ge(wH_ready, 2 * m + (slot - 1))
                    sp.wait_ge(wL_ready, 2 * m + (slot - 1))
                    sp.dma_start(raw[:, slot, :], stream[2 * m + slot]).then_inc(landed[slot], 16)
            for slot in range(2):
                sp.wait_ge(wH_ready, DEPTH * PAIRS + slot - 1)
                sp.wait_ge(wL_ready, DEPTH * PAIRS + slot - 1)
                sp.dma_start(raw[:, slot, :], stream[slot]).then_inc(landed[slot], 16)
            for n, k in enumerate(X_ORDER):
                sp.wait_ge(x_ready, ahead[x_ready] + DEPTH * per_layer[x_ready] - DT + n + 1)
                sp.dma_start(out[:, k, :], x[:, k, :]).then_inc(out_stored, 16)
            sp.wait_ge(out_stored, 16 * DT)

        @block.tensor
        def _(pe):
            mm = nc.tensor.matmul
            pe.sem_inc(pair_done, 2)
            pe.sem_inc(rstd_kept, 1)
            pe.wait_ge(start_ready, 1)
            pe.wait_ge(ident_landed, 16)

            def three(dst, wh, wl, xh, xl, start, stop):
                mm(dst, wh, xh, start=start, stop=False)
                mm(dst, wh, xl, start=False, stop=False)
                return mm(dst, wl, xh, start=False, stop=stop)

            with pe.Fori(0, DEPTH) as layer:
                due = counter(layer)

                def first_pair(p, slot, banks, stage):
                    pe.wait_ge(wH_ready, due(wH_ready, p + 1))
                    pe.wait_ge(wL_ready, due(wL_ready, p + 1))
                    pe.wait_ge(rstd_kept, due(rstd_kept, stage))
                    for n in range(DT + 1):
                        if n < DT:
                            pe.wait_ge(xH_ready, due(xH_ready, DT * stage + n + 1))
                            for j in range(2):
                                at = j * SLAB + X_ORDER[n] * P
                                h = xH[:, X_ORDER[n], :]
                                mm(ps[:, banks[j], :], WH[:, slot, at:at + P], h, start=n == 0, stop=False)
                                mm(ps[:, banks[j], :], WL[:, slot, at:at + P], h, start=False, stop=False)
                        if n:
                            pe.wait_ge(xL_ready, due(xL_ready, DT * stage + n))
                            for j in range(2):
                                at = j * SLAB + X_ORDER[n - 1] * P
                                last = mm(ps[:, banks[j], :], WH[:, slot, at:at + P], xL[:, X_ORDER[n - 1], :],
                                          start=False, stop=n == DT)
                    last.then_inc(pair_done, 1)

                def tiles_pair(p, slot, banks, widths=(P, P), middle=None):
                    pe.wait_ge(wH_ready, due(wH_ready, p + 1))
                    pe.wait_ge(wL_ready, due(wL_ready, p + 1))
                    for n, k in enumerate(X_ORDER):
                        if n == DT // 2 and middle is not None:
                            middle()
                        for j in range(2):
                            at = j * SLAB + k * P
                            last = three(ps[0:widths[j], banks[j], :], WH[:, slot, at:at + widths[j]],
                                         WL[:, slot, at:at + widths[j]], xH[:, k, :], xL[:, k, :],
                                         n == 0, n == DT - 1)
                    last.then_inc(pair_done, 1)

                def columns(bank, squares):
                    pe.wait_ge(sq_used, due(sq_used, squares))
                    for c in range(BLK):
                        last = mm(ps[:, bank, c:c + 1], acc[:, c * P:(c + 1) * P], ones[:], start=True, stop=True)
                    last.then_inc(col_ready, 1)

                def spread(norm, bank):
                    pe.wait_ge(rstd_ready, due(rstd_ready, norm + 1))
                    for c in range(BLK):
                        last = mm(ps[:, bank, c * P:(c + 1) * P], rstd[:, c:c + 1].broadcast_to([P, P]), ident[:],
                                  start=True, stop=True)
                    last.then_inc(spread_ready, 1)

                def down_tile(p, slot, d, moving, first, last_pair):
                    for j in range(2):
                        at = j * SLAB + d * P
                        h, l = moving[j]
                        last = three(ps[:, d, :], WH[:, slot, at:at + P], WL[:, slot, at:at + P], h, l,
                                     first and j == 0, last_pair and j == 1)
                    if last_pair and d != F_ORDER[-1]:
                        last.then_inc(f_ready, 1)
                    return last

                def down_pair(p, slot, moving, first, last_pair, order=F_ORDER, scaled=None):
                    pe.wait_ge(wH_ready, due(wH_ready, p + 1))
                    pe.wait_ge(wL_ready, due(wL_ready, p + 1))
                    for d in order:
                        if scaled is not None and d in (2, 4, 0):
                            pe.wait_ge(gu_scaled, due(gu_scaled, scaled - {2: 2, 4: 1, 0: 0}[d]))
                        last = down_tile(p, slot, d, moving, first, last_pair)
                    last.then_inc(pair_done, 1)

                def ffn(stage, f_stage, base, norm):
                    slot = base % 2
                    first_pair(base, slot, (0, 1), stage)
                    tiles_pair(base + 1, 1 - slot, (2, 3))
                    columns(6, SQUARES * stage + DT)
                    tiles_pair(base + 2, slot, (4, 5), middle=lambda: spread(norm, 6))
                    with pe.Fori(0, (FT - 4) // ROUND_F) as i:
                        for j in range(ROUND_F):
                            f = ROUND_F * i + 3 + j
                            pe.wait_ge(gu_scaled, due(gu_scaled, FT * f_stage + f - 2))
                            tiles_pair(base + f, (slot + 1 + j) % 2, FFN_BANKS[j % 3])
                    pe.wait_ge(gu_scaled, due(gu_scaled, FT * (f_stage + 1) - 3))
                    tiles_pair(base + FT - 1, 1 - slot, (0, 1))
                    pe.wait_ge(spread_kept, due(spread_kept, stage + 1))

                    def hidden(j, f):
                        pe.wait_ge(hH_ready, due(hH_ready, FT * f_stage + f + 2))
                        pe.wait_ge(hL_ready, due(hL_ready, FT * f_stage + f + 2))
                        return [(hH[:, f + a, :], hL[:, f + a, :]) for a in range(2)]

                    for j in range(2):
                        down_pair(base + FT + j, (slot + j) % 2, hidden(j, 2 * j), j == 0, False,
                                  order=FFN_START if j == 0 else F_ORDER,
                                  scaled=FT * (f_stage + 1) if j == 0 else None)
                    with pe.Fori(1, FT // 4) as m:
                        for j in range(2):
                            down_pair(base + FT + 2 * m + j, (slot + j) % 2, hidden(j, 4 * m + 2 * j), False, False)
                    down_pair(base + FT + FT // 2 - 1, slot, hidden(0, FT - 2), False, True)
                    after(stage, norm + 1, base + FT + FT // 2)

                def busy(p, products):
                    for _ in range(products):
                        mm(ps[:, 1, :], WH[:, p % 2, 0:P], WH[:, p % 2, 0:SEQ], start=True, stop=True)

                def after(stage, norm, p):
                    pe.wait_ge(f_kept, due(f_kept, 2 * (stage + 1)))
                    pe.wait_ge(wH_ready, due(wH_ready, p + 1))
                    pe.wait_ge(sq_used, due(sq_used, SQUARES * (stage + 1)))
                    for c in range(BLK):
                        mm(ps[:, 0, c:c + 1], acc[:, c * P:(c + 1) * P], ones[:], start=c == 0, stop=False,
                           skip_group_check=True)
                    busy(p, BUSY[0])
                    pe.wait_ge(sq_ready, due(sq_ready, 2 * DT * (stage + 1)))
                    for c in range(BLK):
                        last = mm(ps[:, 0, c:c + 1], sq[:, 1, c * P:(c + 1) * P], ones[:], start=False, stop=True,
                                  skip_group_check=True)
                    last.then_inc(col_ready, 1)
                    busy(p, BUSY[1])
                    spread(norm, 0)
                    busy(p, BUSY[2])

                def mixer(base, norm):
                    stage = 1
                    slot = base % 2

                    def pair(i, banks, **kw):
                        tiles_pair(base + i, (slot + i) % 2, banks, **kw)

                    def values_pair(i, banks):
                        s = (slot + i) % 2
                        pe.wait_ge(wH_ready, due(wH_ready, base + i + 1))
                        pe.wait_ge(wL_ready, due(wL_ready, base + i + 1))
                        for b in range(BLK):
                            dst = ps[:, banks[b // 2], (b % 2) * GV:(b % 2 + 1) * GV]
                            for k in range(DT):
                                at, tok = k * GV, slice(b * P, (b + 1) * P)
                                mm(dst, xH[:, k, tok], WH[:, s, at:at + GV], start=k == 0, stop=False)
                                mm(dst, xH[:, k, tok], WL[:, s, at:at + GV], start=False, stop=False)
                                last = mm(dst, xL[:, k, tok], WH[:, s, at:at + GV], start=False, stop=k == DT - 1)
                        last.then_inc(pair_done, 1)

                    first_pair(base, slot, (0, 1), stage)
                    pair(1, (2, 3), widths=(P, QK + GATE_RANK))
                    columns(6, SQUARES * stage + DT)
                    pair(2, (4, 5), middle=lambda: spread(norm, 6))
                    pe.wait_ge(in_kept, due(in_kept, 2))
                    pair(3, (0, 1))
                    pe.wait_ge(in_kept, due(in_kept, 4))
                    pe.wait_ge(mix_landed, due(mix_landed, 16 * 7))
                    pe.wait_ge(spread_kept, due(spread_kept, 2))
                    for b in range(BLK):
                        dst = ps[:, 7, b * P:(b + 1) * P]
                        mm(dst, krgg[QK:QK + GATE_RANK, b * P:(b + 1) * P], wgu[QK:QK + GATE_RANK, :], start=True, stop=False)
                        last = mm(dst, ones_row[QK:QK + 1, :], bias[QK:QK + 1, :], start=False, stop=True)
                    last.then_inc(z_ready, 1)
                    values_pair(4, (2, 3))
                    pe.wait_ge(latent_sq, due(latent_sq, 3))
                    for c in range(BLK):
                        tok = slice(c * P, (c + 1) * P)
                        mm(ps[:, 6, c:c + 1], sq[:, 0, tok], ones[:], start=True, stop=False)
                        mm(ps[:, 6, c:c + 1], sq[:, 1, tok], ones[:], start=False, stop=True)
                        last = mm(ps[:, 6, 4 + c:5 + c], acc[:, tok], ones[:], start=True, stop=True)
                    last.then_inc(col_ready, 1)
                    pe.wait_ge(in_kept, due(in_kept, 6))
                    values_pair(5, (4, 5))
                    pe.wait_ge(log_ready, due(log_ready, 1))
                    for b in range(BLK):
                        last = mm(ps[:, 7, b * P:(b + 1) * P], zg[:, b * P:(b + 1) * P], tri, start=True, stop=True)
                    last.then_inc(cum_ready, 1)
                    pe.wait_ge(in_kept, due(in_kept, 8))
                    pair(6, (0, 1))
                    pe.wait_ge(v_kept, due(v_kept, 2))
                    pe.wait_ge(rstd_ready, due(rstd_ready, norm + 2))
                    for c in range(BLK):
                        tok = slice(c * P, (c + 1) * P)
                        mm(ps[:, 6, tok], rstd[:, c:c + 1].broadcast_to([P, P]), ident[:], start=True, stop=True)
                        last = mm(ps[:, 4, tok], rstd[:, 4 + c:5 + c].broadcast_to([P, P]), ident[:], start=True, stop=True)
                    last.then_inc(spread_ready, 1)
                    mm(ps[:, 5, :], rot, rq[:], start=True, stop=True).then_inc(rot_ready, 1)

                    def rotate_rk():
                        pe.wait_ge(exp_ready, due(exp_ready, 3))
                        mm(ps[:, 7, :], rot, rk[:], start=True, stop=True).then_inc(rot_ready, 1)

                    pair(7, (2, 3), middle=rotate_rk)
                    pe.wait_ge(in_kept, due(in_kept, 10))
                    mm(ps[0:QK, 1, :], rot[NOPE:QK, 0:QK], krgg[NOPE:QK, :], start=True, stop=True).then_inc(rot_ready, 1)
                    pe.wait_ge(k_ready, due(k_ready, 3))
                    pe.wait_ge(latent_ready, due(latent_ready, 3))
                    for b in range(BLK):
                        last = nc.tensor.transpose(ps[:, 6, b * P:(b + 1) * P], zg[:, b * P:(b + 1) * P], ident[:])
                    last.then_inc(kt_psum, 1)
                    pe.wait_ge(ret_ready, due(ret_ready, 1))
                    for b in range(BLK):
                        last = nc.tensor.transpose(ps[:, 7, b * P:(b + 1) * P], ks_ret[:, b * P:(b + 1) * P], ident[:])
                    last.then_inc(kt_psum, 1)

                    def make_values(b):
                        mm(ps[:, RING[b], :], ckv[:, b * P:(b + 1) * P],
                           wkv[:].rearrange("p (h c) -> p h c", h=HEADS)[:, :, NOPE:NOPE + DV],
                           start=True, stop=True).then_inc(vm_psum, 1)

                    def make_q(h):
                        if h >= 1:
                            pe.wait_ge(k_kept, due(k_kept, h))
                        if h >= 5 and h % 2:
                            pe.wait_ge(headsL_ready, due(headsL_ready, (h - 3) // 2))
                        for k in range(2):
                            last = mm(ps[:, QK_BANK, :], wq[:, k, h * P:(h + 1) * P], mq[:, k, :],
                                      start=k == 0, stop=k == 1)
                        last.then_inc(q_psum, 1)

                    def make_k(h):
                        pe.wait_ge(q_kept, due(q_kept, h + 1))
                        pe.wait_ge(q_ready, due(q_ready, h + 1))
                        at = h * (NOPE + DV)
                        mm(ps[0:NOPE, QK_BANK, :], wkv[:, at:at + NOPE], ckv[:], start=True, stop=True).then_inc(k_psum, 1)

                    def state_parts(b):
                        if b:
                            pe.wait_ge(state_ready, due(state_ready, b))
                        for c in range(2 if b < BLK - 1 else 1):
                            rows = slice(c * CHUNK, (c + 1) * CHUNK)
                            mm(ps[:, LIN_BANKS[c], 0:GV], kt_gla[rows, b, :], v_tok[rows, b, 0:GV], start=True, stop=True)
                            last = mm(ps[:, LIN_BANKS[c], GV:2 * GV], kt_ret[rows, b, :], v_tok[rows, b, GV:2 * GV],
                                      start=True, stop=True)
                        last.then_inc(ds_ready, 1)

                    def gated_scores(b):
                        tok = slice(b * P, (b + 1) * P)
                        pe.wait_ge(qg_ready, due(qg_ready, b + 1))
                        if b:
                            pe.wait_ge(gr_ready, due(gr_ready, b))
                            pe.wait_ge(o_kept, due(o_kept, b))
                        else:
                            pe.wait_ge(state_ready, due(state_ready, BLK))
                        mm(ps[:, LIN_BANKS[0], :], kf[:, tok], qx[:, 0, b % 2].rearrange("p h i -> p (h i)"), start=True, stop=True)
                        mm(ps[:, LIN_BANKS[1], :], kb[:, tok], qx[:, 1, b % 2].rearrange("p h i -> p (h i)"), start=True,
                           stop=True).then_inc(gated_scored, 1)

                    def retention_scores(b):
                        tok = slice(b * P, (b + 1) * P)
                        pe.wait_ge(qr_ready, due(qr_ready, b + 1))
                        pe.wait_ge(low_kept, due(low_kept, b + 1))
                        mm(ps[:, LIN_BANKS[0], :], rk[:, tok], qx[:, 2, b % 2].rearrange("p h i -> p (h i)"), start=True,
                           stop=True).then_inc(ret_scored, 1)

                    def linear_values(b):
                        pe.wait_ge(gr_ready, due(gr_ready, b + 1))
                        for kind, (attn, state) in enumerate(((attn_g, s_gla), (attn_r, s_ret))):
                            for h in range(GH):
                                rows = slice(DV * (h % 2), DV * (h % 2 + 1))
                                at = (2 * kind + h // 2) * P
                                vcol = slice(kind * GV + h * DV, kind * GV + (h + 1) * DV)
                                last = mm(ps[rows, LIN_BANKS[1], at:at + P], v_tok[:, b, vcol], attn[:, h, :],
                                          start=True, stop=False)
                                for c in range(2):
                                    n = 2 * b + c
                                    if n == 0:
                                        continue
                                    last = mm(ps[rows, LIN_BANKS[1], at + c * CHUNK:at + (c + 1) * CHUNK],
                                              state[:, n - 1, h * DV:(h + 1) * DV],
                                              qx[:, 2 * kind, b % 2, h, c * CHUNK:(c + 1) * CHUNK],
                                              start=False, stop=c == 1)
                        last.then_inc(gr_used, 1)

                    def linear_squares(t):
                        pe.wait_ge(o_sq, due(o_sq, t + 1))
                        for c in range(BLK):
                            last = mm(ps[:, LIN_BANKS[0], t * 8 + 2 * c:t * 8 + 2 * c + 2], sq[:, t % 2, c * P:(c + 1) * P],
                                      head_sel, start=True, stop=True)
                        last.then_inc(o_sq_used if t < 3 else col_ready, 1)

                    def linear_spread(t):
                        if t == 0:
                            pe.wait_ge(rstd_ready, due(rstd_ready, norm + 3))
                        if t >= 2:
                            pe.wait_ge(o_normed, due(o_normed, t - 1))
                        for c in range(BLK):
                            for h in range(2):
                                at = t * 8 + 2 * c + h
                                last = mm(ps[h * DV:(h + 1) * DV, LIN_BANKS[t % 2], c * P:(c + 1) * P],
                                          rstd[:, at:at + 1].broadcast_to([P, DV]), ident[:], start=True, stop=True)
                        last.then_inc(o_spread if t < 3 else spread_ready, 1)

                    def linear(n):
                        if n < LIN_STEP:
                            state_parts(n + 1)
                        elif n < NORM_STEP:
                            b = (n - LIN_STEP) // 3
                            (gated_scores, retention_scores, linear_values)[(n - LIN_STEP) % 3](b)
                        elif NORM_STEP < n <= NORM_STEP + 2:
                            for t in range(2):
                                linear_squares(2 * (n - NORM_STEP - 1) + t)
                        elif GATE_STEP <= n < GATE_STEP + 4:
                            linear_spread(n - GATE_STEP)

                    def scores(m):
                        h, b = divmod(m, BLK)
                        if b == 0:
                            pe.wait_ge(q_ready, due(q_ready, h + 1))
                            pe.wait_ge(k_kept, due(k_kept, h + 1))
                        if m == 0:
                            pe.wait_ge(vm_kept, due(vm_kept, BLK))
                        mm(ps[:, RING[m % 4], 0:(b + 1) * P], qT[:, h % 2, b * P:(b + 1) * P],
                           kT[:, h % 2, 0:(b + 1) * P], start=True, stop=True).then_inc(scored, 1)

                    def turn(m):
                        pe.wait_ge(exped, due(exped, m + 1))
                        for kk in range(m % BLK + 1):
                            last = nc.tensor.transpose(ps[:, RING[m % 4], kk * P:(kk + 1) * P],
                                                       prob[:, m % 3, kk * P:(kk + 1) * P], ident[:])
                        last.then_inc(turned, 1)

                    def values(m):
                        h, b = divmod(m, BLK)
                        pe.wait_ge(turn_kept, due(turn_kept, m + 1))
                        if b == 0 and h:
                            pe.wait_ge(head_kept, due(head_kept, h))
                        for kk in range(b + 1):
                            last = mm(ps[:, OUT_BANK, b * DV:(b + 1) * DV], probT[:, m % 2, kk * P:(kk + 1) * P],
                                      v_mla[:, kk, h * DV:(h + 1) * DV], start=kk == 0, stop=kk == b)
                        last.then_inc(valued, 1)

                    def mixed(i):
                        return [(xH[:, 2 * i + a, :], xL[:, 2 * i + a, :]) for a in range(2)]

                    def turn_heads(i, bank):
                        pe.wait_ge(head_kept, due(head_kept, 2 * i + 2))
                        if bank == QK_BANK:
                            pe.wait_ge(k_kept, due(k_kept, min(2 * i + 5, HEADS)))
                        for b in range(BLK):
                            last = nc.tensor.transpose(ps[:, bank, b * P:(b + 1) * P], pair_out[i % 2][:, b, :], ident[:])
                        last.then_inc(heads_turned, 1)

                    make_values(2)
                    make_values(3)
                    make_q(0)
                    pe.wait_ge(in_kept, due(in_kept, 12))
                    make_values(0)
                    make_values(1)
                    pe.wait_ge(kpe_ready, due(kpe_ready, 1))
                    mm(ps[NOPE:P, LIN_BANKS[0], :], twice[NOPE:QK, :], krgg[NOPE:QK, :], start=True,
                       stop=True).then_inc(kpe_psum, 1)
                    make_k(0)
                    pe.wait_ge(kt_kept, due(kt_kept, 2))
                    pe.wait_ge(kpe_copied, due(kpe_copied, 2))
                    state_parts(0)
                    make_q(1)
                    scores(0)
                    make_k(1)
                    scores(1)
                    scores(2)
                    for n in range(STEPS):
                        h, b = divmod(n, BLK)
                        turn(n)
                        if n:
                            values(n - 1)
                        if h + 2 < HEADS and b == 1:
                            make_q(h + 2)
                        if h + 2 < HEADS and b == 2:
                            make_k(h + 2)
                        if h and h % 2 == 0 and b == 3:
                            turn_heads(h // 2 - 1, QK_BANK)
                        linear(n)
                        if n + AHEAD < STEPS:
                            scores(n + AHEAD)
                        else:
                            if n + AHEAD == STEPS:
                                pe.wait_ge(o_normed, due(o_normed, 4))
                                pe.wait_ge(headsL_ready, due(headsL_ready, 3))
                                pe.wait_ge(wH_ready, due(wH_ready, base + IN_PAIRS + 1))
                                pe.wait_ge(wL_ready, due(wL_ready, base + IN_PAIRS + 1))
                            down_tile(base + IN_PAIRS, slot, MIX_START[n + AHEAD - STEPS], mixed(0), True, False)
                    values(STEPS - 1)
                    for d in MIX_REST:
                        if d == 4:
                            turn_heads(HEADS // 2 - 1, OUT_BANK)
                        if d == OUT_BANK:
                            pe.wait_ge(headsL_ready, due(headsL_ready, HEADS // 2))
                        last = down_tile(base + IN_PAIRS, slot, d, mixed(0), True, False)
                    last.then_inc(pair_done, 1)
                    for i in range(1, OUT_PAIRS):
                        if i == 2:
                            pe.wait_ge(gatedL_ready, due(gatedL_ready, 4))
                        down_pair(base + IN_PAIRS + i, (slot + i) % 2, mixed(i), False, i == OUT_PAIRS - 1)
                    after(stage, norm + 3, base + MIX_PAIRS)

                ffn(0, 0, 0, 0)
                mixer(FFN_PAIRS, 2)
                ffn(2, 1, FFN_PAIRS + MIX_PAIRS, 6)

        @block.scalar
        def _(act):
            af = nc.scalar.activation
            steps = [0]
            act.wait_ge(landed[0], 16)
            af(WH[:, 0, :], raw[:, 0, :], ACT.Copy).then_inc(wH_ready, 1)
            act.wait_ge(first_gains_ready, 1)
            act.wait_ge(x_ready, 1)
            af(xH[:, 0, :], x[:, 0, :], ACT.Copy, scale=first_gains[:, 0:1]).then_inc(xH_ready, 1)
            af(xg[0][:], x[:, 0, :], ACT.Copy, scale=first_gains[:, 0:1]).then_inc(xg_ready, 1)
            act.wait_ge(landed[1], 16)
            af(WH[:, 1, :], raw[:, 1, :], ACT.Copy).then_inc(wH_ready, 1)
            with act.Fori(0, DEPTH) as layer:
                due = counter(layer)
                steps[0] = 0

                def link(instruction):
                    steps[0] += 1
                    instruction.then_inc(act_step, 1)
                    act.wait_ge(act_step, due(act_step, steps[0]))

                def high(p, m, slot):
                    act.wait_ge(landed[slot], due(landed[slot], 16 * (m + 1)))
                    act.wait_ge(pair_done, due(pair_done, p - 1))
                    af(WH[:, slot, :], raw[:, slot, :], ACT.Copy).then_inc(wH_ready, 1)

                def high_at(p):
                    high(p, p // 2, p % 2)

                def split_x(stage):
                    for n, k in enumerate(X_ORDER):
                        if stage == 0 and n == 0:
                            continue
                        act.wait_ge(x_ready, due(x_ready, DT * stage + n + 1 - DT))
                        g = first_gains[:, k:k + 1] if stage == 0 else gains[:, G_PRE[stage] + k:G_PRE[stage] + k + 1]
                        af(xH[:, k, :], x[:, k, :], ACT.Copy, scale=g).then_inc(xH_ready, 1)
                        if n >= 2:
                            act.wait_ge(xL_ready, due(xL_ready, DT * stage + n - 1))
                        af(xg[n % 2][:], x[:, k, :], ACT.Copy, scale=g).then_inc(xg_ready, 1)
                    for n, k in enumerate(X_ORDER):
                        square(n, SQUARES * stage, x[:, k, :])

                def square(n, used, src):
                    if n >= 2:
                        act.wait_ge(sq_used, due(sq_used, used + n - 1))
                    af(sq[:, n % 2, :], src, ACT.Square).then_inc(sq_ready, 1)

                def keep_spread(stage, norm):
                    act.wait_ge(spread_ready, due(spread_ready, norm + 1))
                    af(rstd_x[:], ps[:, 6, :], ACT.Copy).then_inc(spread_kept, 1)

                def hidden(n, f):
                    act.wait_ge(gu_scaled, due(gu_scaled, n + 1))
                    af(gate[:], gate[:], ACT.Silu).then_inc(silu_ready, 1)
                    act.wait_ge(h_ready, due(h_ready, n + 1))
                    af(hH[:, f, :], up[:], ACT.Copy).then_inc(hH_ready, 1)

                def after(stage, p):
                    for n, d in enumerate(F_ORDER):
                        if n < DT - 1:
                            act.wait_ge(f_ready, due(f_ready, (DT - 1) * stage + n + 1))
                        else:
                            act.wait_ge(pair_done, due(pair_done, p + 1))
                        square(n, SQUARES * stage + DT, ps[:, d, :])
                    high_at(p + 2)

                def ffn(stage, f_stage, base, norm):
                    n0 = FT * f_stage
                    if stage == 0:
                        act.wait_ge(first_gains_ready, due(first_gains_ready, 0))
                    split_x(stage)
                    high_at(base + 2)
                    high_at(base + 3)
                    keep_spread(stage, norm)
                    hidden(n0, 0)
                    hidden(n0 + 1, 1)
                    high_at(base + 4)
                    hidden(n0 + 2, 2)
                    with act.Fori(0, (FT - 4) // ROUND_F) as i:
                        for j in range(ROUND_F):
                            f = ROUND_F * i + 3 + j
                            high(base + 2 + f, (base + 5 + j) // 2 + ROUND_F // 2 * i, (base + 5 + j) % 2)
                            hidden(n0 + f, f)
                    high_at(base + FT + 1)
                    hidden(n0 + FT - 1, FT - 1)
                    with act.Fori(1, FT // 4) as m:
                        for j in range(2):
                            high(base + FT + 2 * m + j, (base + FT + j) // 2 + m, (base + FT + j) % 2)
                    high_at(base + FT + FT // 2 - 1)
                    high_at(base + FT + FT // 2)
                    after(stage, base + FFN_PAIRS - 1)

                def mixer(base, norm):
                    split_x(1)
                    high_at(base + 2)
                    act.dma_start(const[:], consts).then_inc(mix_landed, 16)
                    act.dma_start(wgu[QK:QK + GATE_RANK, :], w_gate_up[layer]).then_inc(mix_landed, 16)
                    act.dma_start(bias[QK:QK + 1, :], b_gate[layer]).then_inc(mix_landed, 16)
                    act.dma_start(cos[:].bitcast(I32), positions.partition_broadcast(P)).then_inc(mix_landed, 16)
                    act.dma_start(wq[:, 0, :], w_q_up[layer, 0]).then_inc(mix_landed, 16)
                    act.dma_start(wq[:, 1, :], w_q_up[layer, 1]).then_inc(mix_landed, 16)
                    act.dma_start(wkv[:], w_kv_up[layer]).then_inc(mix_landed, 16)
                    high_at(base + 3)
                    keep_spread(1, norm)
                    act.wait_ge(angle_ready, due(angle_ready, 1))
                    af(cos[:], sin[:], ACT.Sin, scale=0.5).then_inc(sine_ready, 1)
                    act.wait_ge(sine_ready, due(sine_ready, 1))
                    af(sin[:], sin[:], ACT.Sin).then_inc(sine_ready, 1)
                    act.wait_ge(in_kept, due(in_kept, 3))
                    act.wait_ge(mean_ready, due(mean_ready, norm + 1))
                    for j in range(2):
                        af(sq[:, j, :], mq[:, j, :], ACT.Square).then_inc(latent_sq, 1)
                    af(acc[:], ckv[:], ACT.Square).then_inc(latent_sq, 1)
                    high_at(base + 4)

                    def keep_values(i):
                        banks = (2, 3) if i == 0 else (4, 5)
                        act.wait_ge(pair_done, due(pair_done, base + 5 + i))
                        for b in range(BLK):
                            last = af(v_tok[:, b, i * GV:(i + 1) * GV],
                                      ps[:, banks[b // 2], (b % 2) * GV:(b % 2 + 1) * GV], ACT.Copy,
                                      scale=rx_col[:, b:b + 1])
                        last.then_inc(v_kept, 1)

                    high_at(base + 5)
                    keep_values(0)
                    act.wait_ge(z_ready, due(z_ready, 1))
                    link(af(kf[:], ps[:, 7, :], ACT.Abs))
                    link(af(kf[:], kf[:], ACT.Exp, scale=-1.0))
                    af(kf[:], kf[:], ACT.Ln, bias=1.0).then_inc(soft_ready, 1)
                    high_at(base + 6)
                    keep_values(1)
                    act.wait_ge(b_last_ready, due(b_last_ready, 1))
                    af(eb[:], ps[:, 7, :], ACT.Exp).then_inc(exp_ready, 1)
                    af(enb[:], ps[:, 7, :], ACT.Exp, scale=-1.0).then_inc(exp_ready, 1)
                    for n in range(NCHUNK):
                        tok = slice(n * CHUNK, (n + 1) * CHUNK)
                        last = af(zg[:, tok], ps[:, 7, tok], ACT.Exp, bias=b_last[:, n:n + 1], scale=-1.0)
                    last.then_inc(exp_ready, 1)
                    high_at(base + 7)
                    for t in range(4):
                        act.wait_ge(in_kept, due(in_kept, 9 + t))
                        af(gates[t][:], gates[t][:], ACT.Silu).then_inc(gate_silu, 1)
                    high_at(base + 8)
                    af(table_column[:], minus_half[:, 0:1], ACT.Exp)
                    act.wait_ge(kt_psum, due(kt_psum, 1))
                    af(kt_gla[:].rearrange("p b f -> p (b f)"), ps[:, 6, :], ACT.Copy).then_inc(kt_kept, 1)
                    act.wait_ge(kt_psum, due(kt_psum, 2))
                    af(kt_ret[:].rearrange("p b f -> p (b f)"), ps[:, 7, :], ACT.Copy).then_inc(kt_kept, 1)

                    def keep_q(h):
                        act.wait_ge(q_psum, due(q_psum, h + 1))
                        if h >= 2:
                            act.wait_ge(scored, due(scored, (h - 1) * BLK))
                        af(qT[0:NOPE, h % 2, :], ps[0:NOPE, QK_BANK, :], ACT.Copy).then_inc(q_kept, 1)

                    def keep_k(h):
                        act.wait_ge(k_psum, due(k_psum, h + 1))
                        af(kT[0:NOPE, h % 2, :], ps[0:NOPE, QK_BANK, :], ACT.Copy).then_inc(k_kept, 1)

                    def exps(m):
                        width = (m % BLK + 1) * P
                        act.wait_ge(top_ready, due(top_ready, m + 1))
                        if m >= 3:
                            act.wait_ge(turned, due(turned, m - 2))
                        af(prob[:, m % 3, 0:width], ps[:, RING[m % 4], 0:width], ACT.Exp, scale=QK ** -0.5,
                           bias=minus_top[:, m % 4:m % 4 + 1],
                           accum_out=total[:, m // BLK % 2, m % BLK:m % BLK + 1]).then_inc(exped, 1)

                    def keep_turn(m):
                        width = (m % BLK + 1) * P
                        act.wait_ge(turned, due(turned, m + 1))
                        if m >= 2:
                            act.wait_ge(valued, due(valued, m - 1))
                        af(probT[:, m % 2, 0:width], ps[:, RING[m % 4], 0:width], ACT.Copy).then_inc(turn_kept, 1)

                    def keep_heads(i, bank):
                        act.wait_ge(heads_turned, due(heads_turned, i + 1))
                        af(xH[:, i, :], ps[:, bank, :], ACT.Copy).then_inc(headsH_ready, 1)

                    def linear(n):
                        if LIN_STEP <= n < NORM_STEP:
                            b, part = divmod(n - LIN_STEP, 3)
                            if part == 0:
                                act.wait_ge(gated_scored, due(gated_scored, b + 1))
                                if b >= 1:
                                    act.wait_ge(gr_used, due(gr_used, b))
                                up_scores = ps[:, LIN_BANKS[1], :].rearrange("p (h i) -> p h i", h=GH)
                                for c in range(2):
                                    r = slice(c * CHUNK, (c + 1) * CHUNK)
                                    last = af(attn_g[r, :, r], up_scores[r, :, r], ACT.Copy)
                                last.then_inc(up_kept, 1)
                            elif part == 2:
                                act.wait_ge(gr_used, due(gr_used, b + 1))
                                af(heads[:, :, b * P:(b + 1) * P],
                                   ps[:, LIN_BANKS[1], :].rearrange("p (t i) -> p t i", t=4), ACT.Copy).then_inc(o_kept, 1)
                        elif NORM_STEP <= n < NORM_STEP + 2:
                            if n == NORM_STEP:
                                act.wait_ge(o_kept, due(o_kept, BLK))
                            for t in range(2 * (n - NORM_STEP), 2 * (n - NORM_STEP) + 2):
                                if t >= 2:
                                    act.wait_ge(o_sq_used, due(o_sq_used, t - 1))
                                af(sq[:, t % 2, :], heads[:, t, :], ACT.Square).then_inc(o_sq, 1)
                        elif GATE_STEP + 2 <= n < GATE_STEP + 6:
                            t = n - GATE_STEP - 2
                            act.wait_ge(o_gated, due(o_gated, t + 1))
                            af(xH[:, 4 + t, :], heads[:, t, :], ACT.Copy).then_inc(gatedH_ready, 1)

                    for n, b in enumerate((2, 3, 0, 1)):
                        if b == 0:
                            keep_q(0)
                        act.wait_ge(vm_psum, due(vm_psum, n + 1))
                        af(v_mla[:, b, :], ps[:, RING[b], :], ACT.Copy).then_inc(vm_kept, 1)
                    act.wait_ge(kpe_psum, due(kpe_psum, 1))
                    for j in range(2):
                        af(kT[NOPE:P, j, :], ps[NOPE:P, LIN_BANKS[0], :], ACT.Copy).then_inc(kpe_copied, 1)
                    keep_k(0)
                    keep_q(1)
                    exps(0)
                    keep_k(1)
                    exps(1)
                    exps(2)
                    act.wait_ge(cleared, due(cleared, 1))
                    for n in range(STEPS):
                        h, b = divmod(n, BLK)
                        keep_turn(n)
                        if h and h % 2 == 0 and b == 3:
                            keep_heads(h // 2 - 1, QK_BANK)
                        if h + 2 < HEADS and b == 1:
                            keep_q(h + 2)
                        if h + 2 < HEADS and b == 2:
                            keep_k(h + 2)
                        linear(n)
                        if n == NORM_STEP + 2:
                            high_at(base + 9)
                        if n + AHEAD < STEPS:
                            exps(n + AHEAD)
                    keep_heads(HEADS // 2 - 1, OUT_BANK)
                    for i in range(2, OUT_PAIRS + 1):
                        high_at(base + IN_PAIRS + i)
                    after(1, base + MIX_PAIRS - 1)

                ffn(0, 0, 0, 0)
                mixer(FFN_PAIRS, 2)
                ffn(2, 1, FFN_PAIRS + MIX_PAIRS, 6)
                act.wait_ge(first_gains_ready, due(first_gains_ready, 1))
                act.wait_ge(x_ready, due(x_ready, 2 * DT + 1))
                af(xH[:, 0, :], x[:, 0, :], ACT.Copy, scale=first_gains[:, 0:1]).then_inc(xH_ready, 1)
                af(xg[0][:], x[:, 0, :], ACT.Copy, scale=first_gains[:, 0:1]).then_inc(xg_ready, 1)

        @block.vector
        def _(dve):
            tt, ts, stt = nc.vector.tensor_tensor, nc.vector.tensor_scalar, nc.vector.scalar_tensor_tensor
            steps = [0]
            nc.vector.memset(ones[:], 1.0)
            nc.vector.memset(ones_row[:], 1.0)
            nc.vector.memset(minus_half[:], -0.5).then_inc(start_ready, 1)
            dve.wait_ge(gains_landed, 16)
            nc.vector.tensor_copy(first_gains[:], gains_all[:, 0, G_PRE[0]:G_PRE[0] + DT]).then_inc(first_gains_ready, 1)
            nc.vector.tensor_copy(gains[:], gains_all[:, 0, :]).then_inc(gains_ready, 1)
            dve.wait_ge(wH_ready, 1)
            tt(WL[:, 0, :], raw[:, 0, :], WH[:, 0, :].bitcast(F32), ALU.subtract).then_inc(wL_ready, 1)
            dve.wait_ge(wH_ready, 2)
            tt(WL[:, 1, :], raw[:, 1, :], WH[:, 1, :].bitcast(F32), ALU.subtract).then_inc(wL_ready, 1)
            dve.wait_ge(first_gains_ready, 1)
            dve.wait_ge(gains_ready, 1)
            with dve.Fori(0, DEPTH) as layer:
                due = counter(layer)
                steps[0] = 0

                def link(instruction):
                    steps[0] += 1
                    instruction.then_inc(dve_step, 1)
                    dve.wait_ge(dve_step, due(dve_step, steps[0]))

                def lows(p, slot):
                    dve.wait_ge(wH_ready, due(wH_ready, p + 1))
                    tt(WL[:, slot, :], raw[:, slot, :], WH[:, slot, :].bitcast(F32), ALU.subtract).then_inc(wL_ready, 1)

                def low_at(p):
                    lows(p, p % 2)

                def low_half(p, j):
                    if j == 0:
                        dve.wait_ge(wH_ready, due(wH_ready, p + 1))
                    half = slice(j * SLAB, (j + 1) * SLAB)
                    last = tt(WL[:, p % 2, half], raw[:, p % 2, half], WH[:, p % 2, half].bitcast(F32), ALU.subtract)
                    if j:
                        last.then_inc(wL_ready, 1)

                def add_square(n, ready, used):
                    dve.wait_ge(sq_ready, due(sq_ready, ready + n + 1))
                    if n:
                        dve.wait_ge(sq_used, due(sq_used, used + n))
                        tt(acc[:], acc[:], sq[:, n % 2, :], ALU.add).then_inc(sq_used, 1)
                    else:
                        nc.vector.tensor_copy(acc[:], sq[:, 0, :]).then_inc(sq_used, 1)

                def mean_of(norm, bank, scale, eps):
                    dve.wait_ge(col_ready, due(col_ready, norm + 1))
                    ts(mean[:, 0:BLK], ps[:, bank, 0:BLK], scale, eps, ALU.mult, ALU.add).then_inc(mean_ready, 1)

                def hidden(n, f, banks, first=False):
                    if not first:
                        dve.wait_ge(hL_ready, due(hL_ready, n))
                    for j, dst in enumerate((gate, up)):
                        last = tt(dst[:], ps[:, banks[j], :], rstd_x[:], ALU.mult)
                    last.then_inc(gu_scaled, 1)
                    dve.wait_ge(silu_ready, due(silu_ready, n + 1))
                    tt(up[:], gate[:], up[:], ALU.mult).then_inc(h_ready, 1)
                    dve.wait_ge(hH_ready, due(hH_ready, n + 1))
                    tt(hL[:, f, :], up[:], hH[:, f, :].bitcast(F32), ALU.subtract).then_inc(hL_ready, 1)

                def after(stage, norm, share, p):
                    for n in range(DT - 1):
                        add_square(n, 2 * DT * stage + DT, SQUARES * stage + DT)
                        if n < 2:
                            nc.vector.tensor_copy((f_first, up)[n][:], ps[:, n, :]).then_inc(f_kept, 1)
                    mean_of(norm, 0, 1.0 / (D * share * share), EPS / (share * share))
                    low_at(p + 2)
                    dve.wait_ge(spread_ready, due(spread_ready, norm + 1))
                    normed = (acc, sq[:, 0, :])

                    def norm_tile(n):
                        k = X_ORDER[n]
                        a = (f_first[:], up[:])[k] if k < 2 else ps[:, k, :]
                        b = ps[:, 0, :] if k == 0 else gate3[:]
                        if n >= 2:
                            dve.wait_ge(x_ready, due(x_ready, DT * stage + n - 1))
                        tt(normed[n % 2][:], a, b, ALU.mult).then_inc(f_normed, 1)

                    def to_residual(n):
                        k = X_ORDER[n]
                        g = G_POST[stage] + k
                        dve.wait_ge(f_normed, due(f_normed, DT * stage + n + 1))
                        stt(x[:, k, :], normed[n % 2][:], gains[:, g:g + 1], x[:, k, :], ALU.mult,
                            ALU.add).then_inc(x_ready, 1)

                    norm_tile(0)
                    to_residual(0)
                    nc.vector.tensor_copy(gate3[:], ps[:, 0, :]).then_inc(rstd_kept, 1)
                    dve.wait_ge(rstd_kept, due(rstd_kept, stage + 1))
                    norm_tile(1)
                    to_residual(1)
                    norm_tile(2)
                    for n in range(3, DT):
                        norm_tile(n)
                        to_residual(n - 1)
                    to_residual(DT - 1)
                    dve.wait_ge(x_ready, due(x_ready, DT * (stage + 1)))

                def ffn(stage, f_stage, base, norm):
                    n0 = FT * f_stage
                    for n in range(DT):
                        add_square(n, 2 * DT * stage, SQUARES * stage)
                    low_at(base + 2)
                    mean_of(norm, 6, 1.0 / D, EPS)
                    low_at(base + 3)
                    dve.wait_ge(spread_kept, due(spread_kept, stage + 1))
                    hidden(n0, 0, (0, 1), first=True)
                    hidden(n0 + 1, 1, (2, 3))
                    low_at(base + 4)
                    dve.wait_ge(pair_done, due(pair_done, base + 3))
                    hidden(n0 + 2, 2, (4, 5))
                    with dve.Fori(0, (FT - 4) // ROUND_F) as i:
                        for j in range(ROUND_F):
                            f = ROUND_F * i + 3 + j
                            lows(base + 2 + f, (base + 5 + j) % 2)
                            dve.wait_ge(pair_done, due(pair_done, base + f + 1))
                            hidden(n0 + f, f, FFN_BANKS[j % 3])
                    dve.wait_ge(pair_done, due(pair_done, base + FT))
                    hidden(n0 + FT - 1, FT - 1, (0, 1))
                    low_at(base + FT + 1)
                    with dve.Fori(1, FT // 4) as m:
                        for j in range(2):
                            lows(base + FT + 2 * m + j, (base + FT + j) % 2)
                    low_at(base + FT + FT // 2 - 1)
                    low_at(base + FT + FT // 2)
                    after(stage, norm + 1, 0.5, base + FFN_PAIRS - 1)

                def mixer(base, norm):
                    for n in range(DT):
                        add_square(n, 2 * DT, SQUARES)
                    low_at(base + 2)
                    mean_of(norm, 6, 1.0 / D, EPS)
                    low_at(base + 3)

                    def keep(bank, dst, r0=0, r1=P):
                        tt(dst[r0:r1], ps[r0:r1, bank, :], rstd_x[r0:r1, :], ALU.mult).then_inc(in_kept, 1)

                    dve.wait_ge(spread_kept, due(spread_kept, 2))
                    nc.vector.tensor_copy(rx_col[:], rstd[:, 0:BLK])
                    dve.wait_ge(pair_done, due(pair_done, base + 1))
                    keep(0, mq[:, 0, :])
                    keep(1, mq[:, 1, :])
                    dve.wait_ge(pair_done, due(pair_done, base + 2))
                    keep(2, ckv)
                    keep(3, krgg, NOPE, QK + GATE_RANK)
                    dve.wait_ge(mix_landed, due(mix_landed, 16 * 7))
                    link(nc.vector.tensor_copy(sin[:], cos[:].bitcast(I32)))
                    link(ts(sin[:], sin[:], inv_freq, None, ALU.mult))
                    link(ts(cos[:], sin[:], 1.0 / TWO_PI, ROUND, ALU.mult, ALU.add))
                    link(ts(cos[:], cos[:], ROUND, None, ALU.subtract))
                    for c in (C1, C2, C3):
                        link(stt(sin[:], cos[:], -c, sin[:], ALU.mult, ALU.add))
                    ts(sin[:], sin[:], 3.1415925, -3.1415925, ALU.min, ALU.max).then_inc(angle_ready, 1)
                    dve.wait_ge(pair_done, due(pair_done, base + 3))
                    stt(gq, ps[:, 4, :], DK ** -0.5, rstd_x[:], ALU.mult, ALU.mult).then_inc(in_kept, 1)
                    keep(5, gk)
                    low_at(base + 4)
                    dve.wait_ge(sine_ready, due(sine_ready, 2))
                    link(tt(cos[:], cos[:], cos[:], ALU.mult))
                    ts(cos[:], cos[:], -2.0, 1.0, ALU.mult, ALU.add).then_inc(rope_ready, 1)
                    dve.wait_ge(pair_done, due(pair_done, base + 4))
                    keep(0, rq)
                    keep(1, rk)
                    low_at(base + 5)
                    dve.wait_ge(col_ready, due(col_ready, norm + 2))
                    ts(mean[:, 0:BLK], ps[:, 6, 0:BLK], 1.0 / QR, EPS, ALU.mult, ALU.add)
                    ts(mean[:, BLK:2 * BLK], ps[:, 6, BLK:2 * BLK], 1.0 / KVR, EPS, ALU.mult, ALU.add).then_inc(mean_ready, 1)
                    dve.wait_ge(z_ready, due(z_ready, 1))
                    dve.wait_ge(soft_ready, due(soft_ready, 1))
                    stt(zg[:], ps[:, 7, :], 0.0, kf[:], ALU.min, ALU.subtract).then_inc(log_ready, 1)
                    low_at(base + 6)
                    dve.wait_ge(cum_ready, due(cum_ready, 1))
                    nc.vector.tensor_copy(b_last[:], ps[:, 7, CHUNK - 1::CHUNK]).then_inc(b_last_ready, 1)
                    low_at(base + 7)
                    dve.wait_ge(spread_ready, due(spread_ready, norm + 2))
                    for j in range(2):
                        stt(mq[:, j, :], mq[:, j, :], gains[:, G_Q + j:G_Q + j + 1], ps[:, 6, :], ALU.mult,
                            ALU.mult).then_inc(latent_ready, 1)
                    stt(ckv[:], ckv[:], gains[:, G_KV:G_KV + 1], ps[:, 4, :], ALU.mult, ALU.mult).then_inc(latent_ready, 1)
                    dve.wait_ge(exp_ready, due(exp_ready, 3))
                    tt(kf[:], gk[:], enb[:], ALU.mult).then_inc(k_ready, 1)
                    tt(kb[:], gk[:], eb[:], ALU.mult).then_inc(k_ready, 1)
                    tt(zg[:], zg[:], gk[:], ALU.mult).then_inc(k_ready, 1)

                    def turn(i, t, bank, r0, r1):
                        dve.wait_ge(rot_ready, due(rot_ready, i + 1))
                        tmp = attn_r[:].rearrange("p h i -> p (h i)")[r0:r1, :]
                        link(tt(t[r0:r1, :], t[r0:r1, :], cos[r0:r1, :], ALU.mult))
                        link(tt(tmp, ps[r0:r1, bank, :], sin[r0:r1, :], ALU.mult))
                        return tt(t[r0:r1, :], t[r0:r1, :], tmp, ALU.add)

                    dve.wait_ge(pair_done, due(pair_done, base + 7))
                    keep(0, gates[0])
                    keep(1, gates[1])
                    dve.wait_ge(rope_ready, due(rope_ready, 1))
                    link(turn(0, rq, 5, 0, P))
                    link(turn(1, rk, 7, 0, P))
                    tt(ks_ret[:].rearrange("p (n i) -> p n i", n=NCHUNK), rk.rearrange("p (n i) -> p n i", n=NCHUNK),
                       k_dec.rearrange("p (o i) -> p o i", o=1).broadcast_to([P, NCHUNK, CHUNK]),
                       ALU.mult).then_inc(ret_ready, 1)
                    dve.wait_ge(pair_done, due(pair_done, base + 8))
                    keep(2, gates[2])
                    keep(3, gates[3])
                    link(turn(2, krgg, 1, NOPE, QK))
                    ts(cos[QK:P, :], sin[QK:P, :], sign[QK:P, :], None, ALU.mult).then_inc(kpe_ready, 1)
                    dve.wait_ge(kpe_ready, due(kpe_ready, 1))

                    def turn_q(h):
                        dve.wait_ge(q_psum, due(q_psum, h + 1))
                        if h >= 2:
                            dve.wait_ge(scored, due(scored, (h - 1) * BLK))
                        tt(qT[NOPE:P, h % 2, :], ps[NOPE:P, QK_BANK, :], cos[NOPE:P, :], ALU.mult).then_inc(q_ready, 1)

                    def add_states(b):
                        dve.wait_ge(ds_ready, due(ds_ready, b + 1))
                        for c in range(2 if b < BLK - 1 else 1):
                            n = 2 * b + c
                            ds_gla, ds_ret = ps[:, LIN_BANKS[c], 0:GV], ps[:, LIN_BANKS[c], GV:2 * GV]
                            if n == 0:
                                nc.vector.tensor_copy(s_gla[:, 0, :], ds_gla)
                                last = nc.vector.tensor_copy(s_ret[:, 0, :], ds_ret)
                            else:
                                at = n * CHUNK + CHUNK - 1
                                stt(s_gla[:, n, :], s_gla[:, n - 1, :], eb[:, at:at + 1], ds_gla,
                                    ALU.mult, ALU.add)
                                last = stt(s_ret[:, n, :], s_ret[:, n - 1, :], chunk_dec, ds_ret,
                                           ALU.mult, ALU.add)
                            if c == 0 and b < BLK - 1:
                                link(last)
                        last.then_inc(state_ready, 1)
                        dve.wait_ge(state_ready, due(state_ready, b + 1))

                    def keep_low(b):
                        dve.wait_ge(gated_scored, due(gated_scored, b + 1))
                        dve.wait_ge(up_kept, due(up_kept, b + 1))
                        dve.sem_inc(dve_passed)
                        low_scores = ps[:, LIN_BANKS[0], :].rearrange("p (h i) -> p h i", h=GH)
                        for c in range(2):
                            r = slice(c * CHUNK, (c + 1) * CHUNK)
                            last = nc.vector.copy_predicated(
                                attn_g[r, :, r],
                                low[r, :].rearrange("p (o i) -> p o i", o=1).broadcast_to([CHUNK, GH, CHUNK]),
                                low_scores[r, :, r])
                        last.then_inc(low_kept, 1)

                    def decayed(b):
                        dve.wait_ge(ret_scored, due(ret_scored, b + 1))
                        if b >= 1:
                            dve.wait_ge(gr_used, due(gr_used, b))
                        tt(attn_r[:], ps[:, LIN_BANKS[0], :].rearrange("p (h i) -> p h i", h=GH), decay,
                           ALU.mult).then_inc(gr_ready, 1)

                    def normed_output(t):
                        if t == 0:
                            dve.wait_ge(o_kept, due(o_kept, BLK))
                        if t < 3:
                            dve.wait_ge(o_spread, due(o_spread, t + 1))
                        else:
                            dve.wait_ge(spread_ready, due(spread_ready, norm + 3))
                        g = G_GLA if t < 2 else G_RET
                        stt(heads[:, t, :], heads[:, t, :], gains[:, g:g + 1], ps[:, LIN_BANKS[t % 2], :], ALU.mult,
                            ALU.mult).then_inc(o_normed, 1)

                    def linear(n):
                        if n < LIN_STEP:
                            add_states(n + 1)
                        elif n < NORM_STEP:
                            b, part = divmod(n - LIN_STEP, 3)
                            if part == 0:
                                keep_low(b)
                            elif part == 1:
                                decayed(b)
                        elif n == NORM_STEP + 2:
                            dve.wait_ge(col_ready, due(col_ready, norm + 3))
                            ts(mean[:], ps[:, LIN_BANKS[0], 0:32], 1.0 / DV, EPS, ALU.mult, ALU.add).then_inc(mean_ready, 1)
                        if n in (NORM_STEP, NORM_STEP + 1):
                            low_half(base + IN_PAIRS, n - NORM_STEP)
                        if GATE_STEP <= n < GATE_STEP + 4:
                            normed_output(n - GATE_STEP)
                        if n in (GATE_STEP + 9, GATE_STEP + 10):
                            low_half(base + IN_PAIRS + 1, n - GATE_STEP - 9)

                    def tops(m):
                        width = (m % BLK + 1) * P
                        dve.wait_ge(scored, due(scored, m + 1))
                        s = ps[:, RING[m % 4], :]
                        link(nc.vector.memset(s[0:CHUNK, width - CHUNK:width], MASKED))
                        link(nc.vector.reduce_max(top[:, m % 4:m % 4 + 1], s[:, 0:width], AX_X))
                        ts(minus_top[:, m % 4:m % 4 + 1], top[:, m % 4:m % 4 + 1], -(QK ** -0.5), None,
                           ALU.mult).then_inc(top_ready, 1)

                    def shares(h):
                        dve.wait_ge(exped, due(exped, BLK * (h + 1)))
                        link(nc.vector.reciprocal(share[:, h % 2, :], total[:, h % 2, :]))

                    def keep_head(h):
                        dve.wait_ge(valued, due(valued, BLK * (h + 1)))
                        tt(pair_out[h // 2 % 2][:, :, h % 2 * DV:(h % 2 + 1) * DV],
                           ps[:, OUT_BANK, 0:BLK * DV].rearrange("p (b e) -> p b e", b=BLK),
                           share[:, h % 2, :].rearrange("p (b o) -> p b o", o=1).broadcast_to([P, BLK, DV]),
                           ALU.mult).then_inc(head_kept, 1)

                    def low_heads(i, bank):
                        dve.wait_ge(headsH_ready, due(headsH_ready, i + 1))
                        tt(xL[:, i, :], ps[:, bank, :], xH[:, i, :].bitcast(F32),
                           ALU.subtract).then_inc(headsL_ready, 1)

                    turn_q(0)
                    add_states(0)
                    turn_q(1)
                    for m in range(AHEAD):
                        tops(m)
                    for n in range(STEPS):
                        h, b = divmod(n, BLK)
                        if h and b == 0:
                            keep_head(h - 1)
                        if b == 2:
                            shares(h)
                        if h and h % 2 == 0 and b == 3:
                            low_heads(h // 2 - 1, QK_BANK)
                        if h + 2 < HEADS and b == 1:
                            turn_q(h + 2)
                        linear(n)
                        if n + AHEAD < STEPS:
                            tops(n + AHEAD)
                    keep_head(HEADS - 1)
                    low_heads(HEADS // 2 - 1, OUT_BANK)
                    for i in range(2, OUT_PAIRS + 1):
                        low_at(base + IN_PAIRS + i)
                    after(1, norm + 3, 1.0, base + MIX_PAIRS - 1)

                ffn(0, 0, 0, 0)
                dve.sem_inc(dve_passed)
                nc.vector.tensor_copy(first_gains[:], gains_all[:, bass.ds(layer + 1, 1), G_PRE[0]:G_PRE[0] + DT].rearrange("p a g -> p (a g)")).then_inc(first_gains_ready, 1)
                dve.wait_ge(first_gains_ready, due(first_gains_ready, 1))
                mixer(FFN_PAIRS, 2)
                ffn(2, 1, FFN_PAIRS + MIX_PAIRS, 6)
                dve.sem_inc(dve_passed)
                nc.vector.tensor_copy(gains[:], gains_all[:, bass.ds(layer + 1, 1), :].rearrange("p a g -> p (a g)")).then_inc(gains_ready, 1)
                dve.wait_ge(gains_ready, due(gains_ready, 1))

        @block.gpsimd
        def _(pool):
            pool.wait_ge(start_ready, 1)
            pool.wait_ge(xg_ready, 1)
            nc.gpsimd.tensor_tensor(xL[:, 0, :], xg[0][:], xH[:, 0, :].bitcast(F32), ALU.subtract).then_inc(xL_ready, 1)
            with pool.Fori(0, DEPTH) as layer:
                due = counter(layer)
                def low_x(stage, n):
                    pool.wait_ge(xg_ready, due(xg_ready, DT * stage + n + 1))
                    nc.gpsimd.tensor_tensor(xL[:, X_ORDER[n], :], xg[n % 2][:], xH[:, X_ORDER[n], :].bitcast(F32),
                                            ALU.subtract).then_inc(xL_ready, 1)

                def split_x(stage):
                    for n in range(0 if stage else 1, DT):
                        low_x(stage, n)

                def power(norm, width):
                    pool.wait_ge(mean_ready, due(mean_ready, norm + 1))
                    nc.gpsimd.tensor_tensor(rstd[:, 0:width], mean[:, 0:width], minus_half[:, 0:width],
                                            ALU.pow).then_inc(rstd_ready, 1)

                split_x(0)
                power(0, 4)
                power(1, 4)
                split_x(1)
                power(2, 4)
                pool.wait_ge(spread_kept, due(spread_kept, 2))
                pool.sem_inc(pool_passed)
                nc.gpsimd.memset(attn_g[:].rearrange("p h i -> p (h i)"), 0.0)
                power(3, 8)
                pool.wait_ge(pair_done, due(pair_done, FFN_PAIRS + IN_PAIRS))
                pool.sem_inc(pool_passed)
                nc.gpsimd.memset(qx[:].rearrange("p a b h i -> p (a b h i)"), 0.0).then_inc(cleared, 1)
                pool.wait_ge(cleared, due(cleared, 1))

                def queries(b):
                    if b >= 2:
                        pool.wait_ge(gr_used, due(gr_used, b - 1))
                    tok = slice(b * P, (b + 1) * P)
                    for kind, (q, decays) in enumerate(((gq, eb), (gq, enb), (rq, None))):
                        for h in range(GH):
                            r = slice(h * DK, (h + 1) * DK)
                            if decays is not None:
                                last = nc.gpsimd.tensor_tensor(qx[r, kind, b % 2, h, :], q[r, tok], decays[r, tok], ALU.mult)
                            else:
                                last = nc.gpsimd.tensor_tensor(
                                    qx[r, kind, b % 2, h, :].rearrange("p (c i) -> p c i", c=2),
                                    q[r, tok].rearrange("p (c i) -> p c i", c=2),
                                    q_dec[r, :].rearrange("p (o i) -> p o i", o=1).broadcast_to([DK, 2, CHUNK]), ALU.mult)
                        if kind == 1:
                            last.then_inc(qg_ready, 1)
                    last.then_inc(qr_ready, 1)

                pool.wait_ge(mix_landed, due(mix_landed, 16 * 7))
                pool.wait_ge(exp_ready, due(exp_ready, 3))
                pool.wait_ge(ret_ready, due(ret_ready, 1))
                for b in range(BLK):
                    queries(b)
                power(4, 32)

                def low_gated(t):
                    pool.wait_ge(gatedH_ready, due(gatedH_ready, t + 1))
                    nc.gpsimd.tensor_tensor(xL[:, 4 + t, :], heads[:, t, :], xH[:, 4 + t, :].bitcast(F32),
                                            ALU.subtract).then_inc(gatedL_ready, 1)

                pool.wait_ge(gate_silu, due(gate_silu, 4))
                for t in range(4):
                    pool.wait_ge(o_normed, due(o_normed, t + 1))
                    nc.gpsimd.tensor_tensor(heads[:, t, :], heads[:, t, :], gates[t][:], ALU.mult).then_inc(o_gated, 1)
                    if t:
                        low_gated(t - 1)
                low_gated(3)
                power(5, 4)
                split_x(2)
                power(6, 4)
                power(7, 4)
                low_x(3, 0)


def pack(np, inputs):
    def tiles(w):
        return w.reshape(DT, P, w.shape[1]).transpose(1, 0, 2).reshape(P, -1)

    def rows(w):
        return w.reshape(-1, 2, P, D).transpose(0, 2, 1, 3).reshape(-1, P, 2 * SLAB)

    blocks = []
    for l in range(DEPTH):
        def ffn(name):
            wg, wu, wd = (inputs[f"{name}_w_{k}"][l] for k in ("gate", "up", "down"))
            for f in range(FT):
                c = slice(f * P, (f + 1) * P)
                blocks.append(np.concatenate([tiles(wg[:, c]), tiles(wu[:, c])], 1)[None])
            blocks.append(rows(wd))

        ffn("ffn1")
        w = inputs["w_in"][l]
        at = np.cumsum([0, 256, 128, 32, 128, 128, 256, 16, 256, 128, 128, 256, 256])
        mq, mkv, mkr, gq, gk, gv, gg, gr, rq, rk, rv, rg = (int(a) for a in at[:-1])
        kr_gg = np.concatenate([w[:, mkr - NOPE:mkr + ROPE], w[:, gg:gg + GATE_RANK], np.zeros((D, P - QK - GATE_RANK), w.dtype)], 1)
        for a, b in ((w[:, mq:mq + P], w[:, mq + P:mq + 2 * P]), (w[:, mkv:mkv + P], kr_gg),
                     (w[:, gq:gq + P], w[:, gk:gk + P]), (w[:, rq:rq + P], w[:, rk:rk + P])):
            blocks.append(np.concatenate([tiles(a), tiles(b)], 1)[None])
        for a in (gv, rv):
            blocks.append(tiles(w[:, a:a + GV])[None])
        for a in (gr, rg):
            blocks.append(np.concatenate([tiles(w[:, a:a + P]), tiles(w[:, a + P:a + 2 * P])], 1)[None])
        blocks.append(rows(inputs["w_out"][l]))
        ffn("ffn2")
    cols = [inputs[n].reshape(DEPTH, -1, P) for n in ("ffn1_pre_g", "ffn1_post_g", "mix_pre_g", "mix_post_g",
                                                     "ffn2_pre_g", "ffn2_post_g", "mla_q_norm_g", "mla_kv_norm_g")]
    cols += [np.concatenate([inputs[n]] * 2, 1)[:, None, :] for n in ("gla_norm_g", "ret_norm_g")]
    heads = inputs["mla_w_q_up"].reshape(DEPTH, QR, HEADS, QK)
    wide = np.concatenate([heads, heads[..., NOPE + ROPE // 2:], heads[..., NOPE:NOPE + ROPE // 2]], 3)
    return {
        "x_in": inputs["x"][0].T.reshape(DT, P, SEQ).transpose(1, 0, 2),
        "positions": inputs["positions"].reshape(SEQ),
        "stream": np.concatenate(blocks, 0),
        "gains_in": np.concatenate([np.concatenate(cols, 1)] + [np.concatenate(cols, 1)[:1]], 0).transpose(0, 2, 1),
        "w_q_up": wide.reshape(DEPTH, 2, P, HEADS * P),
        "w_kv_up": inputs["mla_w_kv_up"],
        "w_gate_up": inputs["gla_w_gate_up"],
        "b_gate": inputs["gla_b_gate"].reshape(DEPTH, 1, GH * DK),
        "consts": constants(np),
    }


def constants(np):
    c = np.zeros((P, CONSTS), np.float64)
    p, i = np.arange(P)[:, None], np.arange(P)[None, :]
    same = p // CHUNK == i // CHUNK
    c[:, C_ID:C_ID + P] = np.eye(P)
    c[:, C_TRI:C_TRI + P] = (same & (p <= i)) / TAU
    half = ROPE // 2
    group = p // ROPE == i // ROPE
    c[:, C_ROT:C_ROT + P] = (group & (p == i - half)) * 1.0 - (group & (p == i + half)) * 1.0
    gamma = np.log1p(-np.exp2(-5.0 - np.arange(GH)))
    for h in range(GH):
        d = np.abs(p % CHUNK - i % CHUNK) - (i % CHUNK + 1.0)
        c[:, C_DEC + h * P:C_DEC + (h + 1) * P] = same * np.exp(gamma[h] * d) * DK ** -0.5
    j = np.arange(CHUNK)[None, :]
    c[:, C_LOW:C_LOW + CHUNK] = p % CHUNK <= j
    g = gamma[np.arange(P) // DK][:, None]
    c[:, C_QDEC:C_QDEC + CHUNK] = np.exp(g * (j + 1.0))
    c[:, C_KDEC:C_KDEC + CHUNK] = np.exp(g * (CHUNK - 1.0 - j)) * DK ** -0.5
    c[:, C_CDEC:C_CDEC + 1] = np.exp(g * CHUNK)
    c[:, C_SIGN:C_SIGN + 1] = np.where(p % ROPE < half, -1.0, 1.0)
    c[:, C_TWICE:C_TWICE + 2 * ROPE] = p % ROPE == np.arange(2 * ROPE)[None, :] % ROPE
    c[:, C_HSEL:C_HSEL + 2] = p // DV == np.arange(2)[None, :]
    c[:, C_INV:C_INV + 1] = 10000.0 ** (-(2.0 * (p % half)) / ROPE)
    return c.astype(np.float32)


def kernel(**inputs):
    import numpy as np
    import concourse.bacc as bacc
    from concourse.bass_utils import run_bass_kernel_spmd

    nc = bacc.Bacc("TRN2", target_bir_lowering=False, num_devices=1)
    arrays = {k: np.ascontiguousarray(v) for k, v in pack(np, {k: np.asarray(v) for k, v in inputs.items()}).items()}
    args = {k: nc.dram_tensor(k, v.shape, mybir.dt.from_np(v.dtype), kind="ExternalInput").ap()
            for k, v in arrays.items()}
    out = nc.dram_tensor("out", (P, DT, SEQ), F32, kind="ExternalOutput").ap()
    hybrid_trunk(nc, out=out, **args)
    r = run_bass_kernel_spmd(nc, [arrays], core_ids=[0])
    y = r.results[0]["out"]
    return np.ascontiguousarray(y.transpose(1, 0, 2).reshape(D, SEQ).T)[None]
```
